# Optimizing a Trainium2 kernel written in Bass

```python
import math
import jax, jax.numpy as jnp
from jax import lax
import numpy as np

D_MODEL = 1024
BATCH = 1
SEQ = 256
DEPTH = 2

HEAD_DIM = 64
HEADS_A = 8
HEADS_B = 8
HEADS_C = 8
WIDTH = HEADS_A * HEAD_DIM
N_BRANCH = 3
ROPE_DIM = HEAD_DIM // 4
ROPE_THETA = 500000.0
MOBA_BLOCK = 256
MOBA_TOPK = 3
MOBA_Q_CHUNK = 32
IDX_HEADS = 8
IDX_DIM = 64
DSA_TOPK_MAX = 256
Q_BLOCK = 128
RMS_EPS = 1e-6

SECTION_SIZES = (
    WIDTH, WIDTH, WIDTH, WIDTH,
    WIDTH, WIDTH, WIDTH, WIDTH,
    WIDTH, WIDTH, WIDTH, WIDTH,
    IDX_HEADS * IDX_DIM, IDX_DIM, IDX_HEADS,
    HEADS_C,
    N_BRANCH * D_MODEL,
)
D_IN = sum(SECTION_SIZES)
SPLIT_POINTS = tuple(int(v) for v in np.cumsum(SECTION_SIZES)[:-1])


def rms_norm(x, gain):
    xf = x.astype(jnp.float32)
    y = xf * lax.rsqrt(jnp.mean(xf * xf, axis=-1, keepdims=True) + RMS_EPS)
    return (y * gain.astype(jnp.float32)).astype(x.dtype)

def rope_partial(t, pos):
    half = ROPE_DIM // 2
    inv_freq = jnp.power(jnp.float32(ROPE_THETA), -jnp.arange(0, ROPE_DIM, 2, dtype=jnp.float32) / ROPE_DIM)
    ang = pos.astype(jnp.float32)[:, None] * inv_freq[None, :]
    cos = jnp.cos(ang)[None, :, None, :]
    sin = jnp.sin(ang)[None, :, None, :]
    tr = t[..., :ROPE_DIM].astype(jnp.float32)
    t1, t2 = tr[..., :half], tr[..., half:]
    rot = jnp.concatenate([t1 * cos - t2 * sin, t2 * cos + t1 * sin], axis=-1).astype(t.dtype)
    return jnp.concatenate([rot, t[..., ROPE_DIM:]], axis=-1)

def moba_attention(q, k, v):
    B, S, H, d = q.shape
    n_blk = -(-S // MOBA_BLOCK)
    pad = n_blk * MOBA_BLOCK - S
    kp = jnp.pad(k, ((0, 0), (0, pad), (0, 0), (0, 0)))
    vp = jnp.pad(v, ((0, 0), (0, pad), (0, 0), (0, 0)))
    kb = kp.reshape(B, n_blk, MOBA_BLOCK, H, d).transpose(0, 3, 1, 2, 4)
    vb = vp.reshape(B, n_blk, MOBA_BLOCK, H, d).transpose(0, 3, 1, 2, 4)
    k_mean = jnp.mean(kb, axis=3)
    qh = q.transpose(0, 2, 1, 3)
    k_sel = min(MOBA_TOPK, n_blk - 1)
    scale = d ** -0.5
    bi = jnp.arange(B)[:, None, None, None]
    hi = jnp.arange(H)[None, :, None, None]

    def chunk(ci):
        start = ci * MOBA_Q_CHUNK
        qc = lax.dynamic_slice_in_dim(qh, start, MOBA_Q_CHUNK, axis=2)
        qpos = start + jnp.arange(MOBA_Q_CHUNK)
        own = start // MOBA_BLOCK
        k_own = lax.dynamic_index_in_dim(kb, own, axis=2, keepdims=False)
        v_own = lax.dynamic_index_in_dim(vb, own, axis=2, keepdims=False)
        kpos_own = own * MOBA_BLOCK + jnp.arange(MOBA_BLOCK)
        s_own = jnp.einsum('bhqd,bhkd->bhqk', qc, k_own).astype(jnp.float32) * scale
        s_own = jnp.where(kpos_own[None, :] <= qpos[:, None], s_own, -jnp.inf)
        if k_sel == 0:
            p = jax.nn.softmax(s_own, axis=-1).astype(v.dtype)
            return jnp.einsum('bhqk,bhkd->bhqd', p, v_own)
        gate = jnp.einsum('bhqd,bhnd->bhqn', qc, k_mean).astype(jnp.float32)
        gate = jnp.where((jnp.arange(n_blk) < own)[None, None, None, :], gate, -jnp.inf)
        gval, gidx = lax.top_k(gate, k_sel)
        ok = gval > -jnp.inf
        k_g = kb[bi, hi, gidx]
        v_g = vb[bi, hi, gidx]
        s_past = jnp.einsum('bhqd,bhqnkd->bhqnk', qc, k_g).astype(jnp.float32) * scale
        s_past = jnp.where(ok[..., None], s_past, -jnp.inf)
        s_past = s_past.reshape(B, H, MOBA_Q_CHUNK, k_sel * MOBA_BLOCK)
        p = jax.nn.softmax(jnp.concatenate([s_past, s_own], axis=-1), axis=-1).astype(v.dtype)
        p_past = p[..., :k_sel * MOBA_BLOCK].reshape(B, H, MOBA_Q_CHUNK, k_sel, MOBA_BLOCK)
        p_own = p[..., k_sel * MOBA_BLOCK:]
        return (jnp.einsum('bhqnk,bhqnkd->bhqd', p_past, v_g)
                + jnp.einsum('bhqk,bhkd->bhqd', p_own, v_own))

    out = lax.map(chunk, jnp.arange(S // MOBA_Q_CHUNK))
    return out.transpose(1, 0, 3, 2, 4).reshape(B, S, H, d)

def dsa_attention(q, k, v, q_idx, k_idx, w_idx):
    B, S, H, d = q.shape
    top = min(DSA_TOPK_MAX, S // 4)
    scale = d ** -0.5
    bi = jnp.arange(B)[:, None, None]
    kpos = jnp.arange(S)

    def chunk(ci):
        start = ci * Q_BLOCK
        qpos = start + jnp.arange(Q_BLOCK)
        qi = lax.dynamic_slice_in_dim(q_idx, start, Q_BLOCK, axis=1)
        wi = lax.dynamic_slice_in_dim(w_idx, start, Q_BLOCK, axis=1)
        rel = jax.nn.relu(jnp.einsum('bqhd,bsd->bqhs', qi, k_idx))
        isc = jnp.einsum('bqh,bqhs->bqs', wi, rel).astype(jnp.float32)
        isc = jnp.where(kpos[None, None, :] <= qpos[None, :, None], isc, -jnp.inf)
        ival, idx = lax.top_k(isc, top)
        ok = ival > -jnp.inf
        k_g = k[bi, idx]
        v_g = v[bi, idx]
        qc = lax.dynamic_slice_in_dim(q, start, Q_BLOCK, axis=1)
        s = jnp.einsum('bqhd,bqkhd->bhqk', qc, k_g).astype(jnp.float32) * scale
        s = jnp.where(ok[:, None], s, -jnp.inf)
        p = jax.nn.softmax(s, axis=-1).astype(v.dtype)
        return jnp.einsum('bhqk,bqkhd->bqhd', p, v_g)

    out = lax.map(chunk, jnp.arange(S // Q_BLOCK))
    return out.transpose(1, 0, 2, 3, 4).reshape(B, S, H, d)

def forgetting_attention(q, k, v, log_f):
    B, S, H, d = q.shape
    scale = d ** -0.5
    csum = jnp.cumsum(log_f, axis=1).transpose(0, 2, 1)
    qh = q.transpose(0, 2, 1, 3)
    kh = k.transpose(0, 2, 1, 3)
    vh = v.transpose(0, 2, 1, 3)
    kpos = jnp.arange(S)

    def chunk(ci):
        start = ci * Q_BLOCK
        qpos = start + jnp.arange(Q_BLOCK)
        qc = lax.dynamic_slice_in_dim(qh, start, Q_BLOCK, axis=2)
        cq = lax.dynamic_slice_in_dim(csum, start, Q_BLOCK, axis=2)
        s = jnp.einsum('bhqd,bhkd->bhqk', qc, kh).astype(jnp.float32) * scale
        s = s + (cq[..., :, None] - csum[:, :, None, :])
        s = jnp.where(kpos[None, :] <= qpos[:, None], s, -jnp.inf)
        p = jax.nn.softmax(s, axis=-1).astype(v.dtype)
        return jnp.einsum('bhqk,bhkd->bhqd', p, vh)

    out = lax.map(chunk, jnp.arange(S // Q_BLOCK))
    return out.transpose(1, 0, 3, 2, 4).reshape(B, S, H, d)

def hybrid_layer(x, gain, w_in, f_bias, w_branch, w_out):
    B, S, _ = x.shape
    pos = jnp.arange(S)
    h = rms_norm(x, gain)
    proj = jnp.einsum('bsd,de->bse', h, w_in)
    (qa, ka, va, ga, qb, kb_, vb_, gb, qc, kc, vc, gc,
     q_idx, k_idx, w_idx, f_logit, merge_logit) = jnp.split(proj, SPLIT_POINTS, axis=-1)

    def heads(t, n):
        return t.reshape(B, S, n, HEAD_DIM)

    oa = moba_attention(rope_partial(heads(qa, HEADS_A), pos), rope_partial(heads(ka, HEADS_A), pos),
                        heads(va, HEADS_A)).reshape(B, S, WIDTH) * jax.nn.silu(ga)
    qi = rope_partial(q_idx.reshape(B, S, IDX_HEADS, IDX_DIM), pos)
    ki = rope_partial(k_idx[:, :, None, :], pos)[:, :, 0, :]
    wi = w_idx * (IDX_HEADS ** -0.5 * IDX_DIM ** -0.5)
    ob = dsa_attention(rope_partial(heads(qb, HEADS_B), pos), rope_partial(heads(kb_, HEADS_B), pos),
                       heads(vb_, HEADS_B), qi, ki, wi).reshape(B, S, WIDTH) * jax.nn.silu(gb)
    log_f = jax.nn.log_sigmoid((f_logit + f_bias).astype(jnp.float32))
    oc = forgetting_attention(heads(qc, HEADS_C), heads(kc, HEADS_C), heads(vc, HEADS_C),
                              log_f).reshape(B, S, WIDTH) * jax.nn.silu(gc)

    y = jnp.einsum('nbsw,nwd->bsnd', jnp.stack([oa, ob, oc], axis=0), w_branch)
    gates = jax.nn.sigmoid(merge_logit).reshape(B, S, N_BRANCH, D_MODEL)
    merged = jnp.sum(gates * y, axis=2)
    return x + jnp.einsum('bsd,de->bse', merged, w_out)

def first_inputs(seed: int = 0) -> dict:
    key = jax.random.key(seed)
    ks = jax.random.split(key, 8)
    x = jax.random.normal(ks[0], (BATCH, SEQ, D_MODEL), jnp.float32)
    norm_gain = 1.0 + 0.05 * jax.random.normal(ks[1], (DEPTH, D_MODEL), jnp.float32)
    w_in = jax.random.normal(ks[2], (DEPTH, D_MODEL, D_IN), jnp.float32) * D_MODEL ** -0.5
    forget_bias = 3.0 + 0.5 * jax.random.normal(ks[3], (DEPTH, HEADS_C), jnp.float32)
    w_branch = jax.random.normal(ks[4], (DEPTH, N_BRANCH, WIDTH, D_MODEL), jnp.float32) * WIDTH ** -0.5
    w_out = jax.random.normal(ks[5], (DEPTH, D_MODEL, D_MODEL), jnp.float32) * (0.5 * D_MODEL ** -0.5)
    final_gain = 1.0 + 0.05 * jax.random.normal(ks[6], (D_MODEL,), jnp.float32)
    return {"x": x, "norm_gain": norm_gain, "w_in": w_in, "forget_bias": forget_bias,
            "w_branch": w_branch, "w_out": w_out, "final_gain": final_gain}

def first_block(x, norm_gain, w_in, forget_bias, w_branch, w_out, final_gain):
    h = x
    for layer in range(DEPTH):
        h = hybrid_layer(h, norm_gain[layer], w_in[layer], forget_bias[layer],
                         w_branch[layer], w_out[layer])
    return rms_norm(h, final_gain)


GRID_W = 64
CTX_LEN = 256
N_FOURIER_GROUPS = 4
FOURIER_GROUP_DIM = D_MODEL // 8
FOURIER_WIDTH = N_FOURIER_GROUPS * FOURIER_GROUP_DIM
N_SGU_HEADS = 4
SGU_HEAD_DIM = D_MODEL // 8
SGU_WIDTH = N_SGU_HEADS * SGU_HEAD_DIM
CHUNK = 128
EVEN_IN_WIDTH = FOURIER_WIDTH + 2 * SGU_WIDTH
EVEN_OUT_WIDTH = FOURIER_WIDTH + SGU_WIDTH
NA_HEADS = 16
NA_HEAD_DIM = D_MODEL // NA_HEADS
WIN_H = 8
WIN_W = 16
D_FF = 2816
CONV_W = 3
N_MOD = 6
EPS = 1e-6
NEG_INF = -1e30
N_EVEN = (DEPTH + 1) // 2
N_ODD = DEPTH // 2


def rms_norm_2(x, g=None):
    xf = x.astype(jnp.float32)
    y = xf * lax.rsqrt(jnp.mean(xf * xf, axis=-1, keepdims=True) + EPS)
    if g is not None:
        y = y * g.astype(jnp.float32)
    return y.astype(x.dtype)

def modulate(x, g, shift, scale):
    return rms_norm_2(x, g) * (1 + scale) + shift

def fourier_mix(f):
    y = jnp.fft.fftn(f.astype(jnp.float32), axes=(1, 3), norm="ortho").real
    return y.astype(f.dtype)

def chunk_sgu(u, v, w_s, b_s):
    B_, L, G, C = v.shape
    vc = rms_norm_2(v).reshape(B_, L // CHUNK, CHUNK, G, C)
    s = jnp.einsum('gpq,bnqgc->bnpgc', w_s, vc) + b_s.T[None, None, :, :, None]
    return u * s.reshape(B_, L, G, C)

def even_mixer(h, w_in, w_s, b_s, w_out):
    B_, L, _ = h.shape
    p = h @ w_in
    f = p[..., :FOURIER_WIDTH].reshape(B_, L, N_FOURIER_GROUPS, FOURIER_GROUP_DIM)
    uv = jax.nn.gelu(p[..., FOURIER_WIDTH:])
    u = uv[..., :SGU_WIDTH].reshape(B_, L, N_SGU_HEADS, SGU_HEAD_DIM)
    v = uv[..., SGU_WIDTH:].reshape(B_, L, N_SGU_HEADS, SGU_HEAD_DIM)
    a = fourier_mix(f).reshape(B_, L, FOURIER_WIDTH)
    b = chunk_sgu(u, v, w_s, b_s).reshape(B_, L, SGU_WIDTH)
    return jnp.concatenate([a, b], axis=-1) @ w_out

def _heads(t):
    B_, L, _ = t.shape
    return t.reshape(B_, L, NA_HEADS, NA_HEAD_DIM).transpose(0, 2, 1, 3)

def _merge(o):
    B_, H, L, d = o.shape
    return o.transpose(0, 2, 1, 3).reshape(B_, L, H * d)

def qkv_heads(h, w_qkv, q_g, k_g):
    q, k, v = jnp.split(h @ w_qkv, 3, axis=-1)
    return rms_norm_2(_heads(q), q_g), rms_norm_2(_heads(k), k_g), _heads(v)

def neighbourhood_attention(q, k, v, k_c, v_c, rpb):
    B_, H, L, d = q.shape
    rows = L // GRID_W
    kh = min(WIN_H, rows)
    r = jnp.arange(rows)
    row_start = jnp.clip(r - kh // 2, 0, rows - kh)
    row_idx = row_start[:, None] + jnp.arange(kh)[None, :]
    col = jnp.arange(GRID_W)
    col_start = jnp.clip(col - WIN_W // 2, 0, GRID_W - WIN_W)
    col_mask = (col[None, :] >= col_start[:, None]) & (col[None, :] < col_start[:, None] + WIN_W)
    dr = row_idx - r[:, None] + (WIN_H - 1)
    dc = jnp.clip(col[None, :] - col[:, None] + (WIN_W - 1), 0, 2 * WIN_W - 2)
    bias = rpb[:, dr][:, :, :, dc].transpose(0, 1, 3, 2, 4)
    scale = d ** -0.5
    qg = q.reshape(B_, H, rows, GRID_W, d)
    kg = k.reshape(B_, H, rows, GRID_W, d)[:, :, row_idx]
    vg = v.reshape(B_, H, rows, GRID_W, d)[:, :, row_idx]
    s_loc = jnp.einsum('bhrqd,bhrikd->bhrqik', qg, kg).astype(jnp.float32) * scale + bias
    s_loc = jnp.where(col_mask[:, None, :], s_loc, NEG_INF)
    s_ctx = jnp.einsum('bhrqd,bhcd->bhrqc', qg, k_c).astype(jnp.float32) * scale
    n_loc = kh * GRID_W
    s = jnp.concatenate([s_loc.reshape(B_, H, rows, GRID_W, n_loc), s_ctx], axis=-1)
    p = jax.nn.softmax(s, axis=-1).astype(v.dtype)
    p_loc = p[..., :n_loc].reshape(B_, H, rows, GRID_W, kh, GRID_W)
    p_ctx = p[..., n_loc:]
    o = jnp.einsum('bhrqik,bhrikd->bhrqd', p_loc, vg) + jnp.einsum('bhrqc,bhcd->bhrqd', p_ctx, v_c)
    return o.reshape(B_, H, L, d)

def context_attention(q_c, k_c, v_c):
    s = jnp.einsum('bhqd,bhkd->bhqk', q_c, k_c).astype(jnp.float32) * (q_c.shape[-1] ** -0.5)
    p = jax.nn.softmax(s, axis=-1).astype(v_c.dtype)
    return jnp.einsum('bhqk,bhkd->bhqd', p, v_c)

def conv_ffn(h, w_up, conv_w, conv_b, w_down):
    L = h.shape[1]
    a = h @ w_up
    gate, val = a[..., :D_FF], a[..., D_FF:]
    gp = jnp.pad(gate, ((0, 0), (CONV_W // 2, CONV_W // 2), (0, 0)))
    g = gp[:, 0:L] * conv_w[0] + gp[:, 1:1 + L] * conv_w[1] + gp[:, 2:2 + L] * conv_w[2] + conv_b
    return (jax.nn.silu(g) * val) @ w_down

def second_inputs(seed: int = 0) -> dict:
    key = jax.random.key(seed)
    ks = jax.random.split(key, 24)
    nrm = jax.random.normal
    D = D_MODEL
    return {
        "x": nrm(ks[0], (BATCH, SEQ, D), jnp.float32),
        "c": nrm(ks[1], (BATCH, D), jnp.float32),
        "ctx": nrm(ks[2], (BATCH, CTX_LEN, D), jnp.float32),
        "c_ctx": nrm(ks[3], (D,), jnp.float32),
        "norm1_g": 1.0 + 0.1 * nrm(ks[4], (DEPTH, D), jnp.float32),
        "norm2_g": 1.0 + 0.1 * nrm(ks[5], (DEPTH, D), jnp.float32),
        "ada_w": 0.5 * D ** -0.5 * nrm(ks[6], (DEPTH, D, N_MOD * D), jnp.float32),
        "ada_b": 0.02 * nrm(ks[7], (DEPTH, N_MOD * D), jnp.float32),
        "even_w_in": D ** -0.5 * nrm(ks[8], (N_EVEN, D, EVEN_IN_WIDTH), jnp.float32),
        "even_w_s": CHUNK ** -0.5 * nrm(ks[9], (N_EVEN, N_SGU_HEADS, CHUNK, CHUNK), jnp.float32),
        "even_b_s": 1.0 + 0.1 * nrm(ks[10], (N_EVEN, N_SGU_HEADS, CHUNK), jnp.float32),
        "even_w_out": EVEN_OUT_WIDTH ** -0.5 * nrm(ks[11], (N_EVEN, EVEN_OUT_WIDTH, D), jnp.float32),
        "odd_w_qkv": D ** -0.5 * nrm(ks[12], (N_ODD, D, 3 * D), jnp.float32),
        "odd_q_g": 1.0 + 0.1 * nrm(ks[13], (N_ODD, NA_HEAD_DIM), jnp.float32),
        "odd_k_g": 1.0 + 0.1 * nrm(ks[14], (N_ODD, NA_HEAD_DIM), jnp.float32),
        "odd_rpb": 0.1 * nrm(ks[15], (N_ODD, NA_HEADS, 2 * WIN_H - 1, 2 * WIN_W - 1), jnp.float32),
        "odd_w_o": D ** -0.5 * nrm(ks[16], (N_ODD, D, D), jnp.float32),
        "ffn_w_up": D ** -0.5 * nrm(ks[17], (DEPTH, D, 2 * D_FF), jnp.float32),
        "ffn_conv_w": CONV_W ** -0.5 * nrm(ks[18], (DEPTH, CONV_W, D_FF), jnp.float32),
        "ffn_conv_b": 0.02 * nrm(ks[19], (DEPTH, D_FF), jnp.float32),
        "ffn_w_down": D_FF ** -0.5 * nrm(ks[20], (DEPTH, D_FF, D), jnp.float32),
    }

def second_block(x, c, ctx, c_ctx, norm1_g, norm2_g, ada_w, ada_b, even_w_in, even_w_s, even_b_s, even_w_out,
              odd_w_qkv, odd_q_g, odd_k_g, odd_rpb, odd_w_o, ffn_w_up, ffn_conv_w, ffn_conv_b, ffn_w_down):
    s_lat = jax.nn.silu(c)
    s_ctx = jax.nn.silu(c_ctx)
    for layer in range(DEPTH):
        last = layer == DEPTH - 1
        i = layer // 2
        mod = (s_lat @ ada_w[layer] + ada_b[layer])[:, None, :]
        mod_c = s_ctx @ ada_w[layer] + ada_b[layer]
        sh1, sc1, g1, sh2, sc2, g2 = jnp.split(mod, N_MOD, axis=-1)
        csh1, csc1, cg1, csh2, csc2, cg2 = jnp.split(mod_c, N_MOD, axis=-1)
        h = modulate(x, norm1_g[layer], sh1, sc1)
        h_c = modulate(ctx, norm1_g[layer], csh1, csc1)
        if layer % 2 == 0:
            y = even_mixer(h, even_w_in[i], even_w_s[i], even_b_s[i], even_w_out[i])
            if not last:
                y_c = even_mixer(h_c, even_w_in[i], even_w_s[i], even_b_s[i], even_w_out[i])
        else:
            q, k, v = qkv_heads(h, odd_w_qkv[i], odd_q_g[i], odd_k_g[i])
            q_c, k_c, v_c = qkv_heads(h_c, odd_w_qkv[i], odd_q_g[i], odd_k_g[i])
            y = _merge(neighbourhood_attention(q, k, v, k_c, v_c, odd_rpb[i])) @ odd_w_o[i]
            if not last:
                y_c = _merge(context_attention(q_c, k_c, v_c)) @ odd_w_o[i]
        x = x + g1 * y
        x = x + g2 * conv_ffn(modulate(x, norm2_g[layer], sh2, sc2),
                              ffn_w_up[layer], ffn_conv_w[layer], ffn_conv_b[layer], ffn_w_down[layer])
        if not last:
            ctx = ctx + cg1 * y_c
            ctx = ctx + cg2 * conv_ffn(modulate(ctx, norm2_g[layer], csh2, csc2),
                                       ffn_w_up[layer], ffn_conv_w[layer], ffn_conv_b[layer], ffn_w_down[layer])
    return x


def setup_inputs(seed=0):
    out = dict(first_inputs(seed))
    for name, value in second_inputs(seed + 1).items():
        if name != "x":
            out[name + "_2"] = value
    return out


def reference(
    x, norm_gain, w_in, forget_bias, w_branch, w_out, final_gain, c_2, ctx_2, c_ctx_2,
    norm1_g_2, norm2_g_2, ada_w_2, ada_b_2, even_w_in_2, even_w_s_2, even_b_s_2, even_w_out_2,
    odd_w_qkv_2, odd_q_g_2, odd_k_g_2, odd_rpb_2, odd_w_o_2, ffn_w_up_2, ffn_conv_w_2,
    ffn_conv_b_2, ffn_w_down_2,
):
    x = first_block(
        x, norm_gain, w_in, forget_bias, w_branch, w_out, final_gain,
    )
    return second_block(
        x, c_2, ctx_2, c_ctx_2, norm1_g_2, norm2_g_2, ada_w_2, ada_b_2, even_w_in_2, even_w_s_2,
        even_b_s_2, even_w_out_2, odd_w_qkv_2, odd_q_g_2, odd_k_g_2, odd_rpb_2, odd_w_o_2,
        ffn_w_up_2, ffn_conv_w_2, ffn_conv_b_2, ffn_w_down_2,
    )


_drawn_inputs = setup_inputs


def setup_inputs(seed=0):
    import zlib

    import numpy as np

    out = dict(_drawn_inputs(seed))
    spreads = {}
    factors = {'norm_gain': 3.842,
     'even_b_s_2': 3.418,
     'odd_q_g_2': 8.0,
     'odd_k_g_2': 8.0,
     'odd_rpb_2': 38.052,
     'ffn_conv_b_2': 8.0}
    for name, (base, spread) in spreads.items():
        noise = np.random.default_rng([zlib.crc32(name.encode()), seed]).standard_normal(out[name].shape)
        drawn = base * np.exp(spread * noise) if base else spread * noise
        out[name] = __import__('jax').numpy.asarray(drawn.astype(out[name].dtype))
    for name, factor in factors.items():
        out[name] = (out[name] * factor).astype(out[name].dtype)
    return out
```

```python
from contextlib import ExitStack

import numpy as np

import concourse.bass as bass
from concourse import mybir

F32 = mybir.dt.float32
F32R = mybir.dt.float32r
ALU = mybir.AluOpType
ACT = mybir.ActivationFunctionType
AX = mybir.AxisListType

P = 128
D = 1024
KC = D // P
SEQ = 256
CTX = 256
DEPTH = 2
HD = 64
WIDTH = 512
D_IN = 9808
Q_IDX0 = 12 * WIDTH
K_IDX0 = Q_IDX0 + 512
W_IDX0 = K_IDX0 + HD
MERGE0 = W_IDX0 + 16
D_FF = 2816
FC = D_FF // P
N_MOD = 6
EPS = 1e-6
SCALE = HD ** -0.5
NEG = -1.0e30
FILL = -3.0e38
TAKEN = -3.4e38
TOPK = 64
DMA_SCRATCH = 16 * 1024
SBUF_BYTES = 224 * 1024
SLOTS = 3
UNIT = 2048
BANKS = 3
ADA_COL = 256
AHEAD = 2

ROWS = {}
_n = 0
for _name, _count in (("norm_gain", 16), ("final_gain", 8), ("norm1", 16), ("norm2", 16), ("conv_w", 132),
                      ("conv_b", 44), ("c", 8), ("c_ctx", 8), ("q_g", 1), ("k_g", 1), ("pad", 6), ("ada_b", 96),
                      ("end", 32)):
    ROWS[_name] = _n
    _n += _count
VROWS = 384
assert ROWS["end"] <= 352


def constants():
    t = {}
    i = np.arange(P)
    t["ident"] = np.eye(P, dtype=np.float32)
    inv = np.power(np.float32(500000.0), -np.arange(0, 16, 2, dtype=np.float32) / np.float32(16))
    ang = np.arange(SEQ, dtype=np.float32)[:, None] * inv[None, :].astype(np.float32)
    cos, sin = np.cos(ang.astype(np.float32)), np.sin(ang.astype(np.float32))
    rc, rs = np.ones((P, SEQ), np.float32), np.zeros((P, SEQ), np.float32)
    for b in (0, 64):
        rc[b:b + 8], rc[b + 8:b + 16] = cos.T, cos.T
        rs[b:b + 8], rs[b + 8:b + 16] = -sin.T, sin.T
    t["rope"] = np.stack([rc, rs], 1)
    tri = (np.arange(2)[None, :, None] * P + i[:, None, None]) >= np.arange(SEQ)[None, None, :]
    t["causal"] = np.where(tri, 0.0, NEG).astype(np.float32)
    upto = (np.arange(2)[None, :, None] * P + i[:, None, None]) <= np.arange(SEQ)[None, None, :]
    t["upto"] = upto.astype(np.float32)
    pick = np.zeros((P, 8), np.float32)
    for h in range(8):
        pick[h, h] = pick[64 + h, h] = -1.0 / SCALE
    t["pick"] = pick
    t["add_parts"] = np.tile(np.eye(2, dtype=np.float32), (2, 1))
    c = np.outer(i, i).astype(np.float64) * (2 * np.pi / P)
    t["dft_c"] = np.concatenate([np.cos(c), np.sin(c)], 1).astype(np.float32)
    a = np.outer(np.arange(SEQ), np.arange(SEQ)).astype(np.float64) * (2 * np.pi / SEQ)
    s = 1.0 / np.sqrt(SEQ * P)
    ts = np.stack([np.cos(a) * s, -np.sin(a) * s], 1).astype(np.float32)
    t["dft_t"] = np.ascontiguousarray(ts.reshape(2, P, 2, SEQ).transpose(1, 0, 2, 3))
    heads = (np.arange(16)[None, None, :] == 2 * np.arange(KC)[None, :, None] + (i // 64)[:, None, None])
    t["head_sum"] = heads.astype(np.float32)
    t["head_spread"] = np.ascontiguousarray(heads.transpose(2, 1, 0)).astype(np.float32)
    col = np.arange(64)
    start = np.clip(col - 8, 0, 48)
    win = (col[None, :] >= start[:, None]) & (col[None, :] < start[:, None] + 16)
    win = np.where(win, 0.0, NEG).astype(np.float32)
    t["window"] = np.ascontiguousarray(np.tile(win, (2, 4))[:, ::-1])
    return t


class Steps:

    def __init__(self, known=None):
        self.known = known or {}
        self.names = {}
        self.count = {"start": 0, "layer": 0, "end": 0}
        self.part = "start"
        self.layer = 0

    def step(self, *names):
        self.count[self.part] += 1
        for name in names:
            self.names[(self.part, name)] = self.count[self.part]
        return 1

    def total(self, part):
        return self.known.get(part, 0)

    def value(self, part, n):
        per = self.total("layer")
        if part == "start":
            return per + n
        if part == "layer":
            if self.part == "layer":
                return self.layer * per + (per + self.total("start") + n)
            return per + self.total("start") + (DEPTH - 1) * per + n
        return per + self.total("start") + DEPTH * per + n

    def latest(self, *names):
        if self.part == "end":
            return max(self.at(x.lstrip("<"), before=x[0] == "<") for x in names)
        n = [self.known.get(("layer", x.lstrip("<")), 0) - (self.total("layer") if x[0] == "<" else 0) for x in names]
        return self.layer * self.total("layer") + (self.total("layer") + self.total("start") + max(n))

    def at(self, name, before=False):
        if before and self.part == "layer":
            return self.layer * self.total("layer") + (self.total("start") + self.known.get(("layer", name), 0))
        for part in (self.part, "layer", "start"):
            if (part, name) in self.known and not (before and part == "end"):
                return self.value(part, self.known[(part, name)])
        assert not self.known, name
        return 1

    def last(self):
        return self.value(self.part, self.count[self.part])

    def learned(self):
        return {**self.names, **self.count}


SETS = {"a": 0, "b": 1, "c": 0}


def layer_units():
    units = [("qi", 0), ("qi", 1)]
    for x in "abc":
        units += [(s + x, i) for s in "qkvg" for i in range(2)]
    for n in range(3):
        for half in range(2):
            units += [("gate", n * 4 + half * 2), ("gate", n * 4 + half * 2 + 1), ("branch", n * 2 + half)]
    units += [("out", i) for i in range(4)]
    return units


BATCHES = [(x, qt, hg) for x in "iabc" for qt in range(2) for hg in range(2)]


def layer_order():
    order, ada = [], [0]

    def ada_unit(n=1):
        for _ in range(n):
            order.append(("unit", "ada", ada[0]))
            if ada[0]:
                order.append(("ada turn", ada[0] - 1))
            ada[0] += 1

    ada_unit(3)
    order.append(("norm",))
    ada_unit(2)
    order.append(("small",))
    for n, (kind, i) in enumerate(layer_units()):
        order.append(("unit", kind, i))
        if n % 3 == 2 and n < 44 and ada[0] < 21:
            ada_unit()
        if n in (31, 37, 40) and ada[0] < 21:
            ada_unit()
        k = (n - 2) // 2
        if n >= 2 and n % 2 == 0:
            if 4 <= k - 1 < len(BATCHES) and BATCHES[k - 1][1]:
                order.append(("turn", k - 1, 1))
            if k < len(BATCHES):
                order.append(("scores", k))
        if n >= 3 and n % 2 == 1:
            if 4 <= k - 1 < len(BATCHES):
                order.append(("values", k - 1))
            if 4 <= k < len(BATCHES):
                order.append(("turn", k, 0))
        if n == 1:
            order += [("rope", "ki"), ("rope", "qi"), ("csum",)]
        if n in (3, 5):
            order.append(("rope", {3: "qa", 5: "ka"}[n]))
        if n in (11, 13):
            order.append(("rope", {11: "qb", 13: "kb"}[n]))
        if 4 <= n <= 7:
            order.append(("topk", 0, n - 4))
        if 9 <= n <= 12:
            order.append(("topk", 1, n - 9))
        if n == 43:
            order.append(("merged",))
            ada_unit(24 - ada[0])
            order.append(("ada turn", 23))
    assert ada[0] == 24
    return order


ORDER = layer_order()
UNITS = [(kind, i) for what, *rest in ORDER if what == "unit" for kind, i in [rest]]
assert len(UNITS) % SLOTS == 0
JOBS = {}
for _kind, _i in UNITS:
    for _j in range(2 if _kind == "branch" else 1):
        JOBS[(_kind, _i, _j)] = len(JOBS)
assert len(JOBS) % BANKS == 0
JOB_AT = {n: job for job, n in JOBS.items()}


def end_order():
    order = [("ctx",), ("final norm",), ("mod norm", 0, 0)]

    def units(kind, n):
        for i in range(n):
            order.append(("unit", kind, i))

    def ffn(layer):
        for grp in range(2):
            for j in range(FC // 2):
                order.append(("unit", f"up{layer}", grp * (FC // 2) + j))
            order.append(("flush", layer, grp))
            for m in range(KC):
                order.append(("unit", f"down{layer}", grp * KC + m))

    units("f", 2)
    order.append(("sgu weights",))
    order.append(("unit", "u", 0))
    order.append(("dft feature", 0))
    order.append(("unit", "u", 1))
    for g in range(4):
        order.append(("dft time", g))
        if g < 3:
            order.append(("dft feature", g + 1))
        if g < 2:
            order.append(("unit", "vs", g))
    order.append(("v norm",))
    for g in range(4):
        order.append(("sgu", g))
    units("eo", 4)
    order.append(("mod norm", 0, 1))
    ffn(0)
    order.append(("mod norm", 1, 0))
    units("nq", 4)
    units("nk", 4)
    order.append(("qk norm", "q"))
    units("nv", 4)
    order.append(("qk norm", "k"))
    for b in range(18):
        if b < 16:
            order.append(("near scores", b))
        if 1 <= b <= 16:
            order.append(("near turn", b - 1))
        if b >= 2:
            order.append(("near values", b - 2))
    units("wo", 4)
    order.append(("mod norm", 1, 1))
    ffn(1)
    order.append(("finish",))
    return order


END = end_order()
END_UNITS = [(kind, i) for what, *rest in END if what == "unit" for kind, i in [rest]]


def end_jobs(kind):
    return 1 if kind in ("nq", "wo", "up1", "down0", "down1") else 2


END_JOBS = {}
for _kind, _i in END_UNITS:
    for _j in range(end_jobs(_kind)):
        END_JOBS[(_kind, _i, _j)] = len(END_JOBS)
END_JOB_AT = {n: job for job, n in END_JOBS.items()}


def end_evacuator(kind, j):
    if kind in ("f", "u", "vs", "nq", "nk", "nv"):
        return "act"
    return "dve"


def evacuator(kind):
    return "dve" if kind in ("branch", "out", "ga", "gb", "gc") else "act"


def mod_col(part):
    return part * KC


def program(nc, ins, out, known, stop=None):
    with ExitStack() as ctx:
        at = [DMA_SCRATCH]

        def sb(name, shape, dt=F32, offset=None):
            size = 4 * int(np.prod(shape[1:]))
            if offset is None:
                offset = at[0]
                at[0] += (size + 31) // 32 * 32
            return nc.alloc_sbuf_tensor_at(name, shape, dt, offset=offset)

        def bank(name, shape):
            return ctx.enter_context(nc.psum_tensor(name, shape, F32))

        def sem(name):
            return ctx.enter_context(nc.semaphore(name))

        raw = sb("raw", [P, SLOTS, UNIT])
        w_hi = sb("w_hi", [P, SLOTS, UNIT], F32R)
        w_lo = sb("w_lo", [P, SLOTS, UNIT], F32R)
        ident = sb("ident", [P, P])
        ones = sb("ones", [P, P])
        vec = sb("vec", [P, VROWS])
        mod = sb("mod", [P, DEPTH, 48, 2])
        s_parts = sb("s_parts", [P, KC, 4], F32R)
        eps = sb("eps", [P, 1])
        x_t = sb("x_t", [P, KC, SEQ])
        base = at[0]

        h_hi = sb("h_hi", [P, KC, SEQ], F32R)
        h_lo = sb("h_lo", [P, KC, SEQ], F32R)
        o_hi = sb("o_hi", [P, 12, SEQ], F32R)
        o_lo = sb("o_lo", [P, 12, SEQ], F32R)
        h = sb("h", [P, KC, SEQ])
        qk = [sb(f"qk{s}", [P, 8, SEQ]) for s in range(2)]
        v = [sb(f"v{s}", [P, 2, WIDTH]) for s in range(2)]
        g = [sb(f"g{s}", [P, 4, SEQ]) for s in range(2)]
        ki = sb("ki", [P, SEQ])
        root = sb("root", [P, SEQ])
        turned = sb("turned", [P, 4, SEQ])
        scaled = sb("scaled", [P, 4, SEQ])
        probs = [sb(f"probs{s}", [P, 4, SEQ]) for s in range(2)]
        probs_t = sb("probs_t", [P, 2, 4, P])
        gates = scaled[:, :, :].rearrange("p (a b) t -> p a b t", a=2)
        rope = sb("rope", [P, 2, SEQ])
        causal = sb("causal", [P, 2, SEQ])
        upto = sb("upto", [P, 2, SEQ])
        picked = sb("picked", [P, 2, SEQ])
        isc = sb("isc", [P, SEQ])
        work = sb("work", [P, SEQ])
        csum_t = sb("csum_t", [P, SEQ])
        logf = sb("logf", [P, 2, P])
        w_small = sb("w_small", [P, KC, 144])
        o_gated = sb("o_gated", [P, 2, 2, P])
        branch_y = turned[:, 0:2, :]
        pick = sb("pick", [P, 8])
        gain = sb("gain", [P, KC])
        ada_bias = sb("ada_bias", [P, 48])
        mod_now = sb("mod_now", [P, 48, 2])
        ada_row = sb("ada_row", [4, 2, 256])
        add_parts = sb("add_parts", [4, 2])
        fbias = sb("fbias", [P, DEPTH, 8])
        fbias_now = sb("fbias_now", [P, 8])
        w_f = sb("w_f", [P, 2, 16])
        f_abs = sb("f_abs", [P, 2, 8])
        f_min = sb("f_min", [P, 2, 8])
        f_log = sb("f_log", [P, 2, 8])
        csum_q = sb("csum_q", [P, 2, 8])
        negmax = sb("negmax", [P, 2, 4])
        rowsum = sb("rowsum", [P, 2, 4])
        rowinv = sb("rowinv", [P, 4])
        top8 = sb("top8", [P, 8])
        s_f = sb("s_f", [P, 2, KC])
        used1 = at[0]
        at[0] = base
        c_t = sb("c_t", [P, KC, CTX])
        m_root = sb("m_root", [P, 512])
        m_rstd = sb("m_rstd", [P, 512])
        m_gain = sb("m_gain", [P, KC, 2])
        h2 = sb("h2", [P, KC, 512])
        h2_at = at[0] - 16384
        h2_hi_at = at[0]
        h2_hi = sb("h2_hi", [P, KC, 512], F32R)
        h2_lo = sb("h2_lo", [P, KC, 512], F32R)
        f_hi_at = at[0]
        f_hi = sb("f_hi", [P, FC // 2, 512], F32R)
        f_lo_at = at[0]
        f_lo = sb("f_lo", [P, FC // 2, 512], F32R)
        area = at[0]
        conv = sb("conv", [P, 2, 512])
        hidden = sb("hidden", [P, 2, 512])
        used2 = at[0]
        f_t = sb("f_t", [P, 4, 512], offset=h2_at)
        dft_f = [sb(f"dft_f{n}", [P, 4, 256], offset=h2_at + 8192 + 4096 * n) for n in range(2)]
        v_sq = sb("v_sq", [P, 4, 512], offset=h2_at)
        gated_b = sb("gated_b", [P, 2, 512], offset=h2_at + 8192)
        u_t = sb("u_t", [P, 4, 512], offset=area)
        v_s = sb("v_s", [P, 4, 512], offset=area + 8192)
        v_sum = sb("v_sum", [P, 16], offset=area + 16384)
        v_inv = sb("v_inv", [P, 16], offset=area + 16448)
        tail = 8 * 2048
        dft_t = sb("dft_t", [P, 2, 2, SEQ], offset=f_hi_at + tail)
        w_s_t = sb("w_s_t", [P, 4, P], offset=f_hi_at + tail + 4096)
        w_s = sb("w_s", [P, 4, P], offset=f_lo_at + tail)
        b_s = sb("b_s", [1, 4, P], offset=f_lo_at + tail + 2048)
        dft_c = sb("dft_c", [P, 2 * P], offset=f_lo_at + tail + 4096)
        k_n = sb("k_n", [P, KC, 512], offset=h2_at)
        v_n = sb("v_n", [P, 4, D], offset=area)
        q_n = sb("q_n", [P, KC, SEQ], offset=f_hi_at + 8192)
        head_sum = sb("head_sum", [P, KC, 16], offset=f_hi_at + 16384)
        head_spread = sb("head_spread", [16, KC, P], offset=f_hi_at + 16896)
        qk_sq = sb("qk_sq", [P, 4, 512], offset=f_lo_at + 8192)
        window = sb("window", [P, SEQ], offset=f_lo_at + 16384)
        near_gated = sb("near_gated", [P, 2, P], offset=f_lo_at + 17408)
        near_max = sb("near_max", [P, 2, 2], offset=f_lo_at + 18432)
        near_sum = sb("near_sum", [P, 2, 2], offset=f_lo_at + 18464)
        near_inv = sb("near_inv", [P, 2], offset=f_lo_at + 18496)
        near_p = [sb(f"near_p{n}", [P, 2, 512], offset=h2_hi_at + 4096 * n) for n in range(3)]
        near_pt = sb("near_pt", [P, 2, 4, 2, P], offset=h2_hi_at + 12288)
        bias = [sb(f"bias{n}", [P, 4, SEQ], offset=h2_hi_at + 20480 + 4096 * n) for n in range(3)]
        out_sb = sb("out_sb", [P, 2, D], offset=h2_at)
        c_in = sb("c_in", [P, 2, D], offset=h2_at)
        used2 = max(used2, area + 16384 + 256)
        assert used2 <= SBUF_BYTES, used2
        x_in = h[:, :, :].rearrange("p c t -> p (c t)").rearrange("p (t f) -> p t f", t=2)
        vec_in = qk[0][:, 0:2, :].rearrange("p a b -> p (a b)")[:, 0:VROWS].rearrange("p (a b) -> p a b", a=3)
        assert used1 <= SBUF_BYTES, used1

        banks_g = bank("banks_g", [P, BANKS, 512])
        bank_g = [banks_g[:, i, :] for i in range(BANKS)]
        bank_s = bank("bank_s", [P, 4, SEQ])
        bank_t = bank("bank_t", [P, 4, P])
        bank_o = bank("bank_o", [P, 512])
        bank_m = bank("bank_m", [P, 512])

        pe_steps, act_steps, dve_steps, pool_steps = (sem(f"{n}_steps") for n in ("pe", "act", "dve", "pool"))
        raw_loaded = [sem(f"raw_loaded{s}") for s in range(SLOTS)]
        consts_loaded = sem("consts_loaded")
        small_loaded = sem("small_loaded")
        stored = sem("stored")
        ctx_loaded = sem("ctx_loaded")
        end_loaded = sem("end_loaded")
        odd_loaded = sem("odd_loaded")
        bias_loaded = [sem(f"bias_loaded{n}") for n in range(3)]
        sp_passed, dve_passed = sem("sp_passed"), sem("dve_passed")
        pe_, act_, dve_, pool_ = (Steps(known.get(n)) for n in ("pe", "act", "dve", "pool"))
        every = (pe_, act_, dve_, pool_)

        def enter(part, layer=0):
            for s in every:
                s.part, s.layer = part, layer

        def loaded(u, layer):
            return layer * (16 * len(UNITS) // SLOTS) + 16 * (u // SLOTS + 1)

        def streams(kind_or_n):
            return 1 if kind_or_n in ("nq", "wo", "up1", "down1") else 2

        end_value, so_far = [], [16 * DEPTH * len(UNITS) // SLOTS] * SLOTS
        for u, (kind, i) in enumerate(END_UNITS):
            so_far[u % SLOTS] += 32 if kind in ("up0", "up1") else 16
            end_value.append(so_far[u % SLOTS])

        def size(kind):
            return FC // 2 * P if kind in ("down0", "down1") else UNIT

        x_streams = (x_t, c_t)
        END_LOADS = 4

        def backwards(t):
            dims = [list(d) for d in t.ap]
            n = dims[-1][1]
            return bass.AP(t.tensor, t.offset + n - 1, dims[:-1] + [[-1, n]])

        def conv_col(ly, tap, i):
            n = ROWS["conv_b"] + ly * FC + i if tap == 3 else ROWS["conv_w"] + (ly * 3 + tap) * FC + i
            return vec[:, n:n + 1]

        def near_banks(b):
            return bank_s[:, :, :].rearrange("p (e a) k -> p e (a k)", e=2) if b % 2 == 0 else banks_g[:, 1:3, :]

        block = ctx.enter_context(nc.Block())

        CONSTS = 9

        @block.sync
        def _(sp):
            enter("start")
            sp.dma_start(x_in, ins["x"][0].rearrange("(t p) f -> p t f", p=P)).then_inc(consts_loaded, 16)
            sp.dma_start(ident[:, :], ins["ident"]).then_inc(consts_loaded, 16)
            sp.dma_start(vec_in, ins["vectors"].rearrange("(a p) f -> p a f", p=P)).then_inc(consts_loaded, 16)
            sp.dma_start(rope[:, :, :], ins["rope"]).then_inc(consts_loaded, 16)
            sp.dma_start(causal[:, :, :], ins["causal"]).then_inc(consts_loaded, 16)
            sp.dma_start(upto[:, :, :], ins["upto"]).then_inc(consts_loaded, 16)
            sp.dma_start(pick[:, :], ins["pick"]).then_inc(consts_loaded, 16)
            sp.dma_start(add_parts[0:4, :], ins["add_parts"]).then_inc(consts_loaded, 16)
            sp.dma_start(fbias[:, :, :].rearrange("p l h -> p (l h)"),
                         ins["forget_bias"].rearrange("(o l) h -> o (l h)", o=1).to_broadcast([P, DEPTH * 8])
                         ).then_inc(consts_loaded, 16)
            with sp.Fori(0, DEPTH) as layer:
                enter("layer", layer)
                w_in_l = ins["w_in"][bass.ds(layer, 1)].rearrange("l (c p) n -> (l p) c n", p=P)

                def columns(c0, n):
                    return w_in_l[:, :, c0:c0 + n]

                sp.wait_ge(pe_steps, pe_.at("small", before=True))
                for d0, c0, n in ((0, K_IDX0, 64), (64, K_IDX0, 80)):
                    sp.dma_start(w_small[:, :, d0:d0 + n], columns(c0, n)).then_inc(small_loaded, 16)
                for u, (kind, i) in enumerate(UNITS):
                    sp.wait_ge(dve_steps, dve_.at(f"lo{(u - SLOTS) % len(UNITS)}", before=u < SLOTS))
                    sp.sem_inc(sp_passed, 1)
                    slot = raw[:, u % SLOTS, :]
                    if kind == "branch":
                        n, half = divmod(i, 2)
                        src = ins["w_branch"][bass.ds(layer, 1), n].rearrange("l (c p) n -> (l p) c n", p=P)[
                            :, :, half * 512:half * 512 + 512]
                        dst = slot.rearrange("p (c n) -> p c n", c=4)
                    else:
                        dst = slot.rearrange("p (c n) -> p c n", c=KC)
                        if kind == "ada":
                            src = ins["ada_w"][bass.ds(layer, 1)].rearrange("l (c p) n -> (l p) c n", p=P)[
                                :, :, i * 256:i * 256 + 256]
                        elif kind == "out":
                            src = ins["w_out"][bass.ds(layer, 1)].rearrange("l (c p) n -> (l p) c n", p=P)[
                                :, :, i * 256:i * 256 + 256]
                        elif kind == "gate":
                            src = columns(MERGE0 + i * 256, 256)
                        elif kind == "qi":
                            src = columns(Q_IDX0 + i * 256, 256)
                        else:
                            section = "abc".index(kind[1]) * 4 + "qkvg".index(kind[0])
                            src = columns(section * WIDTH + i * 256, 256)
                    sp.dma_start(dst, src).then_inc(raw_loaded[u % SLOTS], 16)
            enter("end")
            for u, (kind, i) in enumerate(END_UNITS):
                sp.wait_ge(dve_steps, dve_.at(f"lo{(u - SLOTS) % len(UNITS) if u < SLOTS else u - SLOTS}",
                                              before=u < SLOTS))
                slot = raw[:, u % SLOTS, :]
                cols = slice(i * 256, i * 256 + 256)
                if kind in ("up0", "up1"):
                    src = ins["w_up"][int(kind[2])].rearrange("(c p) (g n) -> p c g n", p=P, g=2)
                    for gv in range(2):
                        sp.dma_start(slot.rearrange("p (c g n) -> p c g n", c=KC, g=2)[:, :, gv, :],
                                     src[:, :, gv, i * P:i * P + P]).then_inc(raw_loaded[u % SLOTS], 16)
                    continue
                if kind in ("down0", "down1"):
                    grp, m = divmod(i, KC)
                    rows = slice(grp * (D_FF // 2), (grp + 1) * (D_FF // 2))
                    src = ins["w_down"][int(kind[4]), rows, m * P:m * P + P].rearrange("(c p) n -> p c n", p=P)
                    dst = slot[:, 0:FC // 2 * P].rearrange("p (c n) -> p c n", c=FC // 2)
                else:
                    dst = slot.rearrange("p (c n) -> p c n", c=KC)
                    name, c0 = {"f": ("even_in", 0), "u": ("even_in", 512), "vs": ("even_in", 1024),
                                "eo": ("even_out", 0), "nq": ("qkv", 0), "nk": ("qkv", D), "nv": ("qkv", 2 * D),
                                "wo": ("odd_out", 0)}[kind]
                    src = ins[name].rearrange("(c p) n -> p c n", p=P)[:, :, c0 + i * 256:c0 + i * 256 + 256]
                sp.dma_start(dst, src).then_inc(raw_loaded[u % SLOTS], 16)
            sp.wait_ge(act_steps, act_.at("out1"))
            sp.dma_start(out.rearrange("o (t p) f -> p (o t) f", p=P), out_sb[:, :, :]).then_inc(stored, 16)
            sp.wait_ge(stored, 16)

        @block.tensor
        def _(pe):
            enter("start")
            pe.sem_inc(pe_steps, pe_.total("layer") or 1)
            pe.wait_ge(consts_loaded, 16 * CONSTS)
            for b in range(4):
                for j in range(2):
                    for t in range(2):
                        dst = [bank_s[:, 0:2, :], bank_s[:, 2:4, :], bank_o[:, :].rearrange("p (j t) -> p j t", j=2),
                               bank_m[:, :].rearrange("p (j t) -> p j t", j=2)][b][:, j, t * P:t * P + P]
                        last = nc.tensor.transpose(dst, x_in[:, t, (2 * b + j) * P:(2 * b + j + 1) * P], ident[:, :])
                last.then_inc(pe_steps, pe_.step(f"x turned{b}"))
            for a in range(3):
                last = nc.tensor.transpose(bank_t[:, a, :], vec_in[:, a, :], ident[:, :])
            last.then_inc(pe_steps, pe_.step("vec turned"))

            with pe.Fori(0, DEPTH) as layer:
                enter("layer", layer)
                u = 0
                bank_m_read = []
                for what, *arg in ORDER:
                    if what == "unit":
                        kind, i = arg
                        s = u % SLOTS
                        need = [f"lo{u}"]
                        kcs = 4 if kind == "branch" else KC
                        wh = w_hi[:, s, :].rearrange("p (c n) -> p c n", c=kcs)
                        wl = w_lo[:, s, :].rearrange("p (c n) -> p c n", c=kcs)
                        if kind in ("qi", "qa") and i == 0:
                            need.append("h lo1")
                        if kind == "branch" and i % 2 == 0:
                            need.append(f"o lo{7 + 4 * (i // 2)}")
                        if kind == "out" and i == 0:
                            need.append("merged lo1")
                        for j in range(2 if kind == "branch" else 1):
                            k = JOBS[(kind, i, j)]
                            gb = bank_g[k % BANKS]
                            b3 = (k - BANKS) % len(JOBS)
                            who = evacuator(JOB_AT[b3][0])
                            if who == "dve":
                                need.append(("<" if k < BANKS else "") + f"empty{b3}")
                            else:
                                pe.wait_ge(act_steps, act_.at(f"empty{b3}", before=k < BANKS))
                            if need:
                                pe.wait_ge(dve_steps, dve_.latest(*need))
                            need = []
                            if kind == "ada":
                                for c in range(KC):
                                    for w in (wl, wh):
                                        last = nc.tensor.matmul(gb[0:4, 0:256], s_parts[:, c, :], w[:, c, :],
                                                                start=c == 0 and w is wl,
                                                                stop=c == KC - 1 and w is wh)
                            elif kind[0] == "v":
                                ov = gb[:, :].rearrange("p (t n) -> p t n", t=2)
                                for t in range(2):
                                    for c in range(KC):
                                        for n, (a, w) in enumerate(((h_lo, wh), (h_hi, wl), (h_hi, wh))):
                                            last = nc.tensor.matmul(ov[:, t, :], a[:, c, t * P:t * P + P], w[:, c, :],
                                                                    start=c == 0 and n == 0,
                                                                    stop=c == KC - 1 and n == 2)
                            else:
                                ov = gb[:, :].rearrange("p (m t) -> p m t", m=2)
                                ah, al, a0 = (o_hi, o_lo, 4 * (i // 2)) if kind == "branch" else (h_hi, h_lo, 0)
                                for m in range(2):
                                    m0 = j * 256 + m * P
                                    for c in range(kcs):
                                        for n, (w, a) in enumerate(((wl, ah), (wh, al), (wh, ah))):
                                            last = nc.tensor.matmul(ov[:, m, :], w[:, c, m0:m0 + P], a[:, a0 + c, :],
                                                                    start=c == 0 and n == 0,
                                                                    stop=c == kcs - 1 and n == 2)
                            last.then_inc(pe_steps, pe_.step(f"job{k}", f"unit{u}"))
                        u += 1
                    elif what == "ada turn":
                        i, = arg
                        pe.wait_ge(act_steps, act_.latest(f"ada row{i}", *bank_m_read))
                        if i == 0:
                            pe.wait_ge(dve_steps, dve_.at("mod now", before=True))
                        for m in range(2):
                            n = ADA_COL + 4 * i + 2 * m
                            last = nc.tensor.matmul(bank_m[:, n:n + 2], ada_row[0:4, i % 2, m * P:m * P + P],
                                                    add_parts[0:4, :], start=True, stop=True)
                        last.then_inc(pe_steps, pe_.step(f"ada turn{i}"))
                    elif what == "norm":
                        for half in range(2):
                            pe.wait_ge(act_steps, act_.at(f"squares{half}"))
                            for c in range(4 * half, 4 * half + 4):
                                last = nc.tensor.matmul(bank_m[:, 0:SEQ], ones[:, :], qk[1][:, c, :],
                                                        start=c == 0, stop=c == KC - 1)
                        last.then_inc(pe_steps, pe_.step("sumsq"))
                        bank_m_read = ["root"]
                    elif what == "small":
                        pe.wait_ge(small_loaded, layer * 32 + 32)
                        pe.wait_ge(dve_steps, dve_.at("h"))
                        pe.wait_ge(act_steps, act_.at("root"))
                        for c in range(KC):
                            nc.tensor.matmul(bank_m[:, 0:SEQ], w_small[:, c, 0:P], h[:, c, :],
                                             start=c == 0, stop=c == KC - 1)
                        for t in range(2):
                            for c in range(KC):
                                last = nc.tensor.matmul(bank_o[:, t * 16:t * 16 + 16], h[:, c, t * P:t * P + P],
                                                        w_small[:, c, P:144], start=c == 0, stop=c == KC - 1)
                        last.then_inc(pe_steps, pe_.step("small"))
                        bank_m_read = ["ki"]
                    elif what == "csum":
                        pe.wait_ge(dve_steps, dve_.at("logf"))
                        pe.wait_ge(act_steps, act_.at("ki"))
                        for j in range(2):
                            nc.tensor.matmul(bank_m[:, 0:SEQ], logf[:, j, :], upto[:, j, :], start=j == 0, stop=j == 1)
                        for qt in range(2):
                            for j in range(qt + 1):
                                last = nc.tensor.matmul(bank_o[:, 32 + qt * 8:40 + qt * 8],
                                                        upto[:, j, qt * P:qt * P + P], logf[:, j, 0:8],
                                                        start=j == 0, stop=j == qt)
                        last.then_inc(pe_steps, pe_.step("csum"))
                        bank_m_read = ["csum t"]
                    elif what == "scores":
                        k, = arg
                        x, qt, hg = BATCHES[k]
                        nk = P * (qt + 1)
                        need = ["<masked15"] if k == 0 else [f"masked{k - 1}"] if k > 4 else []
                        if 0 < k <= 4:
                            pe.wait_ge(act_steps, act_.at(f"relu{k - 1}"))
                        if x == "i":
                            need.append("rope qi")
                            qs, ks, kc = qk[1], ki, None
                        else:
                            qs = ks = qk[SETS[x]]
                            kc = 4
                            if x == "c":
                                pe.wait_ge(act_steps, act_.latest(f"empty{JOBS[('kc', 1, 0)]}", "csum"))
                            else:
                                need.append("rope k" + x)
                        pe.wait_ge(dve_steps, dve_.latest(*need))
                        for e in range(2):
                            r = slice(64 * e, 64 * e + 64)
                            for j in range(2):
                                c = 2 * hg + j
                                dst = bank_s[:, 2 * e + j, 0:nk]
                                if x == "c":
                                    hh = 4 * hg + 2 * j + e
                                    nc.tensor.matmul(dst, pick[r, hh:hh + 1].to_broadcast([64, P]), csum_t[r, 0:nk],
                                                     start=True, stop=False)
                                keys = ks[r, 0:nk] if kc is None else ks[r, kc + c, 0:nk]
                                last = nc.tensor.matmul(dst, qs[r, c, qt * P:qt * P + P], keys,
                                                        start=x != "c", stop=True)
                        last.then_inc(pe_steps, pe_.step(f"scores{k}"))
                    elif what == "turn":
                        k, kt = arg
                        pe.wait_ge(dve_steps, dve_.at(f"probs{k}"))
                        if (k, kt) == (4, 0):
                            pe.wait_ge(act_steps, act_.at(f"turned15 {BATCHES[15][1]}", before=True))
                        else:
                            pk, pt = (k, 0) if kt else (k - 1, BATCHES[k - 1][1])
                            pe.wait_ge(act_steps, act_.at(f"turned{pk} {pt}"))
                        for s in range(4):
                            last = nc.tensor.transpose(bank_t[:, s, :], probs[k % 2][:, s, kt * P:kt * P + P],
                                                       ident[:, :])
                        last.then_inc(pe_steps, pe_.step(f"turn{k} {kt}"))
                    elif what == "values":
                        k, = arg
                        x, qt, hg = BATCHES[k]
                        pe.wait_ge(act_steps, act_.latest(f"turned{k} {qt}", f"empty{JOBS[('v' + x, 1, 0)]}", "csum"))
                        if k > 4:
                            pe.wait_ge(dve_steps, dve_.at(f"gated{k - 1}"))
                        for e in range(2):
                            for j in range(2):
                                hh = 4 * hg + 2 * j + e
                                for kt in range(qt + 1):
                                    last = nc.tensor.matmul(bank_o[64 * e:64 * e + 64, j * P:j * P + P],
                                                            v[SETS[x]][:, kt, hh * HD:hh * HD + HD],
                                                            probs_t[:, kt, 2 * e + j, :], start=kt == 0, stop=kt == qt)
                        last.then_inc(pe_steps, pe_.step(f"values{k}"))

            enter("end")

            def lanes(t):
                return t[:, :].rearrange("p (a b) -> p a b", a=4)

            u = 0
            for what, *arg in END:
                if what == "unit":
                    kind, i = arg
                    st = u % SLOTS
                    n_s = streams(kind)
                    nt = SEQ * n_s
                    down, up = kind[:4] == "down", kind[:2] == "up"
                    kcs = FC // 2 if down else KC
                    wide = P if down else 256
                    wh = w_hi[:, st, 0:kcs * wide].rearrange("p (c n) -> p c n", c=kcs)
                    wl = w_lo[:, st, 0:kcs * wide].rearrange("p (c n) -> p c n", c=kcs)
                    pe.wait_ge(dve_steps, dve_.at(f"lo{u}"))
                    ah, al, a_ready = h2_hi, h2_lo, None
                    if i == 0 and kind in ("f", "nq", "up0", "up1"):
                        tag = {"f": "00", "nq": "10", "up0": "01", "up1": "11"}[kind]
                        a_ready = [f"h2 lo{tag} {c}" for c in range(KC)]
                    if kind == "eo":
                        ah, al = f_hi, f_lo
                        a_ready = [f"a lo{c}" for c in range(4)] + [f"b lo{c}" for c in range(4)] if i == 0 else None
                    if kind == "wo":
                        ah, al = (t[:, 0:4, :].rearrange("p a (b t) -> p (a b) t", b=2) for t in (f_hi, f_lo))
                        a_ready = ["near lo15"] * KC if i == 0 else None
                    if down:
                        ah, al = f_hi, f_lo
                        if i % KC == 0:
                            pe.wait_ge(dve_steps, dve_.at(f"f lo{kind[4]} {i // KC * (FC // 2) + FC // 2 - 1}"))
                    for j in range(end_jobs(kind)):
                        k = END_JOBS[(kind, i, j)]
                        if k < BANKS:
                            pe.wait_ge(dve_steps, dve_.at(f"empty{len(JOBS) - BANKS + k}", before=True))
                        elif end_evacuator(*END_JOB_AT[k - BANKS][::2]) == "dve":
                            pe.wait_ge(dve_steps, dve_.at(f"empty{k - BANKS}"))
                        else:
                            pe.wait_ge(act_steps, act_.at(f"empty{k - BANKS}"))
                        gb = bank_g[k % BANKS]
                        if kind in ("vs", "nv"):
                            for tt in range(2):
                                t0 = (2 * j + tt) * P
                                for c in range(KC):
                                    for n, (a, w) in enumerate(((h2_lo, wh), (h2_hi, wl), (h2_hi, wh))):
                                        last = nc.tensor.matmul(gb[:, tt * 256:tt * 256 + 256], a[:, c, t0:t0 + P],
                                                                w[:, c, :], start=c == 0 and n == 0,
                                                                stop=c == KC - 1 and n == 2)
                        else:
                            chunks = 1 if nt == 512 or down else 2
                            for m in range(chunks):
                                m0 = (j * chunks + m) * P
                                for c in range(kcs):
                                    if a_ready and j == 0 and m == 0:
                                        pe.wait_ge(dve_steps, dve_.at(a_ready[c]))
                                    for n, (w, a) in enumerate(((wl, ah), (wh, al), (wh, ah))):
                                        last = nc.tensor.matmul(gb[:, m * SEQ:m * SEQ + nt], w[:, c, m0:m0 + P],
                                                                a[:, c, 0:nt], start=c == 0 and n == 0,
                                                                stop=c == kcs - 1 and n == 2)
                        last.then_inc(pe_steps, pe_.step(f"job{k}", f"unit{u}"))
                    u += 1
                elif what == "ctx":
                    pe.wait_ge(ctx_loaded, 16)
                    for b in range(4):
                        dst = [bank_s[:, 0:2, :], bank_s[:, 2:4, :], bank_o[:, :].rearrange("p (j t) -> p j t", j=2),
                               bank_t[:, :, :].rearrange("p (j t) n -> p j (t n)", j=2)][b]
                        for j in range(2):
                            for t in range(2):
                                last = nc.tensor.transpose(dst[:, j, t * P:t * P + P],
                                                           c_in[:, t, (2 * b + j) * P:(2 * b + j + 1) * P], ident[:, :])
                        last.then_inc(pe_steps, pe_.step(f"ctx turned{b}"))
                elif what in ("final norm", "mod norm"):
                    tag = "f" if what == "final norm" else f"{arg[0]}{arg[1]}"
                    nt = SEQ if tag in ("f", "11") else 512
                    for half in range(2):
                        pe.wait_ge(act_steps, act_.at(f"squares{tag} {half}"))
                        for c in range(4 * half, 4 * half + 4):
                            last = nc.tensor.matmul(bank_m[:, 0:nt], ones[:, :], h2[:, c, 0:nt],
                                                    start=c == 0, stop=c == KC - 1)
                    last.then_inc(pe_steps, pe_.step(f"sumsq{tag}"))
                elif what == "sgu weights":
                    pe.wait_ge(end_loaded, 16 * END_LOADS)
                    pe.wait_ge(act_steps, act_.at("ctx3"))
                    for g_ in range(4):
                        last = nc.tensor.transpose(bank_t[:, g_, :], w_s[:, g_, :], ident[:, :])
                    last.then_inc(pe_steps, pe_.step("sgu weights"))
                elif what == "dft feature":
                    g_, = arg
                    pe.wait_ge(act_steps, act_.at("dft feature" + str(g_ - 1) if g_ else f"empty{END_JOBS[('f', 1, 1)]}"))
                    for t in range(4):
                        last = nc.tensor.matmul(bank_s[:, t, :], f_t[:, g_, t * P:t * P + P], dft_c[:, :],
                                                start=True, stop=True)
                    last.then_inc(pe_steps, pe_.step(f"dft feature{g_}"))
                elif what == "dft time":
                    g_, = arg
                    pe.wait_ge(act_steps, act_.at(f"dft feature{g_}"))
                    if g_:
                        pe.wait_ge(dve_steps, dve_.at(f"a lo{g_ - 1}"))
                    bt = bank_t[:, :, :].rearrange("p a b -> p (a b)")
                    for s_ in range(2):
                        n = 0
                        for t in range(2):
                            for cs in range(2):
                                last = nc.tensor.matmul(bt[:, s_ * SEQ:s_ * SEQ + SEQ],
                                                        dft_f[g_ % 2][:, 2 * s_ + t, cs * P:cs * P + P],
                                                        dft_t[:, t, cs, :], start=n == 0, stop=n == 3)
                                n += 1
                    last.then_inc(pe_steps, pe_.step(f"dft time{g_}"))
                elif what == "sgu":
                    g_, = arg
                    pe.wait_ge(dve_steps, dve_.at(f"gated b{g_ - 1}" if g_ else "v norm"))
                    pe.wait_ge(act_steps, act_.at("ctx3"))
                    nc.tensor.matmul(bank_o[:, :], ones[0:1, :], b_s[0:1, g_:g_ + 1, :].to_broadcast([1, 4, P]),
                                     start=True, stop=False)
                    for t in range(4):
                        last = nc.tensor.matmul(bank_o[:, t * P:t * P + P], v_s[:, t, g_ * P:g_ * P + P],
                                                w_s_t[:, g_, :], start=False, stop=t == 3)
                    last.then_inc(pe_steps, pe_.step(f"sgu{g_}"))
                elif what == "qk norm":
                    x, = arg
                    src = qk_sq[:, :, :].rearrange("p a (b t) -> p (a b) t", b=2) if x == "q" else qk_sq
                    nt = SEQ if x == "q" else 512
                    for c in range(KC):
                        if c == 0 or (x == "k" and c == 4):
                            pe.wait_ge(act_steps, act_.at(f"squares{x}{0 if c == 0 else 1}"))
                            if c == 0:
                                pe.wait_ge(odd_loaded, 16 * 3)
                        last = nc.tensor.matmul(bank_m[0:16, 0:nt], head_sum[:, c, :], src[:, c % (8 if x == "q" else 4), :],
                                                start=c == 0, stop=c == KC - 1)
                        if c == 3:
                            last.then_inc(pe_steps, pe_.step(f"sumsq{x} half"))
                    last.then_inc(pe_steps, pe_.step(f"sumsq{x}"))
                    pe.wait_ge(dve_steps, dve_.at(f"rstd{x}"))
                    for c in range(KC):
                        dst = (bank_t[:, :, :].rearrange("p a b -> p (a b)") if c % 2 == 0 else bank_o)[:, 0:nt]
                        if c >= 2:
                            pe.wait_ge(dve_steps, dve_.at(f"normed{x}{c - 2}"))
                        nc.tensor.matmul(dst, head_spread[0:16, c, :], m_rstd[0:16, 0:nt], start=True, stop=True
                                         ).then_inc(pe_steps, pe_.step(f"spread{x}{c}"))
                elif what == "near scores":
                    b, = arg
                    qt, c = divmod(b, KC)
                    if b == 0:
                        pe.wait_ge(dve_steps, dve_.at("normedk7"))
                        pe.wait_ge(act_steps, act_.at(f"empty{END_JOBS[('nv', 3, 1)]}"))
                    if b >= 2:
                        pe.wait_ge(dve_steps, dve_.at(f"near masked{b - 2}"))
                    for e in range(2):
                        r = slice(64 * e, 64 * e + 64)
                        last = nc.tensor.matmul(near_banks(b)[:, e, :], q_n[r, c, qt * P:qt * P + P], k_n[r, c, :],
                                                start=True, stop=True)
                    last.then_inc(pe_steps, pe_.step(f"near scores{b}"))
                elif what == "near turn":
                    b, = arg
                    pe.wait_ge(dve_steps, dve_.at(f"near probs{b}"))
                    for hf in range(2):
                        if b:
                            pe.wait_ge(act_steps, act_.at(f"near turned{b - 1} {hf}"))
                        for kt in range(2):
                            for e in range(2):
                                dst = bank_t[:, 2 * kt + e, :] if hf == 0 else lanes(bank_m)[:, 2 * kt + e, :]
                                t0 = (2 * hf + kt) * P
                                last = nc.tensor.transpose(dst, near_p[b % 3][:, e, t0:t0 + P], ident[:, :])
                        last.then_inc(pe_steps, pe_.step(f"near turn{b} {hf}"))
                elif what == "near values":
                    b, = arg
                    qt, c = divmod(b, KC)
                    pe.wait_ge(act_steps, act_.at(f"near turned{b} 1"))
                    if b >= 2:
                        pe.wait_ge(dve_steps, dve_.at(f"near lo{b - 2}"))
                    ob = bank_o if b % 2 == 0 else bank_g[0]
                    for e in range(2):
                        for kt in range(4):
                            hh = 2 * c + e
                            last = nc.tensor.matmul(ob[64 * e:64 * e + 64, 0:P], v_n[:, kt, hh * HD:hh * HD + HD],
                                                    near_pt[:, b % 2, kt, e, :], start=kt == 0, stop=kt == 3)
                    last.then_inc(pe_steps, pe_.step(f"near values{b}"))
                elif what == "finish":
                    pe.wait_ge(dve_steps, dve_.at(f"empty{len(END_JOBS) - 1}"))
                    for b in range(4):
                        t, c4 = divmod(b, 2)
                        for n in range(4):
                            dst = [bank_s[:, 0:2, :], bank_s[:, 2:4, :]][b] if b < 2 else None
                            dst = dst.rearrange("p a (b n) -> p (a b) n", b=2) if b < 2 else (
                                lanes(bank_o) if b == 2 else bank_t)
                            last = nc.tensor.transpose(dst[:, n, :], x_t[:, 4 * c4 + n, t * P:t * P + P], ident[:, :])
                        last.then_inc(pe_steps, pe_.step(f"finish{b}"))

        @block.scalar
        def _(act):
            enter("start")
            act.sem_inc(act_steps, act_.total("layer") or 1)
            for b in range(4):
                act.wait_ge(pe_steps, pe_.at(f"x turned{b}"))
                src = [bank_s[:, 0:2, :], bank_s[:, 2:4, :], bank_o[:, :].rearrange("p (j t) -> p j t", j=2),
                       bank_m[:, :].rearrange("p (j t) -> p j t", j=2)][b]
                nc.scalar.activation(x_t[:, 2 * b:2 * b + 2, :], src, ACT.Copy).then_inc(act_steps, act_.step("x"))
            act.wait_ge(pe_steps, pe_.at("vec turned"))
            nc.scalar.activation(vec[:, :].rearrange("p (a b) -> p a b", a=3), bank_t[:, 0:3, :], ACT.Copy
                                 ).then_inc(act_steps, act_.step("vec"))
            act.wait_ge(act_steps, act_.last())
            cc = vec[:, ROWS["c"]:ROWS["c"] + 16].rearrange("p (s c) -> p s c", s=2)
            nc.scalar.activation(s_f[:, :, :], cc, ACT.Tanh, scale=0.5).then_inc(act_steps, act_.step("s tanh"))
            act.wait_ge(dve_steps, dve_.at("s"))
            for s in range(2):
                nc.scalar.activation(s_parts[:, :, s], s_f[:, s, :], ACT.Copy, scale=0.5
                                     ).then_inc(act_steps, act_.step("s hi"))

            with act.Fori(0, DEPTH) as layer:
                enter("layer", layer)

                def high(u):
                    act.wait_ge(raw_loaded[u % SLOTS], loaded(u, layer))
                    act.wait_ge(pe_steps, pe_.at(f"unit{(u - SLOTS) % len(UNITS)}", before=u < SLOTS))
                    nc.scalar.activation(w_hi[:, u % SLOTS, :], raw[:, u % SLOTS, :], ACT.Copy
                                         ).then_inc(act_steps, act_.step(f"hi{u}"))

                for u in range(AHEAD):
                    high(u)
                act.wait_ge(dve_steps, dve_.at(f"empty{len(JOBS) - 1}", before=True))
                act.wait_ge(act_steps, act_.last())
                for half in range(2):
                    c = slice(4 * half, 4 * half + 4)
                    nc.scalar.activation(qk[1][:, c, :], x_t[:, c, :], ACT.Square
                                         ).then_inc(act_steps, act_.step(f"squares{half}"))
                u = 0
                for what, *arg in ORDER:
                    if what == "unit":
                        kind, i = arg
                        if u + AHEAD < len(UNITS):
                            high(u + AHEAD)
                        for j in range(2 if kind == "branch" else 1):
                            k = JOBS[(kind, i, j)]
                            gb = bank_g[k % BANKS][:, :].rearrange("p (m t) -> p m t", m=2)
                            if kind == "qi":
                                dst = qk[1][:, 2 * i:2 * i + 2, :]
                            elif kind[0] == "q" or kind[0] == "k":
                                c = (0 if kind[0] == "q" else 4) + 2 * i
                                dst = qk[SETS[kind[1]]][:, c:c + 2, :]
                            elif kind[0] == "v":
                                dst = v[SETS[kind[1]]][:, :, i * 256:i * 256 + 256]
                            elif kind == "gate":
                                if i == 0:
                                    act.wait_ge(dve_steps, dve_.at("rope kb"))
                                if i >= 2:
                                    act.wait_ge(dve_steps, dve_.at(f"empty{JOBS[('branch', (i - 2) // 2, i % 2)]}"))
                                dst = gates[:, i % 2, :, :]
                            elif kind[0] == "g":
                                if kind == "gc" and i == 0:
                                    act.wait_ge(dve_steps, dve_.at("gated7"))
                                dst = g[SETS[kind[1]]][:, 2 * i:2 * i + 2, :]
                            elif kind == "ada":
                                act.wait_ge(pe_steps, pe_.at(f"job{k}"))
                                if i >= 2:
                                    act.wait_ge(pe_steps, pe_.at(f"ada turn{i - 2}"))
                                nc.scalar.activation(ada_row[0:4, i % 2, :], bank_g[k % BANKS][0:4, 0:256], ACT.Copy
                                                     ).then_inc(act_steps, act_.step(f"empty{k}", f"ada row{i}"))
                                continue
                            else:
                                continue
                            act.wait_ge(pe_steps, pe_.at(f"job{k}"))
                            if kind[0] == "g":
                                nc.scalar.activation(dst, gb, ACT.Tanh, scale=0.5).then_inc(
                                    act_steps, act_.step(f"tanh{k}", f"empty{k}"))
                            else:
                                nc.scalar.activation(dst, gb, ACT.Copy).then_inc(act_steps, act_.step(f"empty{k}"))
                        u += 1
                    elif what == "norm":
                        act.wait_ge(pe_steps, pe_.at("sumsq"))
                        nc.scalar.activation(root[:, 0:SEQ], bank_m[:, 0:SEQ], ACT.Sqrt, scale=1.0 / D, bias=eps[:, 0:1]
                                             ).then_inc(act_steps, act_.step("root"))
                        for half in range(2):
                            c = slice(4 * half, 4 * half + 4)
                            act.wait_ge(dve_steps, dve_.at(f"h{half}"))
                            nc.scalar.activation(h_hi[:, c, :], h[:, c, :], ACT.Copy
                                                 ).then_inc(act_steps, act_.step(f"h hi{half}"))
                    elif what == "small":
                        act.wait_ge(pe_steps, pe_.at("small"))
                        nc.scalar.activation(ki[:, :], bank_m[:, 0:SEQ], ACT.Copy
                                             ).then_inc(act_steps, act_.step("ki"))
                        act.wait_ge(dve_steps, dve_.at("f abs"))
                        nc.scalar.activation(f_log[:, :, :], f_abs[:, :, :], ACT.Exp, scale=-1.0
                                             ).then_inc(act_steps, act_.step("f exp"))
                        act.wait_ge(act_steps, act_.last())
                        nc.scalar.activation(f_log[:, :, :], f_log[:, :, :], ACT.Ln, bias=ones[:, 0:1]
                                             ).then_inc(act_steps, act_.step("f log"))
                    elif what == "csum":
                        act.wait_ge(pe_steps, pe_.at("csum"))
                        nc.scalar.activation(csum_t[:, :], bank_m[:, 0:SEQ], ACT.Copy
                                             ).then_inc(act_steps, act_.step("csum t"))
                        nc.scalar.activation(csum_q[:, :, :], bank_o[:, 32:48].rearrange("p (a b) -> p a b", a=2),
                                             ACT.Copy).then_inc(act_steps, act_.step("csum"))
                    elif what == "scores":
                        k, = arg
                        x, qt, hg = BATCHES[k]
                        nk = P * (qt + 1)
                        pb = probs[k % 2]
                        if x == "i":
                            act.wait_ge(pe_steps, pe_.at(f"scores{k}"))
                            if k >= 2:
                                act.wait_ge(dve_steps, dve_.at(f"index{k - 2}"))
                            nc.scalar.activation(pb[:, :, 0:nk], bank_s[:, :, 0:nk], ACT.Relu
                                                 ).then_inc(act_steps, act_.step(f"relu{k}"))
                        else:
                            act.wait_ge(dve_steps, dve_.at(f"negmax{k}"))
                            for s in range(4):
                                last = nc.scalar.activation(pb[:, s, 0:nk], pb[:, s, 0:nk], ACT.Exp,
                                                            bias=negmax[:, k % 2, s:s + 1],
                                                            accum_out=rowsum[:, k % 2, s:s + 1])
                                last.then_inc(act_steps, act_.step(f"exp{k}"))
                    elif what == "turn":
                        k, kt = arg
                        act.wait_ge(pe_steps, pe_.at(f"turn{k} {kt}"))
                        nc.scalar.activation(probs_t[:, kt, :, :], bank_t[:, :, :], ACT.Copy
                                             ).then_inc(act_steps, act_.step(f"turned{k} {kt}"))
                    elif what == "values":
                        k, = arg
                        x, qt, hg = BATCHES[k]
                        c = 4 * "abc".index(x) + 2 * hg
                        act.wait_ge(dve_steps, dve_.at(f"gated{k}"))
                        nc.scalar.activation(o_hi[:, c:c + 2, qt * P:qt * P + P], o_gated[:, k % 2, :, :], ACT.Copy
                                             ).then_inc(act_steps, act_.step(f"o hi{k}"))
                    elif what == "merged":
                        act.wait_ge(pe_steps, pe_.at(f"job{JOBS[('gate', 11, 0)]}"))
                        for half in range(2):
                            c = slice(4 * half, 4 * half + 4)
                            act.wait_ge(dve_steps, dve_.at(f"empty{JOBS[('branch', 4 + half, 1)]}"))
                            nc.scalar.activation(h_hi[:, c, :], h[:, c, :], ACT.Copy, scale=0.5
                                                 ).then_inc(act_steps, act_.step(f"merged hi{half}"))
            enter("end")
            act.wait_ge(dve_steps, dve_.at("mod"))

            def high(u):
                n = size(END_UNITS[u][0])
                act.wait_ge(raw_loaded[u % SLOTS], end_value[u])
                act.wait_ge(pe_steps, pe_.at(f"unit{len(UNITS) - SLOTS + u if u < SLOTS else u - SLOTS}",
                                             before=u < SLOTS))
                nc.scalar.activation(w_hi[:, u % SLOTS, 0:n], raw[:, u % SLOTS, 0:n], ACT.Copy
                                     ).then_inc(act_steps, act_.step(f"hi{u}"))

            act.dma_start(c_in[:, :, :], ins["ctx"][0].rearrange("(t p) f -> p t f", p=P)).then_inc(ctx_loaded, 16)
            act.dma_start(dft_c[:, :], ins["dft_c"]).then_inc(end_loaded, 16)
            act.dma_start(dft_t[:, :, :, :], ins["dft_t"]).then_inc(end_loaded, 16)
            act.dma_start(w_s[:, :, :], ins["w_s"].rearrange("g p q -> p g q")).then_inc(end_loaded, 16)
            act.dma_start(b_s[0:1, :, :], ins["b_s"].rearrange("(o g) p -> o g p", o=1)).then_inc(end_loaded, 16)

            def load_bias(n):
                qt, h4 = divmod(n, 4)
                for r in range(2):
                    src = bass.AP(ins["rpb"].tensor, ((2 * qt + r) * 16 + 4 * h4) * 4 * 31, [[1, 64], [31, 16], [1, 64]])
                    act.dma_start(bias[n % 3][64 * r:64 * r + 64, :, :].rearrange("p h (i k) -> p (h i) k", i=4),
                                  src).then_inc(bias_loaded[n % 3], 16)

            def silu(ly, i):
                act.wait_ge(dve_steps, dve_.at(f"conv{ly} {i}"))
                n = SEQ * streams(f"up{ly}")
                nc.scalar.activation(conv[:, i % 2, 0:n], conv[:, i % 2, 0:n], ACT.Silu
                                     ).then_inc(act_steps, act_.step(f"silu{ly} {i}"))

            def hidden_high(ly, i):
                act.wait_ge(dve_steps, dve_.at(f"hidden{ly} {i}"))
                if i == FC // 2:
                    act.wait_ge(pe_steps, pe_.at(f"job{END_JOBS[(f'down{ly}', KC - 1, 0)]}"))
                n = SEQ * streams(f"up{ly}")
                nc.scalar.activation(f_hi[:, i % (FC // 2), 0:n], hidden[:, i % 2, 0:n], ACT.Copy
                                     ).then_inc(act_steps, act_.step(f"f hi{ly} {i}"))

            for u in range(AHEAD):
                high(u)
            u = 0
            for what, *arg in END:
                if what == "unit":
                    kind, i = arg
                    up = kind[:2] == "up"
                    if up:
                        ly = int(kind[2])
                        n_s = streams(kind)
                        first = i % (FC // 2) == 0
                        if not first:
                            silu(ly, i - 1)
                    if u + AHEAD < len(END_UNITS):
                        high(u + AHEAD)
                    if up:
                        k = END_JOBS[(kind, i, 0)]
                        act.wait_ge(pe_steps, pe_.at(f"job{k}"))
                        if i >= 2:
                            act.wait_ge(dve_steps, dve_.at(f"hidden{ly} {i - 2}"))
                        act.wait_ge(act_steps, act_.last())
                        nc.scalar.activation(conv[:, i % 2, 0:n_s * SEQ], bank_g[k % BANKS][:, 0:n_s * SEQ],
                                             ACT.Identity, scale=conv_col(ly, 1, i), bias=conv_col(ly, 3, i)
                                             ).then_inc(act_steps, act_.step(f"conv{ly} {i}"))
                        if not first:
                            hidden_high(ly, i - 1)
                    for j in range(end_jobs(kind)):
                        k = END_JOBS[(kind, i, j)]
                        if end_evacuator(kind, j) != "act":
                            continue
                        act.wait_ge(pe_steps, pe_.at(f"job{k}"))
                        gb = bank_g[k % BANKS]
                        fn = ACT.Copy
                        src = gb[:, :]
                        if kind == "f":
                            if i == 0 and j == 0:
                                act.wait_ge(dve_steps, dve_.at("h2 lo00 7"))
                            dst = f_t[:, 2 * i + j, :]
                        elif kind == "u":
                            dst, fn = u_t[:, 2 * i + j, :], ACT.Gelu_apprx_tanh
                        elif kind == "vs":
                            fn = ACT.Gelu_apprx_tanh
                            src = gb.rearrange("p (t n) -> p t n", t=2)
                            dst = v_s[:, 2 * j:2 * j + 2, i * 256:i * 256 + 256]
                        elif kind == "nq":
                            src = gb.rearrange("p (m t) -> p m t", m=2)
                            dst = q_n[:, 2 * i:2 * i + 2, :]
                        elif kind == "nk":
                            if i == 0 and j == 0:
                                act.wait_ge(dve_steps, dve_.at("h2 lo10 7"))
                            dst = k_n[:, 2 * i + j, :]
                        else:
                            src = gb.rearrange("p (t n) -> p t n", t=2)
                            dst = v_n[:, 2 * j:2 * j + 2, i * 256:i * 256 + 256]
                        nc.scalar.activation(dst, src, fn).then_inc(act_steps, act_.step(f"empty{k}"))
                    u += 1
                elif what == "flush":
                    ly, grp = arg
                    silu(ly, grp * (FC // 2) + FC // 2 - 1)
                    hidden_high(ly, grp * (FC // 2) + FC // 2 - 1)
                elif what == "ctx":
                    for b in range(4):
                        act.wait_ge(pe_steps, pe_.at(f"ctx turned{b}"))
                        src = [bank_s[:, 0:2, :], bank_s[:, 2:4, :], bank_o[:, :].rearrange("p (j t) -> p j t", j=2),
                               bank_t[:, :, :].rearrange("p (j t) n -> p j (t n)", j=2)][b]
                        nc.scalar.activation(c_t[:, 2 * b:2 * b + 2, :], src, ACT.Copy
                                             ).then_inc(act_steps, act_.step(f"ctx{b}"))
                elif what in ("final norm", "mod norm"):
                    tag = "f" if what == "final norm" else f"{arg[0]}{arg[1]}"
                    n_s = 1 if tag in ("f", "11") else 2
                    before = {"f": None, "00": "x normed", "01": f"empty{END_JOBS[('eo', 3, 1)]}",
                              "10": f"empty{END_JOBS[('down0', 15, 0)]}", "11": f"empty{END_JOBS[('wo', 3, 0)]}"}[tag]
                    if before:
                        act.wait_ge(dve_steps, dve_.at(before))
                    act.wait_ge(act_steps, act_.last())
                    for half in range(2):
                        c = slice(4 * half, 4 * half + 4)
                        for s_ in range(n_s):
                            nc.scalar.activation(h2[:, c, s_ * SEQ:s_ * SEQ + SEQ], x_streams[s_][:, c, :], ACT.Square
                                                 ).then_inc(act_steps, act_.step(f"squares{tag} {half}"))
                    act.wait_ge(pe_steps, pe_.at(f"sumsq{tag}"))
                    nc.scalar.activation(m_root[:, 0:n_s * SEQ], bank_m[:, 0:n_s * SEQ], ACT.Sqrt, scale=1.0 / D,
                                         bias=eps[:, 0:1]).then_inc(act_steps, act_.step(f"root{tag}"))
                    if tag == "f":
                        continue
                    ly, w = arg
                    for c in range(KC):
                        act.wait_ge(dve_steps, dve_.at(f"h2{tag} {c}"))
                        for s_ in range(n_s):
                            t = slice(s_ * SEQ, s_ * SEQ + SEQ)
                            shift = mod[:, ly, mod_col(3 * w) + c, s_:s_ + 1]
                            nc.scalar.activation(h2_hi[:, c, t], h2[:, c, t], ACT.Identity, bias=shift
                                                 ).then_inc(act_steps, act_.step(f"h2 hi{tag} {c}"))
                elif what == "sgu weights":
                    act.wait_ge(pe_steps, pe_.at("sgu weights"))
                    nc.scalar.activation(w_s_t[:, :, :], bank_t[:, :, :], ACT.Copy
                                         ).then_inc(act_steps, act_.step("sgu weights"))
                elif what == "dft feature":
                    g_, = arg
                    act.wait_ge(pe_steps, pe_.at(f"dft feature{g_}"))
                    nc.scalar.activation(dft_f[g_ % 2][:, :, :], bank_s[:, :, :], ACT.Copy
                                         ).then_inc(act_steps, act_.step(f"dft feature{g_}"))
                elif what == "dft time":
                    g_, = arg
                    act.wait_ge(pe_steps, pe_.at(f"dft time{g_}"))
                    nc.scalar.activation(f_hi[:, g_, :], bank_t[:, :, :].rearrange("p a b -> p (a b)"), ACT.Copy
                                         ).then_inc(act_steps, act_.step(f"a hi{g_}"))
                elif what == "v norm":
                    act.wait_ge(dve_steps, dve_.at("v sum"))
                    nc.scalar.activation(v_inv[:, :], v_sum[:, :], ACT.Sqrt, scale=1.0 / P, bias=eps[:, 0:1]
                                         ).then_inc(act_steps, act_.step("v root"))
                elif what == "sgu":
                    g_, = arg
                    act.wait_ge(dve_steps, dve_.at(f"gated b{g_}"))
                    nc.scalar.activation(f_hi[:, 4 + g_, :], gated_b[:, g_ % 2, :], ACT.Copy
                                         ).then_inc(act_steps, act_.step(f"b hi{g_}"))
                elif what == "qk norm":
                    x, = arg
                    if x == "q":
                        act.dma_start(head_sum[:, :, :], ins["head_sum"]).then_inc(odd_loaded, 16)
                        act.dma_start(head_spread[0:16, :, :], ins["head_spread"]).then_inc(odd_loaded, 16)
                        act.dma_start(window[:, :], ins["window"]).then_inc(odd_loaded, 16)
                    nt = SEQ if x == "q" else 512
                    for half in range(2):
                        if half and x == "k":
                            act.wait_ge(pe_steps, pe_.at("sumsqk half"))
                        elif x == "k":
                            act.wait_ge(pe_steps, pe_.at("sumsqq"))
                        act.wait_ge(act_steps, act_.last())
                        if x == "q":
                            src = q_n[:, 4 * half:4 * half + 4, :]
                            dst = qk_sq[:, 2 * half:2 * half + 2, :].rearrange("p a (b t) -> p (a b) t", b=2)
                        else:
                            src, dst = k_n[:, 4 * half:4 * half + 4, :], qk_sq[:, :, :]
                        nc.scalar.activation(dst, src, ACT.Square).then_inc(act_steps,
                                                                            act_.step(f"squares{x}{half}",
                                                                                      *(["squaresq0"] if x == "q" else [])))
                    act.wait_ge(pe_steps, pe_.at(f"sumsq{x}"))
                    nc.scalar.activation(m_root[0:16, 0:nt], bank_m[0:16, 0:nt], ACT.Sqrt, scale=1.0 / HD,
                                         bias=eps[0:16, 0:1]).then_inc(act_steps, act_.step(f"root{x}"))
                    if x == "k":
                        act.wait_ge(pe_steps, pe_.at(f"job{END_JOBS[('nv', 3, 1)]}"))
                        for n in range(3):
                            load_bias(n)
                elif what == "near scores":
                    b, = arg
                    if b >= 2 and b % 2 == 0 and b // 2 + 2 < 8:
                        act.wait_ge(dve_steps, dve_.at(f"near masked{b - 1}"))
                        load_bias(b // 2 + 2)
                    act.wait_ge(dve_steps, dve_.at(f"near max{b}"))
                    for e in range(2):
                        nc.scalar.activation(near_p[b % 3][:, e, :], near_p[b % 3][:, e, :], ACT.Exp,
                                             bias=near_max[:, b % 2, e:e + 1], accum_out=near_sum[:, b % 2, e:e + 1]
                                             ).then_inc(act_steps, act_.step(f"near exp{b}"))
                elif what == "near turn":
                    b, = arg
                    for hf in range(2):
                        act.wait_ge(pe_steps, pe_.at(f"near turn{b} {hf}"))
                        src = bank_t[:, :, :] if hf == 0 else bank_m[:, :].rearrange("p (a b) -> p a b", a=4)
                        nc.scalar.activation(near_pt[:, b % 2, 2 * hf:2 * hf + 2, :, :].rearrange(
                            "p k e q -> p (k e) q"), src, ACT.Copy).then_inc(act_steps,
                                                                             act_.step(f"near turned{b} {hf}"))
                elif what == "near values":
                    b, = arg
                    qt, c = divmod(b, KC)
                    act.wait_ge(pe_steps, pe_.at(f"near values{b}"))
                    ob = bank_o if b % 2 == 0 else bank_g[0]
                    nc.scalar.activation(
                        f_hi[:, 0:4, :].rearrange("p a (b t) -> p (a b) t", b=2)[:, c, qt * P:qt * P + P],
                        ob[:, 0:P], ACT.Copy).then_inc(act_steps, act_.step(f"near hi{b}"))
                elif what == "finish":
                    for b in range(4):
                        t, c4 = divmod(b, 2)
                        act.wait_ge(pe_steps, pe_.at(f"finish{b}"))
                        src = bank_s[:, 2 * b:2 * b + 2, :].rearrange("p a b -> p (a b)") if b < 2 else (
                            bank_o[:, :] if b == 2 else bank_t[:, :, :].rearrange("p a b -> p (a b)"))
                        nc.scalar.activation(out_sb[:, t, 512 * c4:512 * c4 + 512], src, ACT.Copy
                                             ).then_inc(act_steps, act_.step("out", "out1"))

        @block.gpsimd
        def _(pool):
            enter("start")
            pool.sem_inc(pool_steps, pool_.total("layer") or 1)
            nc.gpsimd.memset(eps[:, :], EPS).then_inc(pool_steps, pool_.step("eps"))
            nc.gpsimd.memset(ones[:, :], 1.0).then_inc(pool_steps, pool_.step("ones"))
            nc.gpsimd.memset(logf[:, :, :], 0.0).then_inc(pool_steps, pool_.step("logf"))
            with pool.Fori(0, DEPTH) as layer:
                enter("layer", layer)
                before = "rope kb"
                for what, *arg in ORDER:
                    if what != "rope":
                        continue
                    x, = arg
                    src = ki[:, :].rearrange("p (o t) -> p o t", o=1) if x == "ki" else (
                        qk[1][:, 0:4, :] if x == "qi" else
                        qk[SETS[x[1]]][:, 0:4, :] if x[0] == "q" else qk[SETS[x[1]]][:, 4:8, :])
                    n = 1 if x == "ki" else 4
                    if x == "ki":
                        pool.wait_ge(act_steps, act_.at("ki"))
                    else:
                        pool.wait_ge(act_steps, act_.at(f"empty{JOBS[(x, 1, 0)]}"))
                    pool.wait_ge(dve_steps, dve_.at(before, before=x == "ki"))
                    nc.gpsimd.tensor_tensor(scaled[:, 0:n, :], src, rope[:, 0:1, :].to_broadcast([P, n, SEQ]), ALU.mult
                                            ).then_inc(pool_steps, pool_.step("cos " + x))
                    before = "rope " + x

        @block.vector
        def _(dve):
            enter("start")
            dve.sem_inc(dve_steps, dve_.total("layer") or 1)
            own = lambda: dve.wait_ge(dve_steps, dve_.last())
            plain = lambda: dve.sem_inc(dve_passed, 1)
            dve.wait_ge(act_steps, act_.at("s tanh"))
            cc = vec[:, ROWS["c"]:ROWS["c"] + 16].rearrange("p (s c) -> p s c", s=2)
            nc.vector.scalar_tensor_tensor(s_f[:, :, :], s_f[:, :, :], 1.0, cc, ALU.add, ALU.mult
                                           ).then_inc(dve_steps, dve_.step("s"))
            own()
            dve.wait_ge(act_steps, act_.at("s hi"))
            for s in range(2):
                nc.vector.scalar_tensor_tensor(s_parts[:, :, 2 + s], s_f[:, s, :], 0.5,
                                               s_parts[:, :, s].bitcast(F32), ALU.mult, ALU.subtract
                                               ).then_inc(dve_steps, dve_.step("s split"))
            dve.wait_ge(pool_steps, pool_.at("logf"))
            dve.wait_ge(consts_loaded, 16 * CONSTS)

            with dve.Fori(0, DEPTH) as layer:
                enter("layer", layer)

                def low(u):
                    dve.wait_ge(act_steps, act_.at(f"hi{u}"))
                    nc.vector.tensor_tensor(w_lo[:, u % SLOTS, :], raw[:, u % SLOTS, :],
                                            w_hi[:, u % SLOTS, :].bitcast(F32), ALU.subtract
                                            ).then_inc(dve_steps, dve_.step(f"lo{u}"))

                own()
                nc.vector.tensor_copy(gain[:, :], vec[:, bass.ds(layer * KC + ROWS["norm_gain"], KC)]
                                      ).then_inc(dve_steps, dve_.step("gain"))
                nc.vector.tensor_copy(ada_bias[:, :], vec[:, bass.ds(layer * 48 + ROWS["ada_b"], 48)]
                                      ).then_inc(dve_steps, dve_.step("ada bias"))
                nc.vector.tensor_copy(fbias_now[:, :], fbias[:, bass.ds(layer, 1), :]
                                      ).then_inc(dve_steps, dve_.step("fbias"))
                for u in range(AHEAD):
                    low(u)
                def normalize(k):
                    nk = P * (BATCHES[k][1] + 1)
                    dve.wait_ge(act_steps, act_.at(f"exp{k}"))
                    own()
                    nc.vector.reciprocal(rowinv[:, :], rowsum[:, k % 2, :]).then_inc(dve_steps, dve_.step("rowinv"))
                    own()
                    pb = probs[k % 2][:, :, 0:nk]
                    nc.vector.tensor_tensor(pb, pb, rowinv[:, :].rearrange("p (s o) -> p s o", o=1).to_broadcast(
                        [P, 4, nk]), ALU.mult).then_inc(dve_steps, dve_.step(f"probs{k}"))

                u = 0
                pending = None
                for what, *arg in ORDER:
                    if what == "unit":
                        kind, i = arg
                        if pending is not None:
                            normalize(pending)
                            pending = None
                        if u + AHEAD < len(UNITS):
                            low(u + AHEAD)
                        for j in range(2 if kind == "branch" else 1):
                            k = JOBS[(kind, i, j)]
                            if evacuator(kind) != "dve":
                                continue
                            gb = bank_g[k % BANKS][:, :].rearrange("p (m t) -> p m t", m=2)
                            dve.wait_ge(pe_steps, pe_.at(f"job{k}"))
                            if kind == "branch":
                                n, half = divmod(i, 2)
                                gt = gates[:, j, :, :]
                                dve.wait_ge(act_steps, act_.at(f"empty{JOBS[('gate', 2 * i + j, 0)]}"))
                                c = 4 * half + 2 * j
                                own()
                                dst = branch_y[:, :, :] if n else h[:, c:c + 2, :]
                                nc.vector.scalar_tensor_tensor(dst, gt, 1.0, gb, ALU.add, ALU.mult).then_inc(
                                    dve_steps, dve_.step("y", *([] if n else [f"empty{k}"])))
                                if n:
                                    own()
                                    nc.vector.tensor_tensor(h[:, c:c + 2, :], h[:, c:c + 2, :], branch_y[:, :, :],
                                                            ALU.add).then_inc(dve_steps, dve_.step(f"empty{k}"))
                            elif kind == "out":
                                own()
                                nc.vector.tensor_tensor(x_t[:, 2 * i:2 * i + 2, :], gb, x_t[:, 2 * i:2 * i + 2, :],
                                                        ALU.add).then_inc(dve_steps, dve_.step(f"empty{k}"))
                            else:
                                gg = g[SETS[kind[1]]][:, 2 * i:2 * i + 2, :]
                                dve.wait_ge(act_steps, act_.at(f"tanh{k}"))
                                nc.vector.scalar_tensor_tensor(gg, gg, 1.0, gb, ALU.add, ALU.mult).then_inc(
                                    dve_steps, dve_.step(f"empty{k}"))
                        u += 1
                    elif what == "norm":
                        dve.wait_ge(act_steps, act_.at("root"))
                        nc.vector.reciprocal(root[:, 0:SEQ], root[:, 0:SEQ]).then_inc(dve_steps, dve_.step("rstd"))
                        own()
                        for c in range(KC):
                            nc.vector.scalar_tensor_tensor(h[:, c, :], x_t[:, c, :], gain[:, c:c + 1], root[:, 0:SEQ],
                                                           ALU.mult, ALU.mult).then_inc(
                                dve_steps, dve_.step(*(["h0"] if c < 4 else ["h1", "h"])))
                        own()
                        for half in range(2):
                            c = slice(4 * half, 4 * half + 4)
                            dve.wait_ge(act_steps, act_.at(f"h hi{half}"))
                            nc.vector.tensor_tensor(h_lo[:, c, :], h[:, c, :], h_hi[:, c, :].bitcast(F32), ALU.subtract
                                                    ).then_inc(dve_steps, dve_.step(f"h lo{half}"))
                    elif what == "small":
                        dve.wait_ge(pe_steps, pe_.at("small"))
                        wf = bank_o[:, 0:32].rearrange("p (t n) -> p t n", t=2)
                        nc.vector.tensor_scalar(w_f[:, :, 0:8], wf[:, :, 0:8], 8 ** -0.5 * 64 ** -0.5, None, ALU.mult
                                                ).then_inc(dve_steps, dve_.step("w idx"))
                        nc.vector.tensor_tensor(w_f[:, :, 8:16], wf[:, :, 8:16],
                                                fbias_now[:, :].rearrange("p (o n) -> p o n", o=1).to_broadcast(
                                                    [P, 2, 8]), ALU.add).then_inc(dve_steps, dve_.step("f"))
                        own()
                        nc.vector.tensor_scalar(f_min[:, :, :], w_f[:, :, 8:16], -1.0, None, ALU.mult
                                                ).then_inc(dve_steps, dve_.step("f neg"))
                        own()
                        nc.vector.tensor_tensor(f_abs[:, :, :], f_min[:, :, :], w_f[:, :, 8:16], ALU.max
                                                ).then_inc(dve_steps, dve_.step("f abs"))
                        own()
                        nc.vector.tensor_scalar(f_min[:, :, :], w_f[:, :, 8:16], 0.0, None, ALU.min
                                                ).then_inc(dve_steps, dve_.step("f min"))
                        dve.wait_ge(act_steps, act_.at("f log"))
                        own()
                        for c in (0, 64):
                            nc.vector.tensor_tensor(logf[:, :, c:c + 8], f_min[:, :, :], f_log[:, :, :], ALU.subtract
                                                    ).then_inc(dve_steps, dve_.step("logf"))
                    elif what == "rope":
                        x, = arg
                        buf = ki[:, :].rearrange("p (o t) -> p o t", o=1) if x == "ki" else (
                            qk[1][:, 0:4, :] if x == "qi" else
                            qk[SETS[x[1]]][:, 0:4, :] if x[0] == "q" else qk[SETS[x[1]]][:, 4:8, :])
                        n = 1 if x == "ki" else 4
                        if x == "ki":
                            dve.wait_ge(act_steps, act_.at("ki"))
                        else:
                            dve.wait_ge(act_steps, act_.at(f"empty{JOBS[(x, 1, 0)]}"))
                        own()
                        plain()
                        nc.vector.stream_shuffle(turned[:, 0:n, :], buf, [(m + 8) % 16 if m < 16 else m for m in range(32)]
                                                 ).then_inc(dve_steps, dve_.step("swap"))
                        own()
                        nc.vector.tensor_tensor(turned[:, 0:n, :], turned[:, 0:n, :],
                                                rope[:, 1:2, :].to_broadcast([P, n, SEQ]), ALU.mult
                                                ).then_inc(dve_steps, dve_.step("sin"))
                        dve.wait_ge(pool_steps, pool_.at("cos " + x))
                        own()
                        nc.vector.tensor_tensor(buf, turned[:, 0:n, :], scaled[:, 0:n, :], ALU.add
                                                ).then_inc(dve_steps, dve_.step("rope " + x))
                    elif what == "scores":
                        k, = arg
                        x, qt, hg = BATCHES[k]
                        nk = P * (qt + 1)
                        pb = probs[k % 2]
                        if x == "i":
                            dve.wait_ge(act_steps, act_.at(f"relu{k}"))
                            for s in range(4):
                                hh = 4 * hg + 2 * (s % 2) + s // 2
                                own()
                                if hg == 0 and s == 0:
                                    nc.vector.tensor_scalar(isc[:, 0:nk], pb[:, s, 0:nk], w_f[:, qt, hh:hh + 1], None,
                                                            ALU.mult).then_inc(dve_steps, dve_.step(f"index{k}"))
                                else:
                                    nc.vector.scalar_tensor_tensor(isc[:, 0:nk], pb[:, s, 0:nk], w_f[:, qt, hh:hh + 1],
                                                                   isc[:, 0:nk], ALU.mult, ALU.add).then_inc(
                                        dve_steps, dve_.step(f"index{k}"))
                            if hg == 1:
                                own()
                                nc.vector.scalar_tensor_tensor(work[:, 0:nk], causal[:, qt, 0:nk], FILL / NEG,
                                                               isc[:, 0:nk], ALU.mult, ALU.add).then_inc(
                                    dve_steps, dve_.step("ranked"))
                        else:
                            dve.wait_ge(pe_steps, pe_.at(f"scores{k}"))
                            own()
                            mask = (picked if x == "b" else causal)[:, qt:qt + 1, 0:nk].to_broadcast([P, 4, nk])
                            nc.vector.scalar_tensor_tensor(pb[:, :, 0:nk], bank_s[:, :, 0:nk], SCALE, mask,
                                                           ALU.mult, ALU.add).then_inc(dve_steps,
                                                                                       dve_.step(f"masked{k}"))
                            own()
                            nm = negmax[:, k % 2, :]
                            if x != "c":
                                nc.vector.tensor_reduce(nm, pb[:, :, 0:nk], AX.X, ALU.max, negate=True).then_inc(
                                    dve_steps, dve_.step(f"negmax{k}"))
                            else:
                                nc.vector.tensor_reduce(nm, pb[:, :, 0:nk], AX.X, ALU.max, negate=True).then_inc(
                                    dve_steps, dve_.step("max"))
                                dve.wait_ge(act_steps, act_.at("csum"))
                                cq = csum_q[:, qt, 4 * hg:4 * hg + 4].rearrange("p (j e) -> p e j", j=2)
                                n2 = nm.rearrange("p (e j) -> p e j", e=2)
                                for op, name in ((ALU.subtract, "max"), (ALU.add, f"negmax{k}")):
                                    own()
                                    nc.vector.tensor_tensor(n2, n2, cq, op).then_inc(dve_steps, dve_.step(name))
                            pending = k
                    elif what == "topk":
                        qt, r = arg
                        nk = P * (qt + 1)
                        for _ in range(2):
                            own()
                            plain()
                            nc.vector.max(top8[:, :], work[:, 0:nk]).then_inc(dve_steps, dve_.step("top8"))
                            own()
                            plain()
                            nc.vector.match_replace(work[:, 0:nk], top8[:, :], work[:, 0:nk], TAKEN).then_inc(
                                dve_steps, dve_.step("taken"))
                        if r == 3:
                            own()
                            nc.vector.tensor_scalar(work[:, 0:nk], work[:, 0:nk], TAKEN, 1.0, ALU.is_equal,
                                                    ALU.subtract).then_inc(dve_steps, dve_.step("sel"))
                            own()
                            nc.vector.scalar_tensor_tensor(picked[:, qt, 0:nk], work[:, 0:nk], -NEG,
                                                           causal[:, qt, 0:nk], ALU.mult, ALU.add).then_inc(
                                dve_steps, dve_.step("picked"))
                    elif what == "values":
                        k, = arg
                        x, qt, hg = BATCHES[k]
                        t = slice(qt * P, qt * P + P)
                        dve.wait_ge(pe_steps, pe_.at(f"values{k}"))
                        own()
                        nc.vector.scalar_tensor_tensor(
                            o_gated[:, k % 2, :, :], bank_o[:, 0:2 * P].rearrange("p (j t) -> p j t", j=2), 0.5,
                            g[SETS[x]][:, 2 * hg:2 * hg + 2, t], ALU.mult, ALU.mult
                        ).then_inc(dve_steps, dve_.step(f"gated{k}"))
                        own()
                        dve.wait_ge(act_steps, act_.at(f"o hi{k}"))
                        c = 4 * "abc".index(x) + 2 * hg
                        nc.vector.tensor_tensor(o_lo[:, c:c + 2, t], o_gated[:, k % 2, :, :],
                                                o_hi[:, c:c + 2, t].bitcast(F32), ALU.subtract
                                                ).then_inc(dve_steps, dve_.step(f"o lo{k}"))
                    elif what == "merged":
                        for half in range(2):
                            c = slice(4 * half, 4 * half + 4)
                            dve.wait_ge(act_steps, act_.at(f"merged hi{half}"))
                            own()
                            nc.vector.scalar_tensor_tensor(h_lo[:, c, :], h[:, c, :], 0.5, h_hi[:, c, :].bitcast(F32),
                                                           ALU.mult, ALU.subtract).then_inc(
                                dve_steps, dve_.step(f"merged lo{half}"))
                dve.wait_ge(pe_steps, pe_.at("ada turn23"))
                own()
                nc.vector.tensor_tensor(
                    mod_now[:, :, :], bank_m[:, ADA_COL:ADA_COL + 96].rearrange("p (m s) -> p m s", s=2),
                    ada_bias[:, :].rearrange("p (m o) -> p m o", o=1).to_broadcast([P, 48, 2]), ALU.add
                ).then_inc(dve_steps, dve_.step("mod now"))
                own()
                nc.vector.tensor_copy(mod[:, bass.ds(layer, 1), :, :], mod_now[:, :, :]
                                      ).then_inc(dve_steps, dve_.step("mod"))
            enter("end")

            def low(u):
                n = size(END_UNITS[u][0])
                dve.wait_ge(act_steps, act_.at(f"hi{u}"))
                nc.vector.tensor_tensor(w_lo[:, u % SLOTS, 0:n], raw[:, u % SLOTS, 0:n],
                                        w_hi[:, u % SLOTS, 0:n].bitcast(F32), ALU.subtract
                                        ).then_inc(dve_steps, dve_.step(f"lo{u}"))

            def multiply(ly, i):
                n = SEQ * streams(f"up{ly}")
                job = END_JOBS[(f"up{ly}", i, 1 if ly == 0 else 0)]
                vb = bank_g[job % BANKS][:, 0:512] if ly == 0 else bank_g[job % BANKS][:, SEQ:2 * SEQ]
                dve.wait_ge(act_steps, act_.at(f"silu{ly} {i}"))
                dve.wait_ge(pe_steps, pe_.at(f"job{job}"))
                own()
                nc.vector.tensor_tensor(hidden[:, i % 2, 0:n], conv[:, i % 2, 0:n], vb, ALU.mult).then_inc(
                    dve_steps, dve_.step(f"hidden{ly} {i}", f"empty{job}"))

            def hidden_low(ly, i):
                n = SEQ * streams(f"up{ly}")
                dve.wait_ge(act_steps, act_.at(f"f hi{ly} {i}"))
                nc.vector.tensor_tensor(f_lo[:, i % (FC // 2), 0:n], hidden[:, i % 2, 0:n],
                                        f_hi[:, i % (FC // 2), 0:n].bitcast(F32), ALU.subtract
                                        ).then_inc(dve_steps, dve_.step(f"f lo{ly} {i}"))

            for u in range(AHEAD):
                low(u)
            u = 0
            for what, *arg in END:
                if what == "unit":
                    kind, i = arg
                    up = kind[:2] == "up"
                    n_s = streams(kind)
                    if up:
                        ly = int(kind[2])
                        first = i % (FC // 2) == 0
                        if not first:
                            multiply(ly, i - 1)
                    if u + AHEAD < len(END_UNITS):
                        low(u + AHEAD)
                    if up:
                        k = END_JOBS[(kind, i, 0)]
                        cv = conv[:, i % 2, 0:n_s * SEQ].rearrange("p (s t) -> p s t", s=n_s)
                        gb = bank_g[k % BANKS][:, 0:n_s * SEQ].rearrange("p (s t) -> p s t", s=n_s)
                        dve.wait_ge(act_steps, act_.at(f"conv{ly} {i}"))
                        for tap, to, of in ((0, slice(1, SEQ), slice(0, SEQ - 1)), (2, slice(0, SEQ - 1), slice(1, SEQ))):
                            own()
                            nc.vector.scalar_tensor_tensor(cv[:, :, to], gb[:, :, of], conv_col(ly, tap, i),
                                                           cv[:, :, to], ALU.mult, ALU.add).then_inc(
                                dve_steps, dve_.step(f"conv{ly} {i}", *([f"empty{k}"] if ly == 0 else [])))
                        if not first:
                            hidden_low(ly, i - 1)
                    for j in range(end_jobs(kind)):
                        k = END_JOBS[(kind, i, j)]
                        if end_evacuator(kind, j) != "dve" or up:
                            continue
                        dve.wait_ge(pe_steps, pe_.at(f"job{k}"))
                        own()
                        gb = bank_g[k % BANKS]
                        ly = 0 if kind in ("eo", "down0") else 1
                        part = mod_col(2 if kind in ("eo", "wo") else 5)
                        if kind in ("eo", "down0"):
                            m = 2 * i + j if kind == "eo" else i % KC
                            todo = [(m, s_, gb[:, s_ * SEQ:s_ * SEQ + SEQ]) for s_ in range(2)]
                        elif kind == "wo":
                            todo = [(2 * i + m, 0, gb[:, m * SEQ:m * SEQ + SEQ]) for m in range(2)]
                        else:
                            todo = [(i % KC, 0, gb[:, 0:SEQ])]
                        for m, s_, src in todo:
                            xs = x_streams[s_][:, m, :]
                            nc.vector.scalar_tensor_tensor(xs, src, mod[:, ly, part + m, s_:s_ + 1], xs,
                                                           ALU.mult, ALU.add).then_inc(dve_steps,
                                                                                       dve_.step(f"empty{k}"))
                    u += 1
                elif what == "flush":
                    ly, grp = arg
                    multiply(ly, grp * (FC // 2) + FC // 2 - 1)
                    hidden_low(ly, grp * (FC // 2) + FC // 2 - 1)
                elif what in ("final norm", "mod norm"):
                    tag = "f" if what == "final norm" else f"{arg[0]}{arg[1]}"
                    n_s = 1 if tag in ("f", "11") else 2
                    if tag != "f":
                        ly, w = arg
                        col = ROWS["norm1" if w == 0 else "norm2"] + ly * KC
                        own()
                        nc.vector.scalar_tensor_tensor(
                            m_gain[:, :, :], mod[:, ly, mod_col(3 * w + 1):mod_col(3 * w + 1) + KC, :], 1.0,
                            vec[:, col:col + KC].rearrange("p (c o) -> p c o", o=1).to_broadcast([P, KC, 2]),
                            ALU.add, ALU.mult).then_inc(dve_steps, dve_.step("m gain"))
                    dve.wait_ge(act_steps, act_.at(f"root{tag}"))
                    nc.vector.reciprocal(m_rstd[:, 0:n_s * SEQ], m_root[:, 0:n_s * SEQ]).then_inc(
                        dve_steps, dve_.step("m rstd"))
                    own()
                    if tag == "f":
                        for c in range(KC):
                            n = ROWS["final_gain"] + c
                            nc.vector.scalar_tensor_tensor(x_t[:, c, :], x_t[:, c, :], vec[:, n:n + 1],
                                                           m_rstd[:, 0:SEQ], ALU.mult, ALU.mult).then_inc(
                                dve_steps, dve_.step("x normed"))
                        continue

                    def low_part(c):
                        dve.wait_ge(act_steps, act_.at(f"h2 hi{tag} {c}"))
                        for s_ in range(n_s):
                            t = slice(s_ * SEQ, s_ * SEQ + SEQ)
                            nc.vector.scalar_tensor_tensor(
                                h2_lo[:, c, t], h2[:, c, t], mod[:, ly, mod_col(3 * w) + c, s_:s_ + 1],
                                h2_hi[:, c, t].bitcast(F32), ALU.add, ALU.subtract
                            ).then_inc(dve_steps, dve_.step(f"h2 lo{tag} {c}"))

                    for c in range(KC):
                        for s_ in range(n_s):
                            t = slice(s_ * SEQ, s_ * SEQ + SEQ)
                            nc.vector.scalar_tensor_tensor(h2[:, c, t], x_streams[s_][:, c, :], m_gain[:, c, s_:s_ + 1],
                                                           m_rstd[:, t], ALU.mult, ALU.mult).then_inc(
                                dve_steps, dve_.step(f"h2{tag} {c}"))
                        if c:
                            low_part(c - 1)
                    low_part(KC - 1)
                elif what == "dft time":
                    g_, = arg
                    dve.wait_ge(act_steps, act_.at(f"a hi{g_}"))
                    nc.vector.tensor_tensor(f_lo[:, g_, :], bank_t[:, :, :].rearrange("p a b -> p (a b)"),
                                            f_hi[:, g_, :].bitcast(F32), ALU.subtract
                                            ).then_inc(dve_steps, dve_.step(f"a lo{g_}"))
                elif what == "v norm":
                    dve.wait_ge(act_steps, act_.at(f"empty{END_JOBS[('vs', 1, 1)]}"))
                    dve.wait_ge(pe_steps, pe_.at("dft feature3"))
                    nc.vector.tensor_tensor(v_sq[:, :, :], v_s[:, :, :], v_s[:, :, :], ALU.mult).then_inc(
                        dve_steps, dve_.step("v sq"))
                    own()
                    nc.vector.tensor_reduce(v_sum[:, :], v_sq[:, :, :].rearrange("p t (g c) -> p (t g) c", g=4), AX.X,
                                            ALU.add).then_inc(dve_steps, dve_.step("v sum"))
                    dve.wait_ge(act_steps, act_.at("v root"))
                    nc.vector.reciprocal(v_inv[:, :], v_inv[:, :]).then_inc(dve_steps, dve_.step("v inv"))
                    own()
                    vg = v_s[:, :, :].rearrange("p t (g c) -> p (t g) c", g=4)
                    nc.vector.tensor_tensor(vg, vg, v_inv[:, :].rearrange("p (a o) -> p a o", o=1).to_broadcast(
                        [P, 16, P]), ALU.mult).then_inc(dve_steps, dve_.step("v norm"))
                elif what == "sgu":
                    g_, = arg
                    dve.wait_ge(pe_steps, pe_.at(f"sgu{g_}"))
                    own()
                    nc.vector.tensor_tensor(gated_b[:, g_ % 2, :], bank_o[:, :], u_t[:, g_, :], ALU.mult).then_inc(
                        dve_steps, dve_.step(f"gated b{g_}"))
                    dve.wait_ge(act_steps, act_.at(f"b hi{g_}"))
                    own()
                    nc.vector.tensor_tensor(f_lo[:, 4 + g_, :], gated_b[:, g_ % 2, :], f_hi[:, 4 + g_, :].bitcast(F32),
                                            ALU.subtract).then_inc(dve_steps, dve_.step(f"b lo{g_}"))
                elif what == "qk norm":
                    x, = arg
                    nt = SEQ if x == "q" else 512
                    dve.wait_ge(act_steps, act_.at(f"root{x}"))
                    own()
                    nc.vector.reciprocal(m_rstd[0:16, 0:nt], m_root[0:16, 0:nt]).then_inc(dve_steps,
                                                                                         dve_.step(f"rstd{x}"))
                    own()
                    for c in range(KC):
                        dst = (q_n if x == "q" else k_n)[:, c, :]
                        n = ROWS[x + "_g"]
                        src = (bank_t[:, :, :].rearrange("p a b -> p (a b)") if c % 2 == 0 else bank_o)[:, 0:nt]
                        dve.wait_ge(pe_steps, pe_.at(f"spread{x}{c}"))
                        nc.vector.scalar_tensor_tensor(dst, dst, vec[:, n:n + 1], src, ALU.mult, ALU.mult).then_inc(
                            dve_steps, dve_.step(f"normed{x}{c}"))
                elif what == "near scores":
                    b, = arg
                    qt, c = divmod(b, KC)
                    pb, sbk = near_p[b % 3], near_banks(b)
                    dve.wait_ge(bias_loaded[b // 2 % 3], 32 * (b // 6 + 1))
                    dve.wait_ge(pe_steps, pe_.at(f"near scores{b}"))
                    bt = bias[b // 2 % 3][:, 2 * (c % 2):2 * (c % 2) + 2, :]
                    nc.vector.scalar_tensor_tensor(pb[:, :, 0:SEQ], sbk[:, :, 0:SEQ], SCALE, backwards(bt),
                                                   ALU.mult, ALU.add).then_inc(dve_steps, dve_.step("near"))
                    nc.vector.tensor_scalar(pb[:, :, SEQ:512], sbk[:, :, SEQ:512], SCALE, None, ALU.mult).then_inc(
                        dve_steps, dve_.step(f"near masked{b}"))
                    own()
                    wn = window[:, :].rearrange("p (o k) -> p o k", o=1)
                    nc.vector.tensor_tensor(pb[:, :, 0:SEQ], pb[:, :, 0:SEQ],
                                            backwards(wn).to_broadcast([P, 2, SEQ]), ALU.add).then_inc(
                        dve_steps, dve_.step("near window"))
                    own()
                    nc.vector.tensor_reduce(near_max[:, b % 2, :], pb[:, :, :], AX.X, ALU.max, negate=True).then_inc(
                        dve_steps, dve_.step(f"near max{b}"))
                elif what == "near turn":
                    b, = arg
                    dve.wait_ge(act_steps, act_.at(f"near exp{b}"))
                    own()
                    nc.vector.reciprocal(near_inv[:, :], near_sum[:, b % 2, :]).then_inc(dve_steps,
                                                                                        dve_.step("near inv"))
                    own()
                    nc.vector.tensor_tensor(near_p[b % 3][:, :, :], near_p[b % 3][:, :, :],
                                            near_inv[:, :].rearrange("p (e o) -> p e o", o=1).to_broadcast([P, 2, 512]),
                                            ALU.mult).then_inc(dve_steps, dve_.step(f"near probs{b}"))
                elif what == "near values":
                    b, = arg
                    qt, c = divmod(b, KC)
                    ob = bank_o if b % 2 == 0 else bank_g[0]
                    v8 = lambda t: t[:, 0:4, :].rearrange("p a (b t) -> p (a b) t", b=2)[:, c, qt * P:qt * P + P]
                    dve.wait_ge(act_steps, act_.at(f"near hi{b}"))
                    nc.vector.tensor_tensor(v8(f_lo), ob[:, 0:P], v8(f_hi).bitcast(F32), ALU.subtract).then_inc(
                        dve_steps, dve_.step(f"near lo{b}"))
    return {"pe": pe_.learned(), "act": act_.learned(), "dve": dve_.learned(), "pool": pool_.learned()}


def vectors(inputs):
    parts = [inputs["norm_gain"], inputs["final_gain"], inputs["norm1_g_2"], inputs["norm2_g_2"],
             inputs["ffn_conv_w_2"], inputs["ffn_conv_b_2"], inputs["c_2"], inputs["c_ctx_2"],
             inputs["odd_q_g_2"], inputs["odd_q_g_2"], inputs["odd_k_g_2"], inputs["odd_k_g_2"],
             np.zeros(6 * P, np.float32), inputs["ada_b_2"]]
    flat = np.concatenate([np.asarray(a).reshape(-1) for a in parts])
    return np.concatenate([flat, np.zeros(VROWS * P - flat.size, np.float32)]).reshape(VROWS, P)


def kernel(**inputs):
    import concourse.bacc as bacc
    from concourse.bass_utils import run_bass_kernel_spmd as run

    arrays = {name: np.ascontiguousarray(inputs[key]) for name, key in (
        ("x", "x"), ("w_in", "w_in"), ("w_branch", "w_branch"), ("w_out", "w_out"), ("forget_bias", "forget_bias"),
        ("ada_w", "ada_w_2"), ("ctx", "ctx_2"), ("w_up", "ffn_w_up_2"), ("w_down", "ffn_w_down_2"))}
    for name, key in (("even_in", "even_w_in_2"), ("even_out", "even_w_out_2"), ("w_s", "even_w_s_2"),
                      ("b_s", "even_b_s_2"), ("qkv", "odd_w_qkv_2"), ("odd_out", "odd_w_o_2")):
        arrays[name] = np.ascontiguousarray(inputs[key][0])
    rpb = np.asarray(inputs["odd_rpb_2"])[0, :, ::-1, ::-1]
    rows = np.stack([rpb[:, 4 + r:8 + r, :] for r in range(4)])
    arrays["rpb"] = np.concatenate([np.zeros(48, np.float32), rows.reshape(-1), np.zeros(64, np.float32)])
    arrays["vectors"] = vectors(inputs)
    arrays.update(constants())

    def build(known):
        nc = bacc.Bacc("TRN2", target_bir_lowering=False, num_devices=1)
        ins = {n: nc.dram_tensor(n, a.shape, mybir.dt.from_np(a.dtype), kind="ExternalInput").ap()
               for n, a in arrays.items()}
        out = nc.dram_tensor("out", (1, SEQ, D), F32, kind="ExternalOutput").ap()
        return nc, program(nc, ins, out, known)

    nc, known = build({})
    nc, again = build(known)
    assert known == again
    r = run(nc, [arrays], core_ids=[0])
    return r.results[0]["out"]
```

```python
from contextlib import ExitStack

import numpy as np

import concourse.bass as bass
from concourse import mybir

F32 = mybir.dt.float32
F32R = mybir.dt.float32r
ALU = mybir.AluOpType
ACT = mybir.ActivationFunctionType
AX = mybir.AxisListType

P = 128
D = 1024
KC = D // P
SEQ = 256
CTX = 256
DEPTH = 2
HD = 64
WIDTH = 512
Q_IDX0 = 12 * WIDTH
K_IDX0 = Q_IDX0 + 512
W_IDX0 = K_IDX0 + HD
MERGE0 = W_IDX0 + 16
D_FF = 2816
FC = D_FF // P
EPS = 1e-6
SCALE = HD ** -0.5
NEG = -1.0e30
FILL = -3.0e38
TAKEN = -3.4e38
TOPK = 64
DMA_SCRATCH = 16 * 1024
SBUF_BYTES = 224 * 1024
SLOTS = 3
UNIT = 2048
BANKS = 3
ADA_COL = 256
SUM_COL = 352
AHEAD = 2

ROWS = {}
_n = 0
for _name, _count in (("norm_gain", 16), ("final_gain", 8), ("norm1", 16), ("norm2", 16), ("conv_w", 132),
                      ("conv_b", 44), ("c", 8), ("c_ctx", 8), ("q_g", 1), ("k_g", 1), ("pad", 6), ("ada_b", 96)):
    ROWS[_name] = _n
    _n += _count
VROWS = 384
assert _n <= VROWS


def constants():
    t = {}
    i = np.arange(P)
    t["ident"] = np.eye(P, dtype=np.float32)
    inv = np.power(np.float32(500000.0), -np.arange(0, 16, 2, dtype=np.float32) / np.float32(16))
    ang = np.arange(SEQ, dtype=np.float32)[:, None] * inv[None, :].astype(np.float32)
    cos, sin = np.cos(ang.astype(np.float32)), np.sin(ang.astype(np.float32))
    rc, rs = np.ones((P, SEQ), np.float32), np.zeros((P, SEQ), np.float32)
    for b in (0, 64):
        rc[b:b + 8], rc[b + 8:b + 16] = cos.T, cos.T
        rs[b:b + 8], rs[b + 8:b + 16] = -sin.T, sin.T
    t["rope"] = np.stack([rc, rs], 1)
    tri = (np.arange(2)[None, :, None] * P + i[:, None, None]) >= np.arange(SEQ)[None, None, :]
    t["causal"] = np.where(tri, 0.0, NEG).astype(np.float32)
    upto = (np.arange(2)[None, :, None] * P + i[:, None, None]) <= np.arange(SEQ)[None, None, :]
    t["upto"] = upto.astype(np.float32)
    pick = np.zeros((P, 8), np.float32)
    for h in range(8):
        pick[h, h] = pick[64 + h, h] = -1.0 / SCALE
    t["pick"] = pick
    t["add_parts"] = np.tile(np.eye(2, dtype=np.float32), (2, 1))
    c = np.outer(i, i).astype(np.float64) * (2 * np.pi / P)
    t["dft_c"] = np.concatenate([np.cos(c), np.sin(c)], 1).astype(np.float32)
    a = np.outer(np.arange(SEQ), np.arange(SEQ)).astype(np.float64) * (2 * np.pi / SEQ)
    s = 1.0 / np.sqrt(SEQ * P)
    ts = np.stack([np.cos(a) * s, -np.sin(a) * s], 1).astype(np.float32)
    t["dft_t"] = np.ascontiguousarray(ts.reshape(2, P, 2, SEQ).transpose(1, 0, 2, 3))
    heads = (np.arange(16)[None, None, :] == 2 * np.arange(KC)[None, :, None] + (i // 64)[:, None, None])
    t["head_sum"] = heads.astype(np.float32)
    t["head_spread"] = np.ascontiguousarray(heads.transpose(2, 1, 0)).astype(np.float32)
    col = np.arange(64)
    start = np.clip(col - 8, 0, 48)
    win = (col[None, :] >= start[:, None]) & (col[None, :] < start[:, None] + 16)
    win = np.where(win, 0.0, NEG).astype(np.float32)
    t["window"] = np.ascontiguousarray(np.tile(win, (2, 4))[:, ::-1])
    return t


class Steps:

    def __init__(self, known=None):
        self.known = known or {}
        self.names = {}
        self.count = {"start": 0, "layer": 0, "end": 0}
        self.part = "start"
        self.layer = 0

    def step(self, *names):
        self.count[self.part] += 1
        for name in names:
            self.names[(self.part, name)] = self.count[self.part]
        return 1

    def total(self, part):
        return self.known.get(part, 0)

    def value(self, part, n):
        per = self.total("layer")
        if part == "start":
            return per + n
        if part == "layer":
            if self.part == "layer":
                return self.layer * per + (per + self.total("start") + n)
            return per + self.total("start") + (DEPTH - 1) * per + n
        return per + self.total("start") + DEPTH * per + n

    def latest(self, *names):
        if self.part == "end":
            return max(self.at(x.lstrip("<"), before=x[0] == "<") for x in names)
        n = [self.known.get(("layer", x.lstrip("<")), 0) - (self.total("layer") if x[0] == "<" else 0) for x in names]
        return self.layer * self.total("layer") + (self.total("layer") + self.total("start") + max(n))

    def at(self, name, before=False):
        if before and self.part == "layer":
            return self.layer * self.total("layer") + (self.total("start") + self.known.get(("layer", name), 0))
        for part in (self.part, "layer", "start"):
            if (part, name) in self.known and not (before and part == "end"):
                return self.value(part, self.known[(part, name)])
        assert not self.known, name
        return 1

    def last(self):
        return self.value(self.part, self.count[self.part])

    def learned(self):
        return {**self.names, **self.count}


SETS = {"a": 0, "b": 1, "c": 0}


def layer_units():
    units = [("qi", 0), ("qi", 1)]
    for x in "abc":
        units += [(s + x, i) for s in "qkvg" for i in range(2)]
    for n in range(3):
        for half in range(2):
            units += [("gate", n * 4 + half * 2), ("gate", n * 4 + half * 2 + 1), ("branch", n * 2 + half)]
    units += [("out", i) for i in range(4)]
    return units


BATCHES = [(x, qt, hg) for x in "iabc" for qt in range(2) for hg in range(2)]


def layer_order():
    order, ada = [], [0]

    def ada_unit(n=1):
        for _ in range(n):
            order.append(("unit", "ada", ada[0]))
            if ada[0]:
                order.append(("ada turn", ada[0] - 1))
            ada[0] += 1

    order += [("norm",), ("small",)]
    for n, (kind, i) in enumerate(layer_units()):
        order.append(("unit", kind, i))
        if (n % 2 == 1 and n < 43) or n in (43,):
            ada_unit()
        k = (n - 2) // 2
        if n >= 2 and n % 2 == 0:
            if 4 <= k - 1 < len(BATCHES) and BATCHES[k - 1][1]:
                order.append(("turn", k - 1, 1))
            if k < len(BATCHES):
                order.append(("scores", k))
        if n >= 3 and n % 2 == 1:
            if 4 <= k - 1 < len(BATCHES):
                order.append(("values", k - 1))
            if 4 <= k < len(BATCHES):
                order.append(("turn", k, 0))
        if n == 1:
            order += [("rope", "ki"), ("rope", "qi"), ("csum",)]
        if n in (3, 5):
            order.append(("rope", {3: "qa", 5: "ka"}[n]))
        if n in (11, 13):
            order.append(("rope", {11: "qb", 13: "kb"}[n]))
        if 4 <= n <= 7:
            order.append(("topk", 0, n - 4))
        if 9 <= n <= 12:
            order.append(("topk", 1, n - 9))
        if n == 43:
            order.append(("merged",))
        if n >= 44:
            order.append(("squares", n - 44))
            order.append(("sums", n - 44))
    ada_unit(24 - ada[0])
    order.append(("ada turn", 23))
    assert ada[0] == 24
    return order


ORDER = layer_order()
UNITS = [(kind, i) for what, *rest in ORDER if what == "unit" for kind, i in [rest]]
assert len(UNITS) % SLOTS == 0
JOBS = {}
for _kind, _i in UNITS:
    for _j in range(2 if _kind == "branch" else 1):
        JOBS[(_kind, _i, _j)] = len(JOBS)
assert len(JOBS) % BANKS == 0
JOB_AT = {n: job for job, n in JOBS.items()}


def end_order():
    order = [("final norm",), ("ctx",)]

    def all_squares(tag):
        order.extend(("squares", tag, c) for c in range(KC))
        order.extend(("sums", tag, c) for c in range(KC))

    def units(kind, n):
        for i in range(n):
            order.append(("unit", kind, i))

    def units_before_norm(kind, first, n, per, tag):
        for i in range(n):
            order.append(("unit", kind, first + i))
            order.extend((what, tag, per * i + c) for what in ("squares", "sums") for c in range(per))
        order.append(("mod norm", int(tag[0]), int(tag[1])))

    def ffn(layer):
        for grp in range(2):
            for j in range(FC // 2):
                order.append(("unit", f"up{layer}", grp * (FC // 2) + j))
            order.append(("flush", layer, grp))
            if layer == 0 and grp == 1:
                units_before_norm("down0", KC, KC, 1, "10")
            else:
                for m in range(KC):
                    order.append(("unit", f"down{layer}", grp * KC + m))

    all_squares("00")
    order.append(("mod norm", 0, 0))
    units("vs", 2)
    order.append(("sgu weights",))
    order.append(("unit", "f", 0))
    order.append(("v norm",))
    order.append(("unit", "f", 1))
    order.append(("dft feature", 0))
    order.append(("unit", "u", 0))
    order.append(("dft time", 0))
    order.append(("dft feature", 1))
    order.append(("unit", "u", 1))
    order.append(("sgu", 0))
    for g in range(1, 4):
        order.append(("dft time", g))
        if g < 3:
            order.append(("dft feature", g + 1))
        order.append(("sgu", g))
    units_before_norm("eo", 0, 4, 2, "01")
    ffn(0)
    units("nq", 4)
    between = {"nk1": [("qk squares", "q", 0), ("qk squares", "q", 1)], "nk2": [("qk sum", "q", 0), ("qk sum", "q", 1)],
               "nk3": [("qk spread", "q")], "nv0": [("qk squares", "k", 0)],
               "nv1": [("qk sum", "k", 0), ("qk squares", "k", 1)], "nv2": [("qk sum", "k", 1)],
               "nv3": [("qk spread", "k")]}
    for kind in ("nk", "nv"):
        for i in range(4):
            order.append(("unit", kind, i))
            order += between.get(f"{kind}{i}", [])
    for b in range(19):
        if b < 16:
            order.append(("near scores", b))
        if 2 <= b <= 17:
            order.append(("near turn", b - 2))
        if b >= 3:
            order.append(("near values", b - 3))
        if b < 16:
            order.append(("near exp", b))
    units_before_norm("wo", 0, 4, 2, "11")
    ffn(1)
    order.append(("finish",))
    return order


END = end_order()
END_UNITS = [(kind, i) for what, *rest in END if what == "unit" for kind, i in [rest]]


def end_jobs(kind):
    return 1 if kind in ("nq", "wo", "up1", "down0", "down1") else 2


END_JOBS = {}
for _kind, _i in END_UNITS:
    for _j in range(end_jobs(_kind)):
        END_JOBS[(_kind, _i, _j)] = len(END_JOBS)
END_JOB_AT = {n: job for job, n in END_JOBS.items()}


def end_evacuator(kind, j):
    if kind in ("f", "u", "vs", "nq", "nk", "nv"):
        return "act"
    return "dve"


def evacuator(kind):
    return "dve" if kind in ("branch", "out", "ga", "gb", "gc") else "act"


def mod_col(part):
    return part * KC


def program(nc, ins, out, known):
    with ExitStack() as ctx:
        at = [DMA_SCRATCH]

        def sb(name, shape, dt=F32, offset=None):
            size = 4 * int(np.prod(shape[1:]))
            if offset is None:
                offset = at[0]
                at[0] += (size + 31) // 32 * 32
            return nc.alloc_sbuf_tensor_at(name, shape, dt, offset=offset)

        def bank(name, shape):
            return ctx.enter_context(nc.psum_tensor(name, shape, F32))

        def sem(name):
            return ctx.enter_context(nc.semaphore(name))

        raw = sb("raw", [P, SLOTS, UNIT])
        w_hi = sb("w_hi", [P, SLOTS, UNIT], F32R)
        w_lo = sb("w_lo", [P, SLOTS, UNIT], F32R)
        ident = sb("ident", [P, P])
        ones = sb("ones", [P, P])
        vec = sb("vec", [P, VROWS])
        mod = sb("mod", [P, DEPTH, 48, 2])
        s_parts = sb("s_parts", [P, KC, 4], F32R)
        eps = sb("eps", [P, 1])
        x_t = sb("x_t", [P, KC, SEQ])
        base = at[0]

        h_hi = sb("h_hi", [P, KC, SEQ], F32R)
        h_lo = sb("h_lo", [P, KC, SEQ], F32R)
        o_hi = sb("o_hi", [P, 12, SEQ], F32R)
        o_lo = sb("o_lo", [P, 12, SEQ], F32R)
        h = sb("h", [P, KC, SEQ])
        qk = [sb(f"qk{s}", [P, 8, SEQ]) for s in range(2)]
        v = [sb(f"v{s}", [P, 2, WIDTH]) for s in range(2)]
        g = [sb(f"g{s}", [P, 4, SEQ]) for s in range(2)]
        ki = sb("ki", [P, SEQ])
        token_root1 = sb("token_root1", [P, 2])
        turned = sb("turned", [P, 4, SEQ])
        scaled = sb("scaled", [P, 4, SEQ])
        probs_at = at[0]
        probs = [sb(f"probs{s}", [P, 4, SEQ]) for s in range(2)]
        probs_t = sb("probs_t", [P, 2, 4, P])
        gates = scaled[:, :, :].rearrange("p (a b) t -> p a b t", a=2)
        rope = sb("rope", [P, 2, SEQ])
        causal = sb("causal", [P, 2, SEQ])
        upto = sb("upto", [P, 2, SEQ])
        picked = sb("picked", [P, 2, SEQ])
        isc = sb("isc", [P, SEQ])
        work = sb("work", [P, SEQ])
        csum_t = sb("csum_t", [P, SEQ])
        logf = sb("logf", [P, 2, P])
        w_small = sb("w_small", [P, KC, 144])
        o_gated = sb("o_gated", [P, 2, 2, P])
        branch_y = turned[:, 0:2, :]
        pick = sb("pick", [P, 8])
        gain = sb("gain", [P, KC])
        ada_bias = sb("ada_bias", [P, 48])
        mod_now = sb("mod_now", [P, 48, 2])
        ada_row = sb("ada_row", [4, 2, 256])
        add_parts = sb("add_parts", [4, 2])
        token_rstd1 = sb("token_rstd1", [P, 2])
        fbias = sb("fbias", [P, DEPTH, 8])
        fbias_now = sb("fbias_now", [P, 8])
        w_f = sb("w_f", [P, 2, 16])
        f_abs = sb("f_abs", [P, 2, 8])
        f_min = sb("f_min", [P, 2, 8])
        f_log = sb("f_log", [P, 2, 8])
        csum_q = sb("csum_q", [P, 2, 8])
        negmax = sb("negmax", [P, 2, 4])
        rowsum = sb("rowsum", [P, 2, 4])
        rowinv = sb("rowinv", [P, 4])
        top8 = sb("top8", [P, 8])
        s_f = sb("s_f", [P, 2, KC])
        used1 = at[0]
        at[0] = base
        c_t_at = at[0]
        c_t = sb("c_t", [P, KC, CTX])
        root_at = at[0]
        m_root = sb("m_root", [P, 512])
        m_rstd = sb("m_rstd", [P, 512])
        token_root = sb("token_root", [P, 4])
        token_rstd = sb("token_rstd", [P, 4])
        m_gain = sb("m_gain", [P, KC, 2])
        h2 = sb("h2", [P, KC, 512])
        h2_at = at[0] - 16384
        h2_hi_at = at[0]
        h2_hi = sb("h2_hi", [P, KC, 512], F32R)
        h2_lo = sb("h2_lo", [P, KC, 512], F32R)
        f_hi_at = at[0]
        f_hi = sb("f_hi", [P, FC // 2, 512], F32R)
        f_lo_at = at[0]
        f_lo = sb("f_lo", [P, FC // 2, 512], F32R)
        area = at[0]
        conv = sb("conv", [P, 2, 512])
        hidden = sb("hidden", [P, 2, 512])
        used2 = at[0]
        f_t = sb("f_t", [P, 4, 512], offset=h2_at)
        dft_f = [sb(f"dft_f{n}", [P, 4, 256], offset=h2_at + 8192 + 4096 * n) for n in range(2)]
        v_sq = sb("v_sq", [P, 4, 512], offset=f_lo_at + 8192)
        gated_b = sb("gated_b", [P, 2, 512], offset=root_at)
        u_t = sb("u_t", [P, 4, 512], offset=area)
        v_s = sb("v_s", [P, 4, 512], offset=area + 8192)
        v_sum = sb("v_sum", [P, 16], offset=area + 16384)
        v_inv = sb("v_inv", [P, 16], offset=area + 16448)
        tail = 8 * 2048
        dft_t = sb("dft_t", [P, 2, 2, SEQ], offset=f_hi_at + tail)
        w_s_t = sb("w_s_t", [P, 4, P], offset=f_hi_at + tail + 4096)
        w_s = sb("w_s", [P, 4, P], offset=f_lo_at + tail)
        b_s = sb("b_s", [1, 4, P], offset=f_lo_at + tail + 2048)
        dft_c = sb("dft_c", [P, 2 * P], offset=f_lo_at + tail + 4096)
        k_n = sb("k_n", [P, KC, 512], offset=h2_at)
        v_n = sb("v_n", [P, 4, D], offset=area)
        q_n = sb("q_n", [P, KC, SEQ], offset=f_hi_at + 8192)
        head_sum = sb("head_sum", [P, KC, 16], offset=f_hi_at + 16384)
        head_spread = sb("head_spread", [16, KC, P], offset=f_hi_at + 16896)
        qk_sq = sb("qk_sq", [P, 4, 512], offset=f_lo_at + 8192)
        window = sb("window", [P, SEQ], offset=f_lo_at + 16384)
        near_max = sb("near_max", [P, 2, 2], offset=f_lo_at + 18432)
        near_sum = sb("near_sum", [P, 2, 2], offset=f_lo_at + 18464)
        near_inv = sb("near_inv", [P, 2], offset=f_lo_at + 18496)
        near_p = [sb(f"near_p{n}", [P, 2, 512], offset=h2_hi_at + 4096 * n) for n in range(3)]
        near_pt = sb("near_pt", [P, 2, 4, 2, P], offset=h2_hi_at + 12288)
        bias = [sb(f"bias{n}", [P, 4, SEQ], offset=c_t_at + 4096 * n if n < 2 else h2_hi_at + 20480)
                for n in range(3)]
        out_sb = sb("out_sb", [P, 2, D], offset=h2_at)
        c_in = sb("c_in", [P, 2, D], offset=probs_at)
        used2 = max(used2, area + 16384 + 256)
        assert used2 <= SBUF_BYTES, used2
        x_in = h[:, :, :].rearrange("p c t -> p (c t)").rearrange("p (t f) -> p t f", t=2)
        vec_in = qk[0][:, 0:2, :].rearrange("p a b -> p (a b)")[:, 0:VROWS].rearrange("p (a b) -> p a b", a=3)
        assert used1 <= SBUF_BYTES, used1

        banks_g = bank("banks_g", [P, BANKS, 512])
        bank_g = [banks_g[:, i, :] for i in range(BANKS)]
        bank_s = bank("bank_s", [P, 4, SEQ])
        bank_t = bank("bank_t", [P, 4, P])
        bank_o = bank("bank_o", [P, 512])
        bank_m = bank("bank_m", [P, 512])

        pe_steps, act_steps, dve_steps, pool_steps = (sem(f"{n}_steps") for n in ("pe", "act", "dve", "pool"))
        raw_loaded = [sem(f"raw_loaded{s}") for s in range(SLOTS)]
        x_loaded = sem("x_loaded")
        consts_loaded = sem("consts_loaded")
        small_loaded = sem("small_loaded")
        stored = sem("stored")
        ctx_loaded = sem("ctx_loaded")
        end_loaded = sem("end_loaded")
        odd_loaded = sem("odd_loaded")
        bias_loaded = [sem(f"bias_loaded{n}") for n in range(3)]
        sp_passed, dve_passed, pe_passed = sem("sp_passed"), sem("dve_passed"), sem("pe_passed")
        pe_, act_, dve_, pool_ = (Steps(known.get(n)) for n in ("pe", "act", "dve", "pool"))
        every = (pe_, act_, dve_, pool_)

        def enter(part, layer=0):
            for s in every:
                s.part, s.layer = part, layer

        def loaded(u, layer):
            return layer * (16 * len(UNITS) // SLOTS) + 16 * (u // SLOTS + 1)

        def streams(kind_or_n):
            return 1 if kind_or_n in ("nq", "wo", "up1", "down1") else 2

        end_value, so_far = [], [16 * DEPTH * len(UNITS) // SLOTS] * SLOTS
        for u, (kind, i) in enumerate(END_UNITS):
            so_far[u % SLOTS] += 32 if kind in ("up0", "up1") else 16
            end_value.append(so_far[u % SLOTS])

        def size(kind):
            return FC // 2 * P if kind in ("down0", "down1") else UNIT

        x_streams = (x_t, c_t)

        def norm_tiles(tag):
            return 2 if tag in ("f", "11") else 4

        END_LOADS = 4

        def backwards(t):
            dims = [list(d) for d in t.ap]
            n = dims[-1][1]
            return bass.AP(t.tensor, t.offset + n - 1, dims[:-1] + [[-1, n]])

        def conv_col(ly, tap, i):
            n = ROWS["conv_b"] + ly * FC + i if tap == 3 else ROWS["conv_w"] + (ly * 3 + tap) * FC + i
            return vec[:, n:n + 1]

        def near_banks(b):
            return bank_s[:, :, :].rearrange("p (e a) k -> p e (a k)", e=2) if b % 2 == 0 else banks_g[:, 1:3, :]

        block = ctx.enter_context(nc.Block())

        CONSTS = 6

        @block.sync
        def _(sp):
            enter("start")
            sp.dma_start(ident[:, :], ins["ident"]).then_inc(x_loaded, 16)
            sp.dma_start(vec_in, ins["vectors"].rearrange("(a p) f -> p a f", p=P)).then_inc(x_loaded, 16)
            sp.dma_start(x_in, ins["x"][0].rearrange("(t p) f -> p t f", p=P)).then_inc(x_loaded, 16)
            with sp.Fori(0, DEPTH) as layer:
                enter("layer", layer)
                w_in_l = ins["w_in"][bass.ds(layer, 1)].rearrange("l (c p) n -> (l p) c n", p=P)

                def columns(c0, n):
                    return w_in_l[:, :, c0:c0 + n]

                sp.wait_ge(pe_steps, pe_.at("small", before=True))
                for d0, c0, n in ((0, K_IDX0, 64), (64, K_IDX0, 80)):
                    sp.dma_start(w_small[:, :, d0:d0 + n], columns(c0, n)).then_inc(small_loaded, 16)
                for u, (kind, i) in enumerate(UNITS):
                    before = (u - SLOTS) % len(UNITS)
                    if UNITS[before][0] == "ada":
                        sp.wait_ge(pool_steps, pool_.at(f"lo{before}", before=u < SLOTS))
                    else:
                        sp.wait_ge(dve_steps, dve_.at(f"lo{before}", before=u < SLOTS))
                    sp.sem_inc(sp_passed, 1)
                    slot = raw[:, u % SLOTS, :]
                    if kind == "branch":
                        n, half = divmod(i, 2)
                        src = ins["w_branch"][bass.ds(layer, 1), n].rearrange("l (c p) n -> (l p) c n", p=P)[
                            :, :, half * 512:half * 512 + 512]
                        dst = slot.rearrange("p (c n) -> p c n", c=4)
                    else:
                        dst = slot.rearrange("p (c n) -> p c n", c=KC)
                        if kind == "ada":
                            src = ins["ada_w"][bass.ds(layer, 1)].rearrange("l (c p) n -> (l p) c n", p=P)[
                                :, :, i * 256:i * 256 + 256]
                        elif kind == "out":
                            src = ins["w_out"][bass.ds(layer, 1)].rearrange("l (c p) n -> (l p) c n", p=P)[
                                :, :, i * 256:i * 256 + 256]
                        elif kind == "gate":
                            src = columns(MERGE0 + i * 256, 256)
                        elif kind == "qi":
                            src = columns(Q_IDX0 + i * 256, 256)
                        else:
                            section = "abc".index(kind[1]) * 4 + "qkvg".index(kind[0])
                            src = columns(section * WIDTH + i * 256, 256)
                    sp.dma_start(dst, src).then_inc(raw_loaded[u % SLOTS], 16)
            enter("end")
            sp.wait_ge(pe_steps, pe_.at("values15"))
            sp.dma_start(c_in[:, :, :], ins["ctx"][0].rearrange("(t p) f -> p t f", p=P)).then_inc(ctx_loaded, 16)
            for u, (kind, i) in enumerate(END_UNITS):
                if u >= SLOTS:
                    sp.wait_ge(dve_steps, dve_.at(f"lo{u - SLOTS}"))
                elif UNITS[u - SLOTS][0] == "ada":
                    sp.wait_ge(pool_steps, pool_.at(f"lo{len(UNITS) + u - SLOTS}", before=True))
                else:
                    sp.wait_ge(dve_steps, dve_.at(f"lo{len(UNITS) + u - SLOTS}", before=True))
                slot = raw[:, u % SLOTS, :]
                cols = slice(i * 256, i * 256 + 256)
                if kind in ("up0", "up1"):
                    src = ins["w_up"][int(kind[2])].rearrange("(c p) (g n) -> p c g n", p=P, g=2)
                    for gv in range(2):
                        sp.dma_start(slot.rearrange("p (c g n) -> p c g n", c=KC, g=2)[:, :, gv, :],
                                     src[:, :, gv, i * P:i * P + P]).then_inc(raw_loaded[u % SLOTS], 16)
                    continue
                if kind in ("down0", "down1"):
                    grp, m = divmod(i, KC)
                    rows = slice(grp * (D_FF // 2), (grp + 1) * (D_FF // 2))
                    src = ins["w_down"][int(kind[4]), rows, m * P:m * P + P].rearrange("(c p) n -> p c n", p=P)
                    dst = slot[:, 0:FC // 2 * P].rearrange("p (c n) -> p c n", c=FC // 2)
                else:
                    dst = slot.rearrange("p (c n) -> p c n", c=KC)
                    name, c0 = {"f": ("even_in", 0), "u": ("even_in", 512), "vs": ("even_in", 1024),
                                "eo": ("even_out", 0), "nq": ("qkv", 0), "nk": ("qkv", D), "nv": ("qkv", 2 * D),
                                "wo": ("odd_out", 0)}[kind]
                    src = ins[name].rearrange("(c p) n -> p c n", p=P)[:, :, c0 + i * 256:c0 + i * 256 + 256]
                sp.dma_start(dst, src).then_inc(raw_loaded[u % SLOTS], 16)
            sp.wait_ge(act_steps, act_.at("out1"))
            sp.dma_start(out.rearrange("o (t p) f -> p (o t) f", p=P), out_sb[:, :, :]).then_inc(stored, 16)
            sp.wait_ge(stored, 16)

        @block.tensor
        def _(pe):
            enter("start")
            pe.sem_inc(pe_steps, pe_.total("layer") or 1)
            pe.wait_ge(x_loaded, 16 * 3)
            for b in range(4):
                for j in range(2):
                    for t in range(2):
                        dst = [bank_s[:, 0:2, :], bank_s[:, 2:4, :], bank_o[:, :].rearrange("p (j t) -> p j t", j=2),
                               bank_m[:, :].rearrange("p (j t) -> p j t", j=2)][b][:, j, t * P:t * P + P]
                        last = nc.tensor.transpose(dst, x_in[:, t, (2 * b + j) * P:(2 * b + j + 1) * P], ident[:, :])
                last.then_inc(pe_steps, pe_.step(f"x turned{b}"))
            for a in range(3):
                last = nc.tensor.transpose(bank_t[:, a, :], vec_in[:, a, :], ident[:, :])
            last.then_inc(pe_steps, pe_.step("vec turned"))

            def sum_squares():
                pe.wait_ge(dve_steps, dve_.at("mod now", before=True) if pe_.part == "layer" else dve_.at("mod now"))
                for t in range(2):
                    for j in range(2):
                        last = nc.tensor.matmul(bank_m[:, SUM_COL + t:SUM_COL + t + 1],
                                                qk[1][:, j, t * P:t * P + P], ones[:, 0:1],
                                                start=j == 0, stop=j == 1)
                last.then_inc(pe_steps, pe_.step("sumsq"))

            pe.wait_ge(consts_loaded, 16 * CONSTS)
            pe.wait_ge(pool_steps, pool_.at("ones"))
            pe.wait_ge(dve_steps, dve_.at("added3"))

            with pe.Fori(0, DEPTH) as layer:
                enter("layer", layer)
                u = 0
                bank_m_read = []
                for what, *arg in ORDER:
                    if what == "unit":
                        kind, i = arg
                        s = u % SLOTS
                        need = []
                        if kind == "ada":
                            pe.wait_ge(pool_steps, pool_.at(f"lo{u}"))
                        else:
                            need.append(f"lo{u}")
                        kcs = 4 if kind == "branch" else KC
                        wh = w_hi[:, s, :].rearrange("p (c n) -> p c n", c=kcs)
                        wl = w_lo[:, s, :].rearrange("p (c n) -> p c n", c=kcs)
                        if kind in ("qi", "qa") and i == 0:
                            need.append("h lo1")
                        if kind == "branch" and i % 2 == 0:
                            need.append(f"o lo{7 + 4 * (i // 2)}")
                        if kind == "out" and i == 0:
                            need.append("merged lo1")
                        for j in range(2 if kind == "branch" else 1):
                            k = JOBS[(kind, i, j)]
                            gb = bank_g[k % BANKS]
                            b3 = (k - BANKS) % len(JOBS)
                            who = evacuator(JOB_AT[b3][0])
                            if who == "dve":
                                need.append(("<" if k < BANKS else "") + f"empty{b3}")
                            else:
                                pe.wait_ge(act_steps, act_.at(f"empty{b3}", before=k < BANKS))
                            if need:
                                pe.wait_ge(dve_steps, dve_.latest(*need))
                            need = []
                            if kind == "ada":
                                for c in range(KC):
                                    for w in (wl, wh):
                                        last = nc.tensor.matmul(gb[0:4, 0:256], s_parts[:, c, :], w[:, c, :],
                                                                start=c == 0 and w is wl,
                                                                stop=c == KC - 1 and w is wh)
                            elif kind[0] == "v":
                                ov = gb[:, :].rearrange("p (t n) -> p t n", t=2)
                                for t in range(2):
                                    for c in range(KC):
                                        for n, (a, w) in enumerate(((h_lo, wh), (h_hi, wl), (h_hi, wh))):
                                            last = nc.tensor.matmul(ov[:, t, :], a[:, c, t * P:t * P + P], w[:, c, :],
                                                                    start=c == 0 and n == 0,
                                                                    stop=c == KC - 1 and n == 2)
                            else:
                                ov = gb[:, :].rearrange("p (m t) -> p m t", m=2)
                                ah, al, a0 = (o_hi, o_lo, 4 * (i // 2)) if kind == "branch" else (h_hi, h_lo, 0)
                                for m in range(2):
                                    m0 = j * 256 + m * P
                                    for c in range(kcs):
                                        for n, (w, a) in enumerate(((wl, ah), (wh, al), (wh, ah))):
                                            last = nc.tensor.matmul(ov[:, m, :], w[:, c, m0:m0 + P], a[:, a0 + c, :],
                                                                    start=c == 0 and n == 0,
                                                                    stop=c == kcs - 1 and n == 2)
                            last.then_inc(pe_steps, pe_.step(f"job{k}", f"unit{u}"))
                        u += 1
                    elif what == "ada turn":
                        i, = arg
                        pe.wait_ge(act_steps, act_.latest(f"ada row{i}", *bank_m_read))
                        if i == 0:
                            pe.wait_ge(dve_steps, dve_.at("mod now", before=True))
                        for m in range(2):
                            n = ADA_COL + 4 * i + 2 * m
                            last = nc.tensor.matmul(bank_m[:, n:n + 2], ada_row[0:4, i % 2, m * P:m * P + P],
                                                    add_parts[0:4, :], start=True, stop=True)
                        last.then_inc(pe_steps, pe_.step(f"ada turn{i}"))
                    elif what == "norm":
                        sum_squares()
                        pe.wait_ge(dve_steps, dve_.at("token rstd"))
                        for t in range(2):
                            last = nc.tensor.matmul(bank_o[:, t * P:t * P + P],
                                                    token_rstd1[:, t:t + 1].to_broadcast([P, P]), ident[:, :],
                                                    start=True, stop=True)
                        last.then_inc(pe_steps, pe_.step("spread"))
                        bank_m_read = ["root"]
                    elif what == "small":
                        pe.wait_ge(small_loaded, layer * 32 + 32)
                        pe.wait_ge(act_steps, act_.at("root"))
                        for c in range(KC):
                            pe.wait_ge(dve_steps, dve_.at(f"h{c}"))
                            pe.sem_inc(pe_passed, 1)
                            nc.tensor.matmul(bank_m[:, 0:SEQ], w_small[:, c, 0:P], h[:, c, :],
                                             start=c == 0, stop=c == KC - 1)
                        for t in range(2):
                            for c in range(KC):
                                last = nc.tensor.matmul(bank_o[:, t * 16:t * 16 + 16], h[:, c, t * P:t * P + P],
                                                        w_small[:, c, P:144], start=c == 0, stop=c == KC - 1)
                        last.then_inc(pe_steps, pe_.step("small"))
                        bank_m_read = ["ki"]
                    elif what == "csum":
                        pe.wait_ge(dve_steps, dve_.at("logf"))
                        pe.wait_ge(act_steps, act_.at("ki"))
                        for j in range(2):
                            nc.tensor.matmul(bank_m[:, 0:SEQ], logf[:, j, :], upto[:, j, :], start=j == 0, stop=j == 1)
                        for qt in range(2):
                            for j in range(qt + 1):
                                last = nc.tensor.matmul(bank_o[:, 32 + qt * 8:40 + qt * 8],
                                                        upto[:, j, qt * P:qt * P + P], logf[:, j, 0:8],
                                                        start=j == 0, stop=j == qt)
                        last.then_inc(pe_steps, pe_.step("csum"))
                        bank_m_read = ["csum t"]
                    elif what == "scores":
                        k, = arg
                        x, qt, hg = BATCHES[k]
                        nk = P * (qt + 1)
                        need = ["<masked15"] if k == 0 else [f"masked{k - 1}"] if k > 4 else []
                        if 0 < k <= 4:
                            pe.wait_ge(act_steps, act_.at(f"relu{k - 1}"))
                        if x == "i":
                            need.append("rope qi")
                            qs, ks, kc = qk[1], ki, None
                        else:
                            qs = ks = qk[SETS[x]]
                            kc = 4
                            if x == "c":
                                pe.wait_ge(act_steps, act_.latest(f"empty{JOBS[('kc', 1, 0)]}", "csum"))
                            else:
                                need.append("rope k" + x)
                        pe.wait_ge(dve_steps, dve_.latest(*need))
                        for e in range(2):
                            r = slice(64 * e, 64 * e + 64)
                            for j in range(2):
                                c = 2 * hg + j
                                dst = bank_s[:, 2 * e + j, 0:nk]
                                if x == "c":
                                    hh = 4 * hg + 2 * j + e
                                    nc.tensor.matmul(dst, pick[r, hh:hh + 1].to_broadcast([64, P]), csum_t[r, 0:nk],
                                                     start=True, stop=False)
                                keys = ks[r, 0:nk] if kc is None else ks[r, kc + c, 0:nk]
                                last = nc.tensor.matmul(dst, qs[r, c, qt * P:qt * P + P], keys,
                                                        start=x != "c", stop=True)
                        last.then_inc(pe_steps, pe_.step(f"scores{k}"))
                    elif what == "turn":
                        k, kt = arg
                        pe.wait_ge(dve_steps, dve_.at(f"probs{k}"))
                        if (k, kt) == (4, 0):
                            pe.wait_ge(act_steps, act_.at(f"turned15 {BATCHES[15][1]}", before=True))
                        else:
                            pk, pt = (k, 0) if kt else (k - 1, BATCHES[k - 1][1])
                            pe.wait_ge(act_steps, act_.at(f"turned{pk} {pt}"))
                        for s in range(4):
                            last = nc.tensor.transpose(bank_t[:, s, :], probs[k % 2][:, s, kt * P:kt * P + P],
                                                       ident[:, :])
                        last.then_inc(pe_steps, pe_.step(f"turn{k} {kt}"))
                    elif what == "values":
                        k, = arg
                        x, qt, hg = BATCHES[k]
                        pe.wait_ge(act_steps, act_.latest(f"turned{k} {qt}", f"empty{JOBS[('v' + x, 1, 0)]}", "csum"))
                        if k > 4:
                            pe.wait_ge(dve_steps, dve_.at(f"gated{k - 1}"))
                        for e in range(2):
                            for j in range(2):
                                hh = 4 * hg + 2 * j + e
                                for kt in range(qt + 1):
                                    last = nc.tensor.matmul(bank_o[64 * e:64 * e + 64, j * P:j * P + P],
                                                            v[SETS[x]][:, kt, hh * HD:hh * HD + HD],
                                                            probs_t[:, kt, 2 * e + j, :], start=kt == 0, stop=kt == qt)
                        last.then_inc(pe_steps, pe_.step(f"values{k}"))

            enter("end")

            def lanes(t):
                return t[:, :].rearrange("p (a b) -> p a b", a=4)

            u = 0
            for what, *arg in END:
                if what == "unit":
                    kind, i = arg
                    st = u % SLOTS
                    n_s = streams(kind)
                    nt = SEQ * n_s
                    down, up = kind[:4] == "down", kind[:2] == "up"
                    kcs = FC // 2 if down else KC
                    wide = P if down else 256
                    wh = w_hi[:, st, 0:kcs * wide].rearrange("p (c n) -> p c n", c=kcs)
                    wl = w_lo[:, st, 0:kcs * wide].rearrange("p (c n) -> p c n", c=kcs)
                    pe.wait_ge(dve_steps, dve_.at(f"lo{u}"))
                    ah, al, a_ready = h2_hi, h2_lo, None
                    if i == 0 and kind in ("vs", "nq", "up0", "up1"):
                        tag = {"vs": "00", "nq": "10", "up0": "01", "up1": "11"}[kind]
                        a_ready = [f"h2 lo{tag} {c}" for c in range(KC)]
                    if kind == "eo":
                        ah, al = f_hi, f_lo
                        a_ready = [f"a lo{c}" for c in range(4)] + [f"b lo{c}" for c in range(4)] if i == 0 else None
                    if kind == "wo":
                        ah, al = (t[:, 0:4, :].rearrange("p a (b t) -> p (a b) t", b=2) for t in (f_hi, f_lo))
                        a_ready = ["near lo15"] * KC if i == 0 else None
                    if down:
                        ah, al = f_hi, f_lo
                        if i % KC == 0:
                            a_ready = [f"f lo{kind[4]} {i // KC * (FC // 2) + c}" for c in range(FC // 2)]
                    def bank_empty(k):
                        if k < BANKS:
                            n = len(JOBS) - BANKS + k
                            if evacuator(JOB_AT[n][0]) == "dve":
                                pe.wait_ge(dve_steps, dve_.at(f"empty{n}", before=True))
                            else:
                                pe.wait_ge(act_steps, act_.at(f"empty{n}", before=True))
                        elif end_evacuator(*END_JOB_AT[k - BANKS][::2]) == "dve":
                            pe.wait_ge(dve_steps, dve_.at(f"empty{k - BANKS}"))
                        else:
                            pe.wait_ge(act_steps, act_.at(f"empty{k - BANKS}"))

                    if (kind, i) in (("vs", 0), ("up0", 0), ("up1", 0)):
                        pieces = [(j, m) for j in range(end_jobs(kind)) for m in range(2 // end_jobs(kind))]
                        if kind == "vs":
                            pieces = [(0, 0), (0, 1), (1, 0), (1, 1)]
                        ends = [max(p for p in pieces if p[0] == j) for j in range(end_jobs(kind))]
                        for j in range(end_jobs(kind)):
                            bank_empty(END_JOBS[(kind, i, j)])
                        for c in range(KC):
                            pe.wait_ge(dve_steps, dve_.at(a_ready[c]))
                            for j, m in pieces:
                                gb = bank_g[END_JOBS[(kind, i, j)] % BANKS]
                                for n in range(3):
                                    w, a = ((wl, ah), (wh, al), (wh, ah))[n]
                                    if kind == "vs":
                                        t0 = (2 * j + m) * P
                                        last = nc.tensor.matmul(gb[:, m * 256:m * 256 + 256], a[:, c, t0:t0 + P],
                                                                w[:, c, :], start=(m, c, n) == (0, 0, 0),
                                                                stop=(j, m) in ends and (c, n) == (KC - 1, 2))
                                    else:
                                        m0 = (j + m) * P
                                        last = nc.tensor.matmul(gb[:, m * SEQ:m * SEQ + nt], w[:, c, m0:m0 + P],
                                                                a[:, c, 0:nt], start=(m, c, n) == (0, 0, 0),
                                                                stop=(j, m) in ends and (c, n) == (KC - 1, 2))
                        last.then_inc(pe_steps, pe_.step(*(f"job{END_JOBS[(kind, i, j)]}"
                                                           for j in range(end_jobs(kind))), f"unit{u}"))
                        u += 1
                        continue
                    for j in range(end_jobs(kind)):
                        k = END_JOBS[(kind, i, j)]
                        bank_empty(k)
                        gb = bank_g[k % BANKS]
                        if kind in ("vs", "nv"):
                            for tt in range(2):
                                t0 = (2 * j + tt) * P
                                for c in range(KC):
                                    if a_ready and j == 0 and tt == 0:
                                        pe.wait_ge(dve_steps, dve_.at(a_ready[c]))
                                    for n, (a, w) in enumerate(((h2_lo, wh), (h2_hi, wl), (h2_hi, wh))):
                                        last = nc.tensor.matmul(gb[:, tt * 256:tt * 256 + 256], a[:, c, t0:t0 + P],
                                                                w[:, c, :], start=c == 0 and n == 0,
                                                                stop=c == KC - 1 and n == 2)
                        else:
                            chunks = 1 if nt == 512 or down else 2
                            for m in range(chunks):
                                m0 = (j * chunks + m) * P
                                for c in range(kcs):
                                    if a_ready and j == 0 and m == 0:
                                        pe.wait_ge(dve_steps, dve_.at(a_ready[c]))
                                    for n, (w, a) in enumerate(((wl, ah), (wh, al), (wh, ah))):
                                        last = nc.tensor.matmul(gb[:, m * SEQ:m * SEQ + nt], w[:, c, m0:m0 + P],
                                                                a[:, c, 0:nt], start=c == 0 and n == 0,
                                                                stop=c == kcs - 1 and n == 2)
                        last.then_inc(pe_steps, pe_.step(f"job{k}", f"unit{u}"))
                    u += 1
                elif what == "ctx":
                    pe.wait_ge(ctx_loaded, 16)
                    for b in range(4):
                        dst = [bank_s[:, 0:2, :], bank_s[:, 2:4, :], bank_o[:, :].rearrange("p (j t) -> p j t", j=2),
                               bank_t[:, :, :].rearrange("p (j t) n -> p j (t n)", j=2)][b]
                        for j in range(2):
                            for t in range(2):
                                last = nc.tensor.transpose(dst[:, j, t * P:t * P + P],
                                                           c_in[:, t, (2 * b + j) * P:(2 * b + j + 1) * P], ident[:, :])
                        last.then_inc(pe_steps, pe_.step(f"ctx turned{b}"))
                elif what in ("final norm", "mod norm"):
                    tag = "f" if what == "final norm" else f"{arg[0]}{arg[1]}"
                    if tag == "f":
                        sum_squares()
                    else:
                        pe.wait_ge(dve_steps, dve_.at(f"added{tag} {KC - 1}"))
                        if tag == "11":
                            pe.wait_ge(act_steps, act_.at("near turned15 1"))
                        for t in range(norm_tiles(tag)):
                            last = nc.tensor.matmul(bank_m[:, t:t + 1], h2[:, 0, t * P:t * P + P], ones[:, 0:1],
                                                    start=True, stop=True)
                        last.then_inc(pe_steps, pe_.step(f"sumsq{tag}"))
                    pe.wait_ge(dve_steps, dve_.at(f"token rstd{tag}"))
                    for t in range(norm_tiles(tag)):
                        dst = bank_m[:, t * P:t * P + P] if tag == "f" else bank_t[:, t, :]
                        last = nc.tensor.matmul(dst, token_rstd[:, t:t + 1].to_broadcast([P, P]),
                                                ident[:, :], start=True, stop=True)
                    last.then_inc(pe_steps, pe_.step(f"spread{tag}"))
                elif what == "sgu weights":
                    pe.wait_ge(end_loaded, 16 * END_LOADS)
                    pe.wait_ge(act_steps, act_.at("ctx3"))
                    for g_ in range(4):
                        last = nc.tensor.transpose(bank_t[:, g_, :], w_s[:, g_, :], ident[:, :])
                    last.then_inc(pe_steps, pe_.step("sgu weights"))
                elif what == "dft feature":
                    g_, = arg
                    pe.wait_ge(act_steps, act_.at("dft feature" + str(g_ - 1) if g_ else f"empty{END_JOBS[('f', 1, 1)]}"))
                    for t in range(4):
                        last = nc.tensor.matmul(bank_s[:, t, :], f_t[:, g_, t * P:t * P + P], dft_c[:, :],
                                                start=True, stop=True)
                    last.then_inc(pe_steps, pe_.step(f"dft feature{g_}"))
                elif what == "dft time":
                    g_, = arg
                    pe.wait_ge(act_steps, act_.at(f"dft feature{g_}"))
                    if g_:
                        pe.wait_ge(dve_steps, dve_.at(f"a lo{g_ - 1}"))
                    bt = bank_t[:, :, :].rearrange("p a b -> p (a b)")
                    for s_ in range(2):
                        n = 0
                        for t in range(2):
                            for cs in range(2):
                                last = nc.tensor.matmul(bt[:, s_ * SEQ:s_ * SEQ + SEQ],
                                                        dft_f[g_ % 2][:, 2 * s_ + t, cs * P:cs * P + P],
                                                        dft_t[:, t, cs, :], start=n == 0, stop=n == 3)
                                n += 1
                    last.then_inc(pe_steps, pe_.step(f"dft time{g_}"))
                elif what == "sgu":
                    g_, = arg
                    pe.wait_ge(dve_steps, dve_.at(f"gated b{g_ - 1}" if g_ else "v norm"))
                    pe.wait_ge(act_steps, act_.at("ctx3"))
                    nc.tensor.matmul(bank_o[:, :], ones[0:1, :], b_s[0:1, g_:g_ + 1, :].to_broadcast([1, 4, P]),
                                     start=True, stop=False)
                    for t in range(4):
                        last = nc.tensor.matmul(bank_o[:, t * P:t * P + P], v_s[:, t, g_ * P:g_ * P + P],
                                                w_s_t[:, g_, :], start=False, stop=t == 3)
                    last.then_inc(pe_steps, pe_.step(f"sgu{g_}"))
                elif what == "qk sum":
                    x, half = arg
                    src = qk_sq[:, :, :].rearrange("p a (b t) -> p (a b) t", b=2) if x == "q" else qk_sq
                    nt = SEQ if x == "q" else 512
                    pe.wait_ge(odd_loaded, 16 * 3)
                    pe.wait_ge(act_steps, act_.at(f"squares{x}{half}"))
                    for c in range(4 * half, 4 * half + 4):
                        last = nc.tensor.matmul(bank_m[0:16, 0:nt], head_sum[:, c, :],
                                                src[:, c % (8 if x == "q" else 4), :], start=c == 0, stop=c == KC - 1)
                    last.then_inc(pe_steps, pe_.step(f"sumsq{x}{half}"))
                elif what == "qk spread":
                    x, = arg
                    nt = SEQ if x == "q" else 512
                    pe.wait_ge(dve_steps, dve_.at(f"rstd{x}"))
                    for c in range(KC):
                        dst = (bank_t[:, :, :].rearrange("p a b -> p (a b)") if c % 2 == 0 else bank_o)[:, 0:nt]
                        if c >= 2:
                            pe.wait_ge(dve_steps, dve_.at(f"normed{x}{c - 2}"))
                        nc.tensor.matmul(dst, head_spread[0:16, c, :], m_rstd[0:16, 0:nt], start=True, stop=True
                                         ).then_inc(pe_steps, pe_.step(f"spread{x}{c}"))
                elif what == "near scores":
                    b, = arg
                    qt, c = divmod(b, KC)
                    if b < KC:
                        pe.wait_ge(dve_steps, dve_.at(f"normedk{c}"))
                    if b == 0:
                        pe.wait_ge(act_steps, act_.at(f"empty{END_JOBS[('nv', 3, 1)]}"))
                    if b >= 2:
                        pe.wait_ge(dve_steps, dve_.at(f"near masked{b - 2}"))
                    for e in range(2):
                        r = slice(64 * e, 64 * e + 64)
                        last = nc.tensor.matmul(near_banks(b)[:, e, :], q_n[r, c, qt * P:qt * P + P], k_n[r, c, :],
                                                start=True, stop=True)
                    last.then_inc(pe_steps, pe_.step(f"near scores{b}"))
                elif what == "near turn":
                    b, = arg
                    pe.wait_ge(dve_steps, dve_.at(f"near probs{b}"))
                    for hf in range(2):
                        if b:
                            pe.wait_ge(act_steps, act_.at(f"near turned{b - 1} {hf}"))
                        for kt in range(2):
                            for e in range(2):
                                dst = bank_t[:, 2 * kt + e, :] if hf == 0 else lanes(bank_m)[:, 2 * kt + e, :]
                                t0 = (2 * hf + kt) * P
                                last = nc.tensor.transpose(dst, near_p[b % 3][:, e, t0:t0 + P], ident[:, :])
                        last.then_inc(pe_steps, pe_.step(f"near turn{b} {hf}"))
                elif what == "near values":
                    b, = arg
                    qt, c = divmod(b, KC)
                    pe.wait_ge(act_steps, act_.at(f"near turned{b} 1"))
                    if b >= 2:
                        pe.wait_ge(dve_steps, dve_.at(f"near lo{b - 2}"))
                    ob = bank_o if b % 2 == 0 else bank_g[0]
                    for e in range(2):
                        for kt in range(4):
                            hh = 2 * c + e
                            last = nc.tensor.matmul(ob[64 * e:64 * e + 64, 0:P], v_n[:, kt, hh * HD:hh * HD + HD],
                                                    near_pt[:, b % 2, kt, e, :], start=kt == 0, stop=kt == 3)
                    last.then_inc(pe_steps, pe_.step(f"near values{b}"))
                elif what == "finish":
                    pe.wait_ge(dve_steps, dve_.at(f"empty{len(END_JOBS) - 1}"))
                    for b in range(4):
                        t, c4 = divmod(b, 2)
                        for n in range(4):
                            dst = [bank_s[:, 0:2, :], bank_s[:, 2:4, :]][b] if b < 2 else None
                            dst = dst.rearrange("p a (b n) -> p (a b) n", b=2) if b < 2 else (
                                lanes(bank_o) if b == 2 else bank_t)
                            last = nc.tensor.transpose(dst[:, n, :], x_t[:, 4 * c4 + n, t * P:t * P + P], ident[:, :])
                        last.then_inc(pe_steps, pe_.step(f"finish{b}"))

        @block.scalar
        def _(act):
            enter("start")
            act.sem_inc(act_steps, act_.total("layer") or 1)
            act.dma_start(rope[:, :, :], ins["rope"]).then_inc(consts_loaded, 16)
            act.dma_start(causal[:, :, :], ins["causal"]).then_inc(consts_loaded, 16)
            act.dma_start(upto[:, :, :], ins["upto"]).then_inc(consts_loaded, 16)
            act.dma_start(pick[:, :], ins["pick"]).then_inc(consts_loaded, 16)
            act.dma_start(add_parts[0:4, :], ins["add_parts"]).then_inc(consts_loaded, 16)
            act.dma_start(fbias[:, :, :].rearrange("p l h -> p (l h)"),
                         ins["forget_bias"].rearrange("(o l) h -> o (l h)", o=1).to_broadcast([P, DEPTH * 8])
                         ).then_inc(consts_loaded, 16)
            for b in range(4):
                act.wait_ge(pe_steps, pe_.at(f"x turned{b}"))
                src = [bank_s[:, 0:2, :], bank_s[:, 2:4, :], bank_o[:, :].rearrange("p (j t) -> p j t", j=2),
                       bank_m[:, :].rearrange("p (j t) -> p j t", j=2)][b]
                nc.scalar.activation(x_t[:, 2 * b:2 * b + 2, :], src, ACT.Copy).then_inc(act_steps, act_.step("x"))
            act.wait_ge(act_steps, act_.last())

            def squares(i):
                nc.scalar.activation(qk[1][:, 2 * i:2 * i + 2, :], x_t[:, 2 * i:2 * i + 2, :], ACT.Square
                                     ).then_inc(act_steps, act_.step(f"squares{i}"))

            for i in range(4):
                squares(i)
            act.wait_ge(pe_steps, pe_.at("vec turned"))
            nc.scalar.activation(vec[:, :].rearrange("p (a b) -> p a b", a=3), bank_t[:, 0:3, :], ACT.Copy
                                 ).then_inc(act_steps, act_.step("vec"))
            act.wait_ge(act_steps, act_.last())
            cc = vec[:, ROWS["c"]:ROWS["c"] + 16].rearrange("p (s c) -> p s c", s=2)
            nc.scalar.activation(s_f[:, :, :], cc, ACT.Tanh, scale=0.5).then_inc(act_steps, act_.step("s tanh"))
            act.wait_ge(dve_steps, dve_.at("s"))
            for s in range(2):
                nc.scalar.activation(s_parts[:, :, s], s_f[:, s, :], ACT.Copy, scale=0.5
                                     ).then_inc(act_steps, act_.step("s hi"))
            with act.Fori(0, DEPTH) as layer:
                enter("layer", layer)

                def high(u):
                    act.wait_ge(raw_loaded[u % SLOTS], loaded(u, layer))
                    act.wait_ge(pe_steps, pe_.at(f"unit{(u - SLOTS) % len(UNITS)}", before=u < SLOTS))
                    nc.scalar.activation(w_hi[:, u % SLOTS, :], raw[:, u % SLOTS, :], ACT.Copy
                                         ).then_inc(act_steps, act_.step(f"hi{u}"))

                u = 0
                for what, *arg in ORDER:
                    if what == "unit":
                        kind, i = arg
                        if u + AHEAD < len(UNITS):
                            high(u + AHEAD)
                        for j in range(2 if kind == "branch" else 1):
                            k = JOBS[(kind, i, j)]
                            gb = bank_g[k % BANKS][:, :].rearrange("p (m t) -> p m t", m=2)
                            if kind == "qi":
                                dst = qk[1][:, 2 * i:2 * i + 2, :]
                            elif kind[0] == "q" or kind[0] == "k":
                                c = (0 if kind[0] == "q" else 4) + 2 * i
                                dst = qk[SETS[kind[1]]][:, c:c + 2, :]
                            elif kind[0] == "v":
                                dst = v[SETS[kind[1]]][:, :, i * 256:i * 256 + 256]
                            elif kind == "gate":
                                if i == 0:
                                    act.wait_ge(dve_steps, dve_.at("rope kb"))
                                if i >= 2:
                                    act.wait_ge(dve_steps, dve_.at(f"empty{JOBS[('branch', (i - 2) // 2, i % 2)]}"))
                                dst = gates[:, i % 2, :, :]
                            elif kind[0] == "g":
                                if kind == "gc" and i == 0:
                                    act.wait_ge(dve_steps, dve_.at("gated7"))
                                dst = g[SETS[kind[1]]][:, 2 * i:2 * i + 2, :]
                            elif kind == "ada":
                                act.wait_ge(pe_steps, pe_.at(f"job{k}"))
                                if i >= 2:
                                    act.wait_ge(pe_steps, pe_.at(f"ada turn{i - 2}"))
                                nc.scalar.activation(ada_row[0:4, i % 2, :], bank_g[k % BANKS][0:4, 0:256], ACT.Copy
                                                     ).then_inc(act_steps, act_.step(f"empty{k}", f"ada row{i}"))
                                continue
                            else:
                                continue
                            act.wait_ge(pe_steps, pe_.at(f"job{k}"))
                            if kind[0] == "g":
                                nc.scalar.activation(dst, gb, ACT.Tanh, scale=0.5).then_inc(
                                    act_steps, act_.step(f"tanh{k}", f"empty{k}"))
                            else:
                                nc.scalar.activation(dst, gb, ACT.Copy).then_inc(act_steps, act_.step(f"empty{k}"))
                        u += 1
                    elif what == "squares":
                        i, = arg
                        act.wait_ge(dve_steps, dve_.at(f"empty{JOBS[('out', i, 0)]}"))
                        squares(i)
                    elif what == "norm":
                        act.wait_ge(pe_steps, pe_.at("sumsq"))
                        nc.scalar.activation(token_root1[:, :], bank_m[:, SUM_COL:SUM_COL + 2], ACT.Sqrt,
                                             scale=1.0 / D, bias=eps[:, 0:1]).then_inc(act_steps, act_.step("root"))
                        for half in range(2):
                            c = slice(4 * half, 4 * half + 4)
                            act.wait_ge(dve_steps, dve_.at(f"h{4 * half + 3}"))
                            nc.scalar.activation(h_hi[:, c, :], h[:, c, :], ACT.Copy
                                                 ).then_inc(act_steps, act_.step(f"h hi{half}"))
                        for n in range(AHEAD):
                            high(n)
                    elif what == "small":
                        act.wait_ge(pe_steps, pe_.at("small"))
                        nc.scalar.activation(ki[:, :], bank_m[:, 0:SEQ], ACT.Copy
                                             ).then_inc(act_steps, act_.step("ki"))
                        act.wait_ge(dve_steps, dve_.at("f abs"))
                        nc.scalar.activation(f_log[:, :, :], f_abs[:, :, :], ACT.Exp, scale=-1.0
                                             ).then_inc(act_steps, act_.step("f exp"))
                        act.wait_ge(act_steps, act_.last())
                        nc.scalar.activation(f_log[:, :, :], f_log[:, :, :], ACT.Ln, bias=ones[:, 0:1]
                                             ).then_inc(act_steps, act_.step("f log"))
                    elif what == "csum":
                        act.wait_ge(pe_steps, pe_.at("csum"))
                        nc.scalar.activation(csum_t[:, :], bank_m[:, 0:SEQ], ACT.Copy
                                             ).then_inc(act_steps, act_.step("csum t"))
                        nc.scalar.activation(csum_q[:, :, :], bank_o[:, 32:48].rearrange("p (a b) -> p a b", a=2),
                                             ACT.Copy).then_inc(act_steps, act_.step("csum"))
                    elif what == "scores":
                        k, = arg
                        x, qt, hg = BATCHES[k]
                        nk = P * (qt + 1)
                        pb = probs[k % 2]
                        if x == "i":
                            act.wait_ge(pe_steps, pe_.at(f"scores{k}"))
                            if k >= 2:
                                act.wait_ge(dve_steps, dve_.at(f"index{k - 2}"))
                            nc.scalar.activation(pb[:, :, 0:nk], bank_s[:, :, 0:nk], ACT.Relu
                                                 ).then_inc(act_steps, act_.step(f"relu{k}"))
                        else:
                            act.wait_ge(dve_steps, dve_.at(f"negmax{k}"))
                            for s in range(4):
                                last = nc.scalar.activation(pb[:, s, 0:nk], pb[:, s, 0:nk], ACT.Exp,
                                                            bias=negmax[:, k % 2, s:s + 1],
                                                            accum_out=rowsum[:, k % 2, s:s + 1])
                                last.then_inc(act_steps, act_.step(f"exp{k}"))
                    elif what == "turn":
                        k, kt = arg
                        act.wait_ge(pe_steps, pe_.at(f"turn{k} {kt}"))
                        nc.scalar.activation(probs_t[:, kt, :, :], bank_t[:, :, :], ACT.Copy
                                             ).then_inc(act_steps, act_.step(f"turned{k} {kt}"))
                    elif what == "values":
                        k, = arg
                        x, qt, hg = BATCHES[k]
                        c = 4 * "abc".index(x) + 2 * hg
                        act.wait_ge(dve_steps, dve_.at(f"gated{k}"))
                        nc.scalar.activation(o_hi[:, c:c + 2, qt * P:qt * P + P], o_gated[:, k % 2, :, :], ACT.Copy
                                             ).then_inc(act_steps, act_.step(f"o hi{k}"))
                    elif what == "merged":
                        act.wait_ge(pe_steps, pe_.at(f"job{JOBS[('gate', 11, 0)]}"))
                        for half in range(2):
                            c = slice(4 * half, 4 * half + 4)
                            act.wait_ge(dve_steps, dve_.at(f"empty{JOBS[('branch', 4 + half, 1)]}"))
                            nc.scalar.activation(h_hi[:, c, :], h[:, c, :], ACT.Copy, scale=0.5
                                                 ).then_inc(act_steps, act_.step(f"merged hi{half}"))
            enter("end")
            act.wait_ge(dve_steps, dve_.at("mod"))

            def high(u):
                n = size(END_UNITS[u][0])
                act.wait_ge(raw_loaded[u % SLOTS], end_value[u])
                act.wait_ge(pe_steps, pe_.at(f"unit{len(UNITS) - SLOTS + u if u < SLOTS else u - SLOTS}",
                                             before=u < SLOTS))
                nc.scalar.activation(w_hi[:, u % SLOTS, 0:n], raw[:, u % SLOTS, 0:n], ACT.Copy
                                     ).then_inc(act_steps, act_.step(f"hi{u}"))

            act.wait_ge(pe_steps, pe_.at("sumsq"))
            act.dma_start(dft_c[:, :], ins["dft_c"]).then_inc(end_loaded, 16)
            act.dma_start(dft_t[:, :, :, :], ins["dft_t"]).then_inc(end_loaded, 16)
            act.dma_start(w_s[:, :, :], ins["w_s"].rearrange("g p q -> p g q")).then_inc(end_loaded, 16)
            act.dma_start(b_s[0:1, :, :], ins["b_s"].rearrange("(o g) p -> o g p", o=1)).then_inc(end_loaded, 16)

            def load_bias(n):
                qt, h4 = divmod(n, 4)
                for r in range(2):
                    src = bass.AP(ins["rpb"].tensor, ((2 * qt + r) * 16 + 4 * h4) * 4 * 31, [[1, 64], [31, 16], [1, 64]])
                    act.dma_start(bias[n % 3][64 * r:64 * r + 64, :, :].rearrange("p h (i k) -> p (h i) k", i=4),
                                  src).then_inc(bias_loaded[n % 3], 16)

            def silu(ly, i):
                act.wait_ge(dve_steps, dve_.at(f"conv{ly} {i}"))
                n = SEQ * streams(f"up{ly}")
                nc.scalar.activation(conv[:, i % 2, 0:n], conv[:, i % 2, 0:n], ACT.Silu
                                     ).then_inc(act_steps, act_.step(f"silu{ly} {i}"))

            def hidden_high(ly, i):
                act.wait_ge(dve_steps, dve_.at(f"hidden{ly} {i}"))
                if i == FC // 2:
                    act.wait_ge(pe_steps, pe_.at(f"job{END_JOBS[(f'down{ly}', KC - 1, 0)]}"))
                n = SEQ * streams(f"up{ly}")
                nc.scalar.activation(f_hi[:, i % (FC // 2), 0:n], hidden[:, i % 2, 0:n], ACT.Copy
                                     ).then_inc(act_steps, act_.step(f"f hi{ly} {i}"))

            u = 0
            for what, *arg in END:
                if what == "unit":
                    kind, i = arg
                    up = kind[:2] == "up"
                    if up:
                        ly = int(kind[2])
                        n_s = streams(kind)
                        first = i % (FC // 2) == 0
                        if not first:
                            silu(ly, i - 1)
                    if u + AHEAD < len(END_UNITS):
                        high(u + AHEAD)
                    if up:
                        k = END_JOBS[(kind, i, 0)]
                        act.wait_ge(pe_steps, pe_.at(f"job{k}"))
                        if i >= 2:
                            act.wait_ge(dve_steps, dve_.at(f"hidden{ly} {i - 2}"))
                        act.wait_ge(act_steps, act_.last())
                        nc.scalar.activation(conv[:, i % 2, 0:n_s * SEQ], bank_g[k % BANKS][:, 0:n_s * SEQ],
                                             ACT.Identity, scale=conv_col(ly, 1, i), bias=conv_col(ly, 3, i)
                                             ).then_inc(act_steps, act_.step(f"conv{ly} {i}"))
                        if not first:
                            hidden_high(ly, i - 1)
                    for j in range(end_jobs(kind)):
                        k = END_JOBS[(kind, i, j)]
                        if end_evacuator(kind, j) != "act":
                            continue
                        act.wait_ge(pe_steps, pe_.at(f"job{k}"))
                        gb = bank_g[k % BANKS]
                        fn = ACT.Copy
                        src = gb[:, :]
                        if kind == "f":
                            if i == 0 and j == 0:
                                act.wait_ge(dve_steps, dve_.at("h2 lo00 7"))
                            dst = f_t[:, 2 * i + j, :]
                        elif kind == "u":
                            dst, fn = u_t[:, 2 * i + j, :], ACT.Gelu_apprx_tanh
                        elif kind == "vs":
                            fn = ACT.Gelu_apprx_tanh
                            src = gb.rearrange("p (t n) -> p t n", t=2)
                            dst = v_s[:, 2 * j:2 * j + 2, i * 256:i * 256 + 256]
                        elif kind == "nq":
                            src = gb.rearrange("p (m t) -> p m t", m=2)
                            dst = q_n[:, 2 * i:2 * i + 2, :]
                        elif kind == "nk":
                            if i == 0 and j == 0:
                                act.wait_ge(dve_steps, dve_.at("h2 lo10 7"))
                            dst = k_n[:, 2 * i + j, :]
                        else:
                            src = gb.rearrange("p (t n) -> p t n", t=2)
                            dst = v_n[:, 2 * j:2 * j + 2, i * 256:i * 256 + 256]
                        nc.scalar.activation(dst, src, fn).then_inc(act_steps, act_.step(f"empty{k}"))
                    u += 1
                elif what == "flush":
                    ly, grp = arg
                    silu(ly, grp * (FC // 2) + FC // 2 - 1)
                    hidden_high(ly, grp * (FC // 2) + FC // 2 - 1)
                elif what == "ctx":
                    for b in range(4):
                        act.wait_ge(pe_steps, pe_.at(f"ctx turned{b}"))
                        src = [bank_s[:, 0:2, :], bank_s[:, 2:4, :], bank_o[:, :].rearrange("p (j t) -> p j t", j=2),
                               bank_t[:, :, :].rearrange("p (j t) n -> p j (t n)", j=2)][b]
                        nc.scalar.activation(c_t[:, 2 * b:2 * b + 2, :], src, ACT.Copy
                                             ).then_inc(act_steps, act_.step(f"ctx{b}"))
                elif what == "squares":
                    tag, c = arg
                    kind, per = {"01": ("eo", 2), "10": ("down0", 1), "11": ("wo", 2)}.get(tag, (None, 1))
                    if kind:
                        i = c // per + (KC if kind == "down0" else 0)
                        job = END_JOBS[(kind, i, c % 2 if kind == "eo" else 0)]
                        act.wait_ge(dve_steps, dve_.at(f"empty{job}"))
                    elif tag == "00":
                        act.wait_ge(dve_steps, dve_.at(f"x normed{c}"))
                    if c == 0 and not kind:
                        act.wait_ge(act_steps, act_.last())
                    for s_ in range(norm_tiles(tag) // 2):
                        nc.scalar.activation(h2[:, c, s_ * SEQ:s_ * SEQ + SEQ], x_streams[s_][:, c, :], ACT.Square
                                             ).then_inc(act_steps, act_.step(f"squares{tag} {c}"))
                elif what in ("final norm", "mod norm"):
                    tag = "f" if what == "final norm" else f"{arg[0]}{arg[1]}"
                    tiles = norm_tiles(tag)
                    if tag == "00":
                        high(0)
                    col = SUM_COL if tag == "f" else 0
                    act.wait_ge(pe_steps, pe_.at("sumsq" if tag == "f" else f"sumsq{tag}"))
                    nc.scalar.activation(token_root[:, 0:tiles], bank_m[:, col:col + tiles], ACT.Sqrt, scale=1.0 / D,
                                         bias=eps[:, 0:1]).then_inc(act_steps, act_.step(f"root{tag}"))
                    if tag == "f":
                        continue
                    if tag == "00":
                        high(1)
                    ly, w = arg
                    for c in range(KC):
                        if c == 1:
                            act.wait_ge(dve_steps, dve_.at(f"normed{tag} 1"))
                            nc.scalar.activation(m_rstd[:, 0:tiles * P].rearrange("p (a t) -> p a t", a=tiles),
                                                 bank_t[:, 0:tiles, :], ACT.Copy).then_inc(act_steps,
                                                                                           act_.step(f"rstd{tag}"))
                        if c < 2:
                            act.wait_ge(dve_steps, dve_.at(f"normed{tag} {c}"))
                        else:
                            act.wait_ge(pool_steps, pool_.at(f"normed{tag} {c}"))
                        for s_ in range(tiles // 2):
                            t = slice(s_ * SEQ, s_ * SEQ + SEQ)
                            nc.scalar.activation(h2[:, c, t], h2[:, c, t], ACT.Identity,
                                                 scale=m_gain[:, c, s_:s_ + 1],
                                                 bias=mod[:, ly, mod_col(3 * w) + c, s_:s_ + 1]
                                                 ).then_inc(act_steps, act_.step(f"h2{tag} {c}"))
                elif what == "sgu weights":
                    act.wait_ge(pe_steps, pe_.at("sgu weights"))
                    nc.scalar.activation(w_s_t[:, :, :], bank_t[:, :, :], ACT.Copy
                                         ).then_inc(act_steps, act_.step("sgu weights"))
                elif what == "dft feature":
                    g_, = arg
                    act.wait_ge(pe_steps, pe_.at(f"dft feature{g_}"))
                    nc.scalar.activation(dft_f[g_ % 2][:, :, :], bank_s[:, :, :], ACT.Copy
                                         ).then_inc(act_steps, act_.step(f"dft feature{g_}"))
                elif what == "dft time":
                    g_, = arg
                    act.wait_ge(pe_steps, pe_.at(f"dft time{g_}"))
                    nc.scalar.activation(f_hi[:, g_, :], bank_t[:, :, :].rearrange("p a b -> p (a b)"), ACT.Copy
                                         ).then_inc(act_steps, act_.step(f"a hi{g_}"))
                elif what == "v norm":
                    act.wait_ge(dve_steps, dve_.at("v sum"))
                    nc.scalar.activation(v_inv[:, :], v_sum[:, :], ACT.Sqrt, scale=1.0 / P, bias=eps[:, 0:1]
                                         ).then_inc(act_steps, act_.step("v root"))
                elif what == "sgu":
                    g_, = arg
                    act.wait_ge(dve_steps, dve_.at(f"gated b{g_}"))
                    nc.scalar.activation(f_hi[:, 4 + g_, :], gated_b[:, g_ % 2, :], ACT.Copy
                                         ).then_inc(act_steps, act_.step(f"b hi{g_}"))
                elif what == "qk squares":
                    x, half = arg
                    if (x, half) == ("q", 0):
                        act.dma_start(head_sum[:, :, :], ins["head_sum"]).then_inc(odd_loaded, 16)
                        act.dma_start(head_spread[0:16, :, :], ins["head_spread"]).then_inc(odd_loaded, 16)
                        act.dma_start(window[:, :], ins["window"]).then_inc(odd_loaded, 16)
                        for n in range(2):
                            load_bias(n)
                    if x == "q":
                        src = q_n[:, 4 * half:4 * half + 4, :]
                        dst = qk_sq[:, 2 * half:2 * half + 2, :].rearrange("p a (b t) -> p (a b) t", b=2)
                    else:
                        act.wait_ge(pe_steps, pe_.at("sumsqk0" if half else "sumsqq1"))
                        src, dst = k_n[:, 4 * half:4 * half + 4, :], qk_sq[:, :, :]
                    act.wait_ge(act_steps, act_.last())
                    nc.scalar.activation(dst, src, ACT.Square).then_inc(act_steps, act_.step(f"squares{x}{half}"))
                elif what == "qk sum":
                    x, half = arg
                    if half:
                        nt = SEQ if x == "q" else 512
                        act.wait_ge(pe_steps, pe_.at(f"sumsq{x}1"))
                        nc.scalar.activation(m_root[0:16, 0:nt], bank_m[0:16, 0:nt], ACT.Sqrt, scale=1.0 / HD,
                                             bias=eps[0:16, 0:1]).then_inc(act_steps, act_.step(f"root{x}"))
                elif what == "qk spread":
                    x, = arg
                    if x == "k":
                        act.wait_ge(pe_steps, pe_.at(f"job{END_JOBS[('nv', 3, 1)]}"))
                        load_bias(2)
                elif what == "near exp":
                    b, = arg
                    if b >= 2 and b % 2 == 0 and b // 2 + 2 < 8:
                        act.wait_ge(dve_steps, dve_.at(f"near masked{b - 1}"))
                        load_bias(b // 2 + 2)
                    act.wait_ge(dve_steps, dve_.at(f"near max{b}"))
                    for e in range(2):
                        nc.scalar.activation(near_p[b % 3][:, e, :], near_p[b % 3][:, e, :], ACT.Exp,
                                             bias=near_max[:, b % 2, e:e + 1], accum_out=near_sum[:, b % 2, e:e + 1]
                                             ).then_inc(act_steps, act_.step(f"near exp{b}"))
                elif what == "near turn":
                    b, = arg
                    for hf in range(2):
                        act.wait_ge(pe_steps, pe_.at(f"near turn{b} {hf}"))
                        src = bank_t[:, :, :] if hf == 0 else bank_m[:, :].rearrange("p (a b) -> p a b", a=4)
                        nc.scalar.activation(near_pt[:, b % 2, 2 * hf:2 * hf + 2, :, :].rearrange(
                            "p k e q -> p (k e) q"), src, ACT.Copy).then_inc(act_steps,
                                                                             act_.step(f"near turned{b} {hf}"))
                elif what == "near values":
                    b, = arg
                    qt, c = divmod(b, KC)
                    act.wait_ge(pe_steps, pe_.at(f"near values{b}"))
                    ob = bank_o if b % 2 == 0 else bank_g[0]
                    nc.scalar.activation(
                        f_hi[:, 0:4, :].rearrange("p a (b t) -> p (a b) t", b=2)[:, c, qt * P:qt * P + P],
                        ob[:, 0:P], ACT.Copy).then_inc(act_steps, act_.step(f"near hi{b}"))
                elif what == "finish":
                    for b in range(4):
                        t, c4 = divmod(b, 2)
                        act.wait_ge(pe_steps, pe_.at(f"finish{b}"))
                        src = bank_s[:, 2 * b:2 * b + 2, :].rearrange("p a b -> p (a b)") if b < 2 else (
                            bank_o[:, :] if b == 2 else bank_t[:, :, :].rearrange("p a b -> p (a b)"))
                        nc.scalar.activation(out_sb[:, t, 512 * c4:512 * c4 + 512], src, ACT.Copy
                                             ).then_inc(act_steps, act_.step("out", "out1"))

        @block.gpsimd
        def _(pool):
            enter("start")
            pool.sem_inc(pool_steps, pool_.total("layer") or 1)
            nc.gpsimd.memset(eps[:, :], EPS).then_inc(pool_steps, pool_.step("eps"))
            nc.gpsimd.memset(ones[:, :], 1.0).then_inc(pool_steps, pool_.step("ones"))
            nc.gpsimd.memset(logf[:, :, :], 0.0).then_inc(pool_steps, pool_.step("logf"))
            pool.wait_ge(consts_loaded, 16 * CONSTS)
            with pool.Fori(0, DEPTH) as layer:
                enter("layer", layer)
                before = "rope kb"
                u = 0
                for what, *arg in ORDER:
                    if what == "unit":
                        n = u + AHEAD
                        u += 1
                        if n < len(UNITS) and UNITS[n][0] == "ada":
                            pool.wait_ge(act_steps, act_.at(f"hi{n}"))
                            nc.gpsimd.tensor_tensor(w_lo[:, n % SLOTS, :], raw[:, n % SLOTS, :],
                                                    w_hi[:, n % SLOTS, :].bitcast(F32), ALU.subtract
                                                    ).then_inc(pool_steps, pool_.step(f"lo{n}"))
                    if what != "rope":
                        continue
                    x, = arg
                    src = ki[:, :].rearrange("p (o t) -> p o t", o=1) if x == "ki" else (
                        qk[1][:, 0:4, :] if x == "qi" else
                        qk[SETS[x[1]]][:, 0:4, :] if x[0] == "q" else qk[SETS[x[1]]][:, 4:8, :])
                    n = 1 if x == "ki" else 4
                    if x == "ki":
                        pool.wait_ge(act_steps, act_.at("ki"))
                    else:
                        pool.wait_ge(act_steps, act_.at(f"empty{JOBS[(x, 1, 0)]}"))
                    pool.wait_ge(dve_steps, dve_.at(before, before=x == "ki"))
                    nc.gpsimd.tensor_tensor(scaled[:, 0:n, :], src, rope[:, 0:1, :].to_broadcast([P, n, SEQ]), ALU.mult
                                            ).then_inc(pool_steps, pool_.step("cos " + x))
                    before = "rope " + x
            enter("end")
            for what, *arg in END:
                if what == "near scores" and arg[0] % 2 == 0:
                    n = arg[0] // 2
                    pool.wait_ge(bias_loaded[n % 3], 32 * (n // 3 + 1))
                    pool.wait_ge(odd_loaded, 16 * 3)
                    nc.gpsimd.tensor_tensor(
                        bias[n % 3][:, :, :], bias[n % 3][:, :, :],
                        window[:, :].rearrange("p (o k) -> p o k", o=1).to_broadcast([P, 4, SEQ]), ALU.add
                    ).then_inc(pool_steps, pool_.step(f"windowed{n}"))
                if what != "mod norm":
                    continue
                tag = f"{arg[0]}{arg[1]}"
                n_s = norm_tiles(tag) // 2
                pool.wait_ge(act_steps, act_.at(f"rstd{tag}"))
                for c in range(2, KC):
                    for s_ in range(n_s):
                        t = slice(s_ * SEQ, s_ * SEQ + SEQ)
                        nc.gpsimd.tensor_tensor(h2[:, c, t], x_streams[s_][:, c, :], m_rstd[:, t], ALU.mult
                                                ).then_inc(pool_steps, pool_.step(f"normed{tag} {c}"))

        @block.vector
        def _(dve):
            enter("start")
            dve.sem_inc(dve_steps, dve_.total("layer") or 1)
            own = lambda: dve.wait_ge(dve_steps, dve_.last())
            plain = lambda: dve.sem_inc(dve_passed, 1)
            def add_squares(i):
                own()
                nc.vector.tensor_tensor(qk[1][:, 0:2, :], qk[1][:, 0:2, :], qk[1][:, 2 * i:2 * i + 2, :], ALU.add
                                        ).then_inc(dve_steps, dve_.step(f"added{i}"))

            dve.wait_ge(act_steps, act_.at("squares3"))
            add_squares(1)
            add_squares(2)
            add_squares(3)
            dve.wait_ge(act_steps, act_.at("s tanh"))
            cc = vec[:, ROWS["c"]:ROWS["c"] + 16].rearrange("p (s c) -> p s c", s=2)
            nc.vector.scalar_tensor_tensor(s_f[:, :, :], s_f[:, :, :], 1.0, cc, ALU.add, ALU.mult
                                           ).then_inc(dve_steps, dve_.step("s"))
            own()
            dve.wait_ge(act_steps, act_.at("s hi"))
            for s in range(2):
                nc.vector.scalar_tensor_tensor(s_parts[:, :, 2 + s], s_f[:, s, :], 0.5,
                                               s_parts[:, :, s].bitcast(F32), ALU.mult, ALU.subtract
                                               ).then_inc(dve_steps, dve_.step("s split"))
            dve.wait_ge(pool_steps, pool_.at("logf"))
            dve.wait_ge(consts_loaded, 16 * CONSTS)

            with dve.Fori(0, DEPTH) as layer:
                enter("layer", layer)

                def low(u):
                    if UNITS[u][0] == "ada":
                        return
                    dve.wait_ge(act_steps, act_.at(f"hi{u}"))
                    nc.vector.tensor_tensor(w_lo[:, u % SLOTS, :], raw[:, u % SLOTS, :],
                                            w_hi[:, u % SLOTS, :].bitcast(F32), ALU.subtract
                                            ).then_inc(dve_steps, dve_.step(f"lo{u}"))

                own()
                nc.vector.tensor_copy(gain[:, :], vec[:, bass.ds(layer * KC + ROWS["norm_gain"], KC)]
                                      ).then_inc(dve_steps, dve_.step("gain"))
                nc.vector.tensor_copy(ada_bias[:, :], vec[:, bass.ds(layer * 48 + ROWS["ada_b"], 48)]
                                      ).then_inc(dve_steps, dve_.step("ada bias"))
                nc.vector.tensor_copy(fbias_now[:, :], fbias[:, bass.ds(layer, 1), :]
                                      ).then_inc(dve_steps, dve_.step("fbias"))
                def normalize(k):
                    nk = P * (BATCHES[k][1] + 1)
                    dve.wait_ge(act_steps, act_.at(f"exp{k}"))
                    own()
                    nc.vector.reciprocal(rowinv[:, :], rowsum[:, k % 2, :]).then_inc(dve_steps, dve_.step("rowinv"))
                    own()
                    pb = probs[k % 2][:, :, 0:nk]
                    nc.vector.tensor_tensor(pb, pb, rowinv[:, :].rearrange("p (s o) -> p s o", o=1).to_broadcast(
                        [P, 4, nk]), ALU.mult).then_inc(dve_steps, dve_.step(f"probs{k}"))

                u = 0
                pending = None
                for what, *arg in ORDER:
                    if what == "unit":
                        kind, i = arg
                        if pending is not None:
                            normalize(pending)
                            pending = None
                        if u + AHEAD < len(UNITS):
                            low(u + AHEAD)
                        for j in range(2 if kind == "branch" else 1):
                            k = JOBS[(kind, i, j)]
                            if evacuator(kind) != "dve":
                                continue
                            gb = bank_g[k % BANKS][:, :].rearrange("p (m t) -> p m t", m=2)
                            dve.wait_ge(pe_steps, pe_.at(f"job{k}"))
                            if kind == "branch":
                                n, half = divmod(i, 2)
                                gt = gates[:, j, :, :]
                                dve.wait_ge(act_steps, act_.at(f"empty{JOBS[('gate', 2 * i + j, 0)]}"))
                                c = 4 * half + 2 * j
                                own()
                                dst = branch_y[:, :, :] if n else h[:, c:c + 2, :]
                                nc.vector.scalar_tensor_tensor(dst, gt, 1.0, gb, ALU.add, ALU.mult).then_inc(
                                    dve_steps, dve_.step("y", *([] if n else [f"empty{k}"])))
                                if n:
                                    own()
                                    nc.vector.tensor_tensor(h[:, c:c + 2, :], h[:, c:c + 2, :], branch_y[:, :, :],
                                                            ALU.add).then_inc(dve_steps, dve_.step(f"empty{k}"))
                            elif kind == "out":
                                own()
                                nc.vector.tensor_tensor(x_t[:, 2 * i:2 * i + 2, :], gb, x_t[:, 2 * i:2 * i + 2, :],
                                                        ALU.add).then_inc(dve_steps, dve_.step(f"empty{k}"))
                            else:
                                gg = g[SETS[kind[1]]][:, 2 * i:2 * i + 2, :]
                                dve.wait_ge(act_steps, act_.at(f"tanh{k}"))
                                nc.vector.scalar_tensor_tensor(gg, gg, 1.0, gb, ALU.add, ALU.mult).then_inc(
                                    dve_steps, dve_.step(f"empty{k}"))
                        u += 1
                    elif what == "sums" and arg[0]:
                        dve.wait_ge(act_steps, act_.at(f"squares{arg[0]}"))
                        add_squares(arg[0])
                    elif what == "norm":
                        dve.wait_ge(act_steps, act_.at("root"))
                        nc.vector.reciprocal(token_rstd1[:, :], token_root1[:, :]).then_inc(
                            dve_steps, dve_.step("token rstd"))
                        dve.wait_ge(pe_steps, pe_.at("spread"))
                        own()
                        for c in range(KC):
                            nc.vector.scalar_tensor_tensor(h[:, c, :], x_t[:, c, :], gain[:, c:c + 1],
                                                           bank_o[:, 0:SEQ], ALU.mult, ALU.mult).then_inc(
                                dve_steps, dve_.step(f"h{c}"))
                        own()
                        for half in range(2):
                            c = slice(4 * half, 4 * half + 4)
                            dve.wait_ge(act_steps, act_.at(f"h hi{half}"))
                            nc.vector.tensor_tensor(h_lo[:, c, :], h[:, c, :], h_hi[:, c, :].bitcast(F32), ALU.subtract
                                                    ).then_inc(dve_steps, dve_.step(f"h lo{half}"))
                        for n in range(AHEAD):
                            low(n)
                    elif what == "small":
                        dve.wait_ge(pe_steps, pe_.at("small"))
                        wf = bank_o[:, 0:32].rearrange("p (t n) -> p t n", t=2)
                        nc.vector.tensor_scalar(w_f[:, :, 0:8], wf[:, :, 0:8], 8 ** -0.5 * 64 ** -0.5, None, ALU.mult
                                                ).then_inc(dve_steps, dve_.step("w idx"))
                        nc.vector.tensor_tensor(w_f[:, :, 8:16], wf[:, :, 8:16],
                                                fbias_now[:, :].rearrange("p (o n) -> p o n", o=1).to_broadcast(
                                                    [P, 2, 8]), ALU.add).then_inc(dve_steps, dve_.step("f"))
                        own()
                        nc.vector.tensor_scalar(f_min[:, :, :], w_f[:, :, 8:16], -1.0, None, ALU.mult
                                                ).then_inc(dve_steps, dve_.step("f neg"))
                        own()
                        nc.vector.tensor_tensor(f_abs[:, :, :], f_min[:, :, :], w_f[:, :, 8:16], ALU.max
                                                ).then_inc(dve_steps, dve_.step("f abs"))
                        own()
                        nc.vector.tensor_scalar(f_min[:, :, :], w_f[:, :, 8:16], 0.0, None, ALU.min
                                                ).then_inc(dve_steps, dve_.step("f min"))
                        dve.wait_ge(act_steps, act_.at("f log"))
                        own()
                        for c in (0, 64):
                            nc.vector.tensor_tensor(logf[:, :, c:c + 8], f_min[:, :, :], f_log[:, :, :], ALU.subtract
                                                    ).then_inc(dve_steps, dve_.step("logf"))
                    elif what == "rope":
                        x, = arg
                        buf = ki[:, :].rearrange("p (o t) -> p o t", o=1) if x == "ki" else (
                            qk[1][:, 0:4, :] if x == "qi" else
                            qk[SETS[x[1]]][:, 0:4, :] if x[0] == "q" else qk[SETS[x[1]]][:, 4:8, :])
                        n = 1 if x == "ki" else 4
                        if x == "ki":
                            dve.wait_ge(act_steps, act_.at("ki"))
                        else:
                            dve.wait_ge(act_steps, act_.at(f"empty{JOBS[(x, 1, 0)]}"))
                        own()
                        plain()
                        nc.vector.stream_shuffle(turned[:, 0:n, :], buf, [(m + 8) % 16 if m < 16 else m for m in range(32)]
                                                 ).then_inc(dve_steps, dve_.step("swap"))
                        own()
                        nc.vector.tensor_tensor(turned[:, 0:n, :], turned[:, 0:n, :],
                                                rope[:, 1:2, :].to_broadcast([P, n, SEQ]), ALU.mult
                                                ).then_inc(dve_steps, dve_.step("sin"))
                        dve.wait_ge(pool_steps, pool_.at("cos " + x))
                        own()
                        nc.vector.tensor_tensor(buf, turned[:, 0:n, :], scaled[:, 0:n, :], ALU.add
                                                ).then_inc(dve_steps, dve_.step("rope " + x))
                    elif what == "scores":
                        k, = arg
                        x, qt, hg = BATCHES[k]
                        nk = P * (qt + 1)
                        pb = probs[k % 2]
                        if x == "i":
                            dve.wait_ge(act_steps, act_.at(f"relu{k}"))
                            for s in range(4):
                                hh = 4 * hg + 2 * (s % 2) + s // 2
                                own()
                                if hg == 0 and s == 0:
                                    nc.vector.tensor_scalar(isc[:, 0:nk], pb[:, s, 0:nk], w_f[:, qt, hh:hh + 1], None,
                                                            ALU.mult).then_inc(dve_steps, dve_.step(f"index{k}"))
                                else:
                                    nc.vector.scalar_tensor_tensor(isc[:, 0:nk], pb[:, s, 0:nk], w_f[:, qt, hh:hh + 1],
                                                                   isc[:, 0:nk], ALU.mult, ALU.add).then_inc(
                                        dve_steps, dve_.step(f"index{k}"))
                            if hg == 1:
                                own()
                                nc.vector.scalar_tensor_tensor(work[:, 0:nk], causal[:, qt, 0:nk], FILL / NEG,
                                                               isc[:, 0:nk], ALU.mult, ALU.add).then_inc(
                                    dve_steps, dve_.step("ranked"))
                        else:
                            dve.wait_ge(pe_steps, pe_.at(f"scores{k}"))
                            own()
                            mask = (picked if x == "b" else causal)[:, qt:qt + 1, 0:nk].to_broadcast([P, 4, nk])
                            nc.vector.scalar_tensor_tensor(pb[:, :, 0:nk], bank_s[:, :, 0:nk], SCALE, mask,
                                                           ALU.mult, ALU.add).then_inc(dve_steps,
                                                                                       dve_.step(f"masked{k}"))
                            own()
                            nm = negmax[:, k % 2, :]
                            if x != "c":
                                nc.vector.tensor_reduce(nm, pb[:, :, 0:nk], AX.X, ALU.max, negate=True).then_inc(
                                    dve_steps, dve_.step(f"negmax{k}"))
                            else:
                                nc.vector.tensor_reduce(nm, pb[:, :, 0:nk], AX.X, ALU.max, negate=True).then_inc(
                                    dve_steps, dve_.step("max"))
                                dve.wait_ge(act_steps, act_.at("csum"))
                                cq = csum_q[:, qt, 4 * hg:4 * hg + 4].rearrange("p (j e) -> p e j", j=2)
                                n2 = nm.rearrange("p (e j) -> p e j", e=2)
                                for op, name in ((ALU.subtract, "max"), (ALU.add, f"negmax{k}")):
                                    own()
                                    nc.vector.tensor_tensor(n2, n2, cq, op).then_inc(dve_steps, dve_.step(name))
                            pending = k
                    elif what == "topk":
                        qt, r = arg
                        nk = P * (qt + 1)
                        for _ in range(TOPK // 8 // 4):
                            own()
                            plain()
                            nc.vector.max(top8[:, :], work[:, 0:nk]).then_inc(dve_steps, dve_.step("top8"))
                            own()
                            plain()
                            nc.vector.match_replace(work[:, 0:nk], top8[:, :], work[:, 0:nk], TAKEN).then_inc(
                                dve_steps, dve_.step("taken"))
                        if r == 3:
                            own()
                            nc.vector.tensor_scalar(work[:, 0:nk], work[:, 0:nk], TAKEN, 1.0, ALU.is_equal,
                                                    ALU.subtract).then_inc(dve_steps, dve_.step("sel"))
                            own()
                            nc.vector.scalar_tensor_tensor(picked[:, qt, 0:nk], work[:, 0:nk], -NEG,
                                                           causal[:, qt, 0:nk], ALU.mult, ALU.add).then_inc(
                                dve_steps, dve_.step("picked"))
                    elif what == "values":
                        k, = arg
                        x, qt, hg = BATCHES[k]
                        t = slice(qt * P, qt * P + P)
                        dve.wait_ge(pe_steps, pe_.at(f"values{k}"))
                        own()
                        nc.vector.scalar_tensor_tensor(
                            o_gated[:, k % 2, :, :], bank_o[:, 0:2 * P].rearrange("p (j t) -> p j t", j=2), 0.5,
                            g[SETS[x]][:, 2 * hg:2 * hg + 2, t], ALU.mult, ALU.mult
                        ).then_inc(dve_steps, dve_.step(f"gated{k}"))
                        own()
                        dve.wait_ge(act_steps, act_.at(f"o hi{k}"))
                        c = 4 * "abc".index(x) + 2 * hg
                        nc.vector.tensor_tensor(o_lo[:, c:c + 2, t], o_gated[:, k % 2, :, :],
                                                o_hi[:, c:c + 2, t].bitcast(F32), ALU.subtract
                                                ).then_inc(dve_steps, dve_.step(f"o lo{k}"))
                    elif what == "ada turn" and arg[0] == 23:
                        dve.wait_ge(pe_steps, pe_.at("ada turn23"))
                        nc.vector.tensor_tensor(
                            mod_now[:, :, :], bank_m[:, ADA_COL:ADA_COL + 96].rearrange("p (m s) -> p m s", s=2),
                            ada_bias[:, :].rearrange("p (m o) -> p m o", o=1).to_broadcast([P, 48, 2]), ALU.add
                        ).then_inc(dve_steps, dve_.step("mod now"))
                    elif what == "merged":
                        for half in range(2):
                            c = slice(4 * half, 4 * half + 4)
                            dve.wait_ge(act_steps, act_.at(f"merged hi{half}"))
                            own()
                            nc.vector.scalar_tensor_tensor(h_lo[:, c, :], h[:, c, :], 0.5, h_hi[:, c, :].bitcast(F32),
                                                           ALU.mult, ALU.subtract).then_inc(
                                dve_steps, dve_.step(f"merged lo{half}"))
                own()
                nc.vector.tensor_copy(mod[:, bass.ds(layer, 1), :, :], mod_now[:, :, :]
                                      ).then_inc(dve_steps, dve_.step("mod"))
            enter("end")

            def low(u):
                n = size(END_UNITS[u][0])
                dve.wait_ge(act_steps, act_.at(f"hi{u}"))
                nc.vector.tensor_tensor(w_lo[:, u % SLOTS, 0:n], raw[:, u % SLOTS, 0:n],
                                        w_hi[:, u % SLOTS, 0:n].bitcast(F32), ALU.subtract
                                        ).then_inc(dve_steps, dve_.step(f"lo{u}"))

            def multiply(ly, i):
                n = SEQ * streams(f"up{ly}")
                job = END_JOBS[(f"up{ly}", i, 1 if ly == 0 else 0)]
                vb = bank_g[job % BANKS][:, 0:512] if ly == 0 else bank_g[job % BANKS][:, SEQ:2 * SEQ]
                dve.wait_ge(act_steps, act_.at(f"silu{ly} {i}"))
                dve.wait_ge(pe_steps, pe_.at(f"job{job}"))
                own()
                nc.vector.tensor_tensor(hidden[:, i % 2, 0:n], conv[:, i % 2, 0:n], vb, ALU.mult).then_inc(
                    dve_steps, dve_.step(f"hidden{ly} {i}", f"empty{job}"))

            def hidden_low(ly, i):
                n = SEQ * streams(f"up{ly}")
                dve.wait_ge(act_steps, act_.at(f"f hi{ly} {i}"))
                nc.vector.tensor_tensor(f_lo[:, i % (FC // 2), 0:n], hidden[:, i % 2, 0:n],
                                        f_hi[:, i % (FC // 2), 0:n].bitcast(F32), ALU.subtract
                                        ).then_inc(dve_steps, dve_.step(f"f lo{ly} {i}"))

            def near_normalize(b):
                dve.wait_ge(act_steps, act_.at(f"near exp{b}"))
                nc.vector.reciprocal(near_inv[:, :], near_sum[:, b % 2, :]).then_inc(dve_steps, dve_.step("near inv"))
                own()
                nc.vector.tensor_tensor(near_p[b % 3][:, :, :], near_p[b % 3][:, :, :],
                                        near_inv[:, :].rearrange("p (e o) -> p e o", o=1).to_broadcast([P, 2, 512]),
                                        ALU.mult).then_inc(dve_steps, dve_.step(f"near probs{b}"))

            u = 0
            for what, *arg in END:
                if what == "unit":
                    kind, i = arg
                    up = kind[:2] == "up"
                    n_s = streams(kind)
                    if up:
                        ly = int(kind[2])
                        first = i % (FC // 2) == 0
                        if not first:
                            multiply(ly, i - 1)
                    if u + AHEAD < len(END_UNITS):
                        low(u + AHEAD)
                    if up:
                        k = END_JOBS[(kind, i, 0)]
                        cv = conv[:, i % 2, 0:n_s * SEQ].rearrange("p (s t) -> p s t", s=n_s)
                        gb = bank_g[k % BANKS][:, 0:n_s * SEQ].rearrange("p (s t) -> p s t", s=n_s)
                        dve.wait_ge(act_steps, act_.at(f"conv{ly} {i}"))
                        for tap, to, of in ((0, slice(1, SEQ), slice(0, SEQ - 1)), (2, slice(0, SEQ - 1), slice(1, SEQ))):
                            own()
                            nc.vector.scalar_tensor_tensor(cv[:, :, to], gb[:, :, of], conv_col(ly, tap, i),
                                                           cv[:, :, to], ALU.mult, ALU.add).then_inc(
                                dve_steps, dve_.step(f"conv{ly} {i}", *([f"empty{k}"] if ly == 0 else [])))
                        if not first:
                            hidden_low(ly, i - 1)
                    for j in range(end_jobs(kind)):
                        k = END_JOBS[(kind, i, j)]
                        if end_evacuator(kind, j) != "dve" or up:
                            continue
                        dve.wait_ge(pe_steps, pe_.at(f"job{k}"))
                        own()
                        gb = bank_g[k % BANKS]
                        ly = 0 if kind in ("eo", "down0") else 1
                        part = mod_col(2 if kind in ("eo", "wo") else 5)
                        if kind in ("eo", "down0"):
                            m = 2 * i + j if kind == "eo" else i % KC
                            todo = [(m, s_, gb[:, s_ * SEQ:s_ * SEQ + SEQ]) for s_ in range(2)]
                        elif kind == "wo":
                            todo = [(2 * i + m, 0, gb[:, m * SEQ:m * SEQ + SEQ]) for m in range(2)]
                        else:
                            todo = [(i % KC, 0, gb[:, 0:SEQ])]
                        for m, s_, src in todo:
                            xs = x_streams[s_][:, m, :]
                            nc.vector.scalar_tensor_tensor(xs, src, mod[:, ly, part + m, s_:s_ + 1], xs,
                                                           ALU.mult, ALU.add).then_inc(dve_steps,
                                                                                       dve_.step(f"empty{k}"))
                    u += 1
                elif what == "flush":
                    ly, grp = arg
                    multiply(ly, grp * (FC // 2) + FC // 2 - 1)
                    hidden_low(ly, grp * (FC // 2) + FC // 2 - 1)
                elif what == "sums":
                    tag, c = arg
                    ly, w = int(tag[0]), int(tag[1])
                    if c == 0:
                        col = ROWS["norm1" if w == 0 else "norm2"] + ly * KC
                        own()
                        nc.vector.scalar_tensor_tensor(
                            m_gain[:, :, :], mod[:, ly, mod_col(3 * w + 1):mod_col(3 * w + 1) + KC, :], 1.0,
                            vec[:, col:col + KC].rearrange("p (c o) -> p c o", o=1).to_broadcast([P, KC, 2]),
                            ALU.add, ALU.mult).then_inc(dve_steps, dve_.step("m gain"))
                    dve.wait_ge(act_steps, act_.at(f"squares{tag} {c}"))
                    if c:
                        own()
                        t = slice(0, norm_tiles(tag) * P)
                        nc.vector.tensor_tensor(h2[:, 0, t], h2[:, 0, t], h2[:, c, t], ALU.add).then_inc(
                            dve_steps, dve_.step(f"added{tag} {c}"))
                elif what in ("final norm", "mod norm"):
                    tag = "f" if what == "final norm" else f"{arg[0]}{arg[1]}"
                    tiles = norm_tiles(tag)
                    dve.wait_ge(act_steps, act_.at(f"root{tag}"))
                    nc.vector.reciprocal(token_rstd[:, 0:tiles], token_root[:, 0:tiles]).then_inc(
                        dve_steps, dve_.step(f"token rstd{tag}"))
                    if tag == "f":
                        dve.wait_ge(pe_steps, pe_.at("spreadf"))
                        for c in range(KC):
                            n = ROWS["final_gain"] + c
                            nc.vector.scalar_tensor_tensor(
                                x_t[:, c, :], x_t[:, c, :], vec[:, n:n + 1],
                                bank_m[:, 0:SEQ], ALU.mult, ALU.mult
                            ).then_inc(dve_steps, dve_.step(f"x normed{c}"))
                        continue
                    if tag == "00":
                        for n in range(AHEAD):
                            low(n)
                    dve.wait_ge(pe_steps, pe_.at(f"spread{tag}"))
                    for c in range(2):
                        for s_ in range(tiles // 2):
                            nc.vector.tensor_tensor(
                                h2[:, c, s_ * SEQ:s_ * SEQ + SEQ], x_streams[s_][:, c, :],
                                bank_t[:, 2 * s_:2 * s_ + 2, :].rearrange("p a t -> p (a t)"), ALU.mult
                            ).then_inc(dve_steps, dve_.step(f"normed{tag} {c}"))
                    for c in range(KC):
                        t = slice(0, tiles * P)
                        dve.wait_ge(act_steps, act_.at(f"h2{tag} {c}"))
                        nc.vector.tensor_copy(h2_hi[:, c, t], h2[:, c, t]).then_inc(dve_steps,
                                                                                    dve_.step(f"h2 hi{tag} {c}"))
                        own()
                        nc.vector.tensor_tensor(h2_lo[:, c, t], h2[:, c, t], h2_hi[:, c, t].bitcast(F32), ALU.subtract
                                                ).then_inc(dve_steps, dve_.step(f"h2 lo{tag} {c}"))
                elif what == "dft time":
                    g_, = arg
                    dve.wait_ge(act_steps, act_.at(f"a hi{g_}"))
                    nc.vector.tensor_tensor(f_lo[:, g_, :], bank_t[:, :, :].rearrange("p a b -> p (a b)"),
                                            f_hi[:, g_, :].bitcast(F32), ALU.subtract
                                            ).then_inc(dve_steps, dve_.step(f"a lo{g_}"))
                elif what == "v norm":
                    dve.wait_ge(act_steps, act_.at(f"empty{END_JOBS[('vs', 1, 1)]}"))
                    nc.vector.tensor_tensor(v_sq[:, :, :], v_s[:, :, :], v_s[:, :, :], ALU.mult).then_inc(
                        dve_steps, dve_.step("v sq"))
                    own()
                    nc.vector.tensor_reduce(v_sum[:, :], v_sq[:, :, :].rearrange("p t (g c) -> p (t g) c", g=4), AX.X,
                                            ALU.add).then_inc(dve_steps, dve_.step("v sum"))
                    dve.wait_ge(act_steps, act_.at("v root"))
                    nc.vector.reciprocal(v_inv[:, :], v_inv[:, :]).then_inc(dve_steps, dve_.step("v inv"))
                    own()
                    vg = v_s[:, :, :].rearrange("p t (g c) -> p (t g) c", g=4)
                    nc.vector.tensor_tensor(vg, vg, v_inv[:, :].rearrange("p (a o) -> p a o", o=1).to_broadcast(
                        [P, 16, P]), ALU.mult).then_inc(dve_steps, dve_.step("v norm"))
                elif what == "sgu":
                    g_, = arg
                    dve.wait_ge(pe_steps, pe_.at(f"sgu{g_}"))
                    own()
                    nc.vector.tensor_tensor(gated_b[:, g_ % 2, :], bank_o[:, :], u_t[:, g_, :], ALU.mult).then_inc(
                        dve_steps, dve_.step(f"gated b{g_}"))
                    dve.wait_ge(act_steps, act_.at(f"b hi{g_}"))
                    own()
                    nc.vector.tensor_tensor(f_lo[:, 4 + g_, :], gated_b[:, g_ % 2, :], f_hi[:, 4 + g_, :].bitcast(F32),
                                            ALU.subtract).then_inc(dve_steps, dve_.step(f"b lo{g_}"))
                elif what == "qk sum":
                    x, half = arg
                    if half:
                        nt = SEQ if x == "q" else 512
                        dve.wait_ge(act_steps, act_.at(f"root{x}"))
                        own()
                        nc.vector.reciprocal(m_rstd[0:16, 0:nt], m_root[0:16, 0:nt]).then_inc(
                            dve_steps, dve_.step(f"rstd{x}"))
                elif what == "qk spread":
                    x, = arg
                    nt = SEQ if x == "q" else 512
                    for c in range(KC):
                        dst = (q_n if x == "q" else k_n)[:, c, :]
                        n = ROWS[x + "_g"]
                        src = (bank_t[:, :, :].rearrange("p a b -> p (a b)") if c % 2 == 0 else bank_o)[:, 0:nt]
                        dve.wait_ge(pe_steps, pe_.at(f"spread{x}{c}"))
                        nc.vector.scalar_tensor_tensor(dst, dst, vec[:, n:n + 1], src, ALU.mult, ALU.mult).then_inc(
                            dve_steps, dve_.step(f"normed{x}{c}"))
                elif what == "near scores":
                    b, = arg
                    qt, c = divmod(b, KC)
                    pb, sbk = near_p[b % 3], near_banks(b)
                    dve.wait_ge(pool_steps, pool_.at(f"windowed{b // 2}"))
                    dve.wait_ge(pe_steps, pe_.at(f"near scores{b}"))
                    bt = bias[b // 2 % 3][:, 2 * (c % 2):2 * (c % 2) + 2, :]
                    nc.vector.scalar_tensor_tensor(pb[:, :, 0:SEQ], sbk[:, :, 0:SEQ], SCALE, backwards(bt),
                                                   ALU.mult, ALU.add).then_inc(dve_steps, dve_.step("near"))
                    nc.vector.tensor_scalar(pb[:, :, SEQ:512], sbk[:, :, SEQ:512], SCALE, None, ALU.mult).then_inc(
                        dve_steps, dve_.step(f"near masked{b}"))
                    if b:
                        near_normalize(b - 1)
                    own()
                    nc.vector.tensor_reduce(near_max[:, b % 2, :], pb[:, :, :], AX.X, ALU.max, negate=True).then_inc(
                        dve_steps, dve_.step(f"near max{b}"))
                    if b == 15:
                        near_normalize(b)
                elif what == "near values":
                    b, = arg
                    qt, c = divmod(b, KC)
                    ob = bank_o if b % 2 == 0 else bank_g[0]
                    v8 = lambda t: t[:, 0:4, :].rearrange("p a (b t) -> p (a b) t", b=2)[:, c, qt * P:qt * P + P]
                    dve.wait_ge(act_steps, act_.at(f"near hi{b}"))
                    nc.vector.tensor_tensor(v8(f_lo), ob[:, 0:P], v8(f_hi).bitcast(F32), ALU.subtract).then_inc(
                        dve_steps, dve_.step(f"near lo{b}"))
    return {"pe": pe_.learned(), "act": act_.learned(), "dve": dve_.learned(), "pool": pool_.learned()}


def vectors(inputs):
    parts = [inputs["norm_gain"], inputs["final_gain"], inputs["norm1_g_2"], inputs["norm2_g_2"],
             inputs["ffn_conv_w_2"], inputs["ffn_conv_b_2"], inputs["c_2"], inputs["c_ctx_2"],
             inputs["odd_q_g_2"], inputs["odd_q_g_2"], inputs["odd_k_g_2"], inputs["odd_k_g_2"],
             np.zeros(6 * P, np.float32), inputs["ada_b_2"]]
    flat = np.concatenate([np.asarray(a).reshape(-1) for a in parts])
    return np.concatenate([flat, np.zeros(VROWS * P - flat.size, np.float32)]).reshape(VROWS, P)


def kernel(**inputs):
    import concourse.bacc as bacc
    from concourse.bass_utils import run_bass_kernel_spmd as run

    arrays = {name: np.ascontiguousarray(inputs[key]) for name, key in (
        ("x", "x"), ("w_in", "w_in"), ("w_branch", "w_branch"), ("w_out", "w_out"), ("forget_bias", "forget_bias"),
        ("ada_w", "ada_w_2"), ("ctx", "ctx_2"), ("w_up", "ffn_w_up_2"), ("w_down", "ffn_w_down_2"))}
    for name, key in (("even_in", "even_w_in_2"), ("even_out", "even_w_out_2"), ("w_s", "even_w_s_2"),
                      ("b_s", "even_b_s_2"), ("qkv", "odd_w_qkv_2"), ("odd_out", "odd_w_o_2")):
        arrays[name] = np.ascontiguousarray(inputs[key][0])
    rpb = np.asarray(inputs["odd_rpb_2"])[0, :, ::-1, ::-1]
    rows = np.stack([rpb[:, 4 + r:8 + r, :] for r in range(4)])
    arrays["rpb"] = np.concatenate([np.zeros(48, np.float32), rows.reshape(-1), np.zeros(64, np.float32)])
    arrays["vectors"] = vectors(inputs)
    arrays.update(constants())

    def build(known):
        nc = bacc.Bacc("TRN2", target_bir_lowering=False, num_devices=1)
        ins = {n: nc.dram_tensor(n, a.shape, mybir.dt.from_np(a.dtype), kind="ExternalInput").ap()
               for n, a in arrays.items()}
        out = nc.dram_tensor("out", (1, SEQ, D), F32, kind="ExternalOutput").ap()
        return nc, program(nc, ins, out, known)

    nc, known = build({})
    nc, again = build(known)
    assert known == again
    r = run(nc, [arrays], core_ids=[0])
    return r.results[0]["out"]
```
